# Optimizing a Trainium2 kernel written in Bass

```python
import jax, jax.numpy as jnp
from jax import lax
import numpy as np

D_MODEL = 1024
BATCH = 1
SEQ = 1024
DEPTH = 1

CHUNK = 64
Q_BLOCK = 128
ATTN_HEADS = 8
ATTN_HEAD_DIM = 64
D_ATTN = ATTN_HEADS * ATTN_HEAD_DIM
SSD_HEADS = 16
SSD_HEAD_DIM = 64
D_SSD = SSD_HEADS * SSD_HEAD_DIM
SSD_GROUPS = 2
SSD_STATE = 128
CONV_WIDTH = 4
CONV_CH = D_SSD + 2 * SSD_GROUPS * SSD_STATE
N_EXPERT_GROUPS = 4
EXPERTS_PER_GROUP = 8
N_EXPERTS = N_EXPERT_GROUPS * EXPERTS_PER_GROUP
TOP_K = 2
EXPERT_FF = 512
MOE_BLOCK = 256
EPS = 1e-6
IN_WIDTHS = (D_ATTN, D_ATTN, D_ATTN, ATTN_HEADS, D_SSD, CONV_CH, SSD_HEADS, D_MODEL, D_MODEL)
IN_SPLITS = tuple(sum(IN_WIDTHS[:i + 1]) for i in range(len(IN_WIDTHS) - 1))
IN_COLS = sum(IN_WIDTHS)

kernel_name = "fox_ssd_gated_hier_moe_trunk"

def rmsnorm(x, g):
    xf = x.astype(jnp.float32)
    y = xf * lax.rsqrt(jnp.mean(xf * xf, axis=-1, keepdims=True) + EPS)
    return (y * g.astype(jnp.float32)).astype(x.dtype)

def forgetting_attention(q, k, v, f_logit):
    Bb, S, H, Dh = q.shape
    log_f = jax.nn.log_sigmoid(f_logit.astype(jnp.float32))
    F = jnp.cumsum(log_f, axis=1).transpose(0, 2, 1)
    kh = k.transpose(0, 2, 1, 3)
    vh = v.transpose(0, 2, 1, 3)
    nq = S // Q_BLOCK
    q_blocks = q.transpose(0, 2, 1, 3).reshape(Bb, H, nq, Q_BLOCK, Dh).transpose(2, 0, 1, 3, 4)
    F_blocks = F.reshape(Bb, H, nq, Q_BLOCK).transpose(2, 0, 1, 3)
    key_pos = jnp.arange(S)
    scale = Dh ** -0.5

    def one_block(args):
        qb, Fq, i = args
        s = jnp.einsum("bhqd,bhkd->bhqk", qb, kh, preferred_element_type=jnp.float32) * scale
        s = s + Fq[..., None] - F[:, :, None, :]
        q_pos = i * Q_BLOCK + jnp.arange(Q_BLOCK)
        s = jnp.where(key_pos[None, :] <= q_pos[:, None], s, -jnp.inf)
        p = jax.nn.softmax(s, axis=-1)
        return jnp.einsum("bhqk,bhkd->bhqd", p.astype(vh.dtype), vh)

    out = lax.map(one_block, (q_blocks, F_blocks, jnp.arange(nq)))
    return out.transpose(1, 0, 3, 2, 4).reshape(Bb, S, H * Dh)

def causal_depthwise_conv(x, w, b):
    C = x.shape[-1]
    y = lax.conv_general_dilated(x, w[:, None, :].astype(x.dtype), window_strides=(1,),
                                 padding=[(CONV_WIDTH - 1, 0)],
                                 dimension_numbers=("NWC", "WIO", "NWC"),
                                 feature_group_count=C)
    return y + b

def ssd_chunked(xh, dt, A, Bg, Cg):
    Bb, S, H, P = xh.shape
    G, N = Bg.shape[2], Bg.shape[3]
    E = H // G
    nc, L = S // CHUNK, CHUNK
    x = (xh * dt[..., None].astype(xh.dtype)).reshape(Bb, nc, L, G, E, P)
    a = jnp.moveaxis((dt * A).reshape(Bb, nc, L, G, E), 2, -1)
    a_cs = jnp.cumsum(a, axis=-1)
    Bc = Bg.reshape(Bb, nc, L, G, N)
    Cc = Cg.reshape(Bb, nc, L, G, N)
    causal = jnp.tril(jnp.ones((L, L), dtype=bool))
    seg = a_cs[..., :, None] - a_cs[..., None, :]
    decay = jnp.exp(jnp.where(causal, seg, -jnp.inf))
    cb = jnp.einsum("bclgn,bcsgn->bcgls", Cc, Bc)
    m = cb[:, :, :, None] * decay
    y_diag = jnp.einsum("bcgels,bcsgep->bclgep", m, x)
    decay_to_end = jnp.exp(a_cs[..., -1:] - a_cs)
    chunk_states = jnp.einsum("bclgn,bcgel,bclgep->bcgepn", Bc, decay_to_end, x)
    chunk_decay = jnp.exp(a_cs[..., -1])

    def step(state, inp):
        s_c, d_c = inp
        return state * d_c[..., None, None] + s_c, state

    init = jnp.zeros((Bb, G, E, P, N), chunk_states.dtype)
    _, prev = lax.scan(step, init, (jnp.moveaxis(chunk_states, 1, 0), jnp.moveaxis(chunk_decay, 1, 0)))
    prev = jnp.moveaxis(prev, 0, 1)
    y_off = jnp.einsum("bclgn,bcgepn,bcgel->bclgep", Cc, prev, jnp.exp(a_cs))
    return (y_diag + y_off).reshape(Bb, S, H, P).astype(xh.dtype)

def hybrid_mixer(h, w_in, b_f, conv_w, conv_b, dt_bias, a_log, d_skip, ssd_norm_g,
                 w_br_attn, w_br_ssd, w_out):
    Bb, S, _ = h.shape
    proj = h @ w_in
    q, k, v, f_logit, z, xbc, dt_raw, g_attn, g_ssd = jnp.split(proj, IN_SPLITS, axis=-1)
    hs = (Bb, S, ATTN_HEADS, ATTN_HEAD_DIM)
    y_attn = forgetting_attention(q.reshape(hs), k.reshape(hs), v.reshape(hs), f_logit + b_f)
    xbc = jax.nn.silu(causal_depthwise_conv(xbc, conv_w, conv_b))
    xs, Bm, Cm = jnp.split(xbc, (D_SSD, D_SSD + SSD_GROUPS * SSD_STATE), axis=-1)
    dt = jax.nn.softplus(dt_raw.astype(jnp.float32) + dt_bias.astype(jnp.float32))
    A = -jnp.exp(a_log.astype(jnp.float32))
    xh = xs.reshape(Bb, S, SSD_HEADS, SSD_HEAD_DIM)
    y = ssd_chunked(xh, dt, A, Bm.reshape(Bb, S, SSD_GROUPS, SSD_STATE),
                    Cm.reshape(Bb, S, SSD_GROUPS, SSD_STATE))
    y = (y + xh * d_skip[:, None]).reshape(Bb, S, D_SSD)
    y_ssd = rmsnorm(y * jax.nn.silu(z), ssd_norm_g)
    merged = jax.nn.sigmoid(g_attn) * (y_attn @ w_br_attn) + jax.nn.sigmoid(g_ssd) * (y_ssd @ w_br_ssd)
    return merged @ w_out

def hierarchical_moe(h, w_gr, b_gr, w_er, b_er, w1, w3, w2):
    Bb, S, D = h.shape
    t = h.reshape(-1, D)
    T = t.shape[0]
    g_prob = jax.nn.softmax((t @ w_gr).astype(jnp.float32) + b_gr.astype(jnp.float32), axis=-1)
    g_w, g_idx = lax.top_k(g_prob, 1)
    e_logits = ((t @ w_er).astype(jnp.float32) + b_er.astype(jnp.float32)).reshape(T, N_EXPERT_GROUPS, EXPERTS_PER_GROUP)
    e_logits = jnp.take_along_axis(e_logits, g_idx[:, :, None], axis=1)[:, 0]
    e_w, e_local = lax.top_k(jax.nn.softmax(e_logits, axis=-1), TOP_K)
    expert_idx = g_idx * EXPERTS_PER_GROUP + e_local
    gate = g_w * e_w
    flat_e = expert_idx.reshape(-1)
    order = jnp.argsort(flat_e)
    sorted_e = flat_e[order]
    tok = order // TOP_K
    counts = jnp.zeros((N_EXPERTS,), jnp.int32).at[flat_e].add(1)
    padded = (counts + MOE_BLOCK - 1) // MOE_BLOCK * MOE_BLOCK
    start = jnp.cumsum(counts) - counts
    pad_start = jnp.cumsum(padded) - padded
    dest = pad_start[sorted_e] + jnp.arange(T * TOP_K) - start[sorted_e]
    n_blocks = -(-(T * TOP_K) // MOE_BLOCK) + N_EXPERTS
    buf = jnp.zeros((n_blocks * MOE_BLOCK, D), t.dtype).at[dest].set(t[tok])
    block_end = jnp.cumsum(padded) // MOE_BLOCK
    block_expert = jnp.minimum(jnp.searchsorted(block_end, jnp.arange(n_blocks), side="right"), N_EXPERTS - 1)

    def expert_block(args):
        xb, e = args
        return (jax.nn.silu(xb @ w1[e]) * (xb @ w3[e])) @ w2[e]

    out = lax.map(expert_block, (buf.reshape(n_blocks, MOE_BLOCK, D), block_expert)).reshape(-1, D)
    y_sorted = out[dest] * gate.reshape(-1)[order][:, None].astype(out.dtype)
    y = jnp.zeros((T * TOP_K, D), out.dtype).at[order].set(y_sorted).reshape(T, TOP_K, D).sum(axis=1)
    return y.reshape(Bb, S, D)

def setup_inputs(seed: int = 0) -> dict:
    key = jax.random.key(seed)
    ks = jax.random.split(key, 24)
    f32 = jnp.float32
    nrm = lambda k, shape, fan: jax.random.normal(k, shape, f32) * fan ** -0.5
    dt0 = jnp.exp(jax.random.uniform(ks[7], (DEPTH, SSD_HEADS), f32) * (np.log(0.1) - np.log(0.001)) + np.log(0.001))
    return {
        "x": jax.random.normal(ks[0], (BATCH, SEQ, D_MODEL), f32),
        "norm_mix_g": 1.0 + 0.05 * jax.random.normal(ks[1], (DEPTH, D_MODEL), f32),
        "w_in": nrm(ks[2], (DEPTH, D_MODEL, IN_COLS), D_MODEL),
        "b_f": jax.random.uniform(ks[3], (DEPTH, ATTN_HEADS), f32, 1.0, 6.0),
        "conv_w": nrm(ks[4], (DEPTH, CONV_WIDTH, CONV_CH), CONV_WIDTH),
        "conv_b": 0.02 * jax.random.normal(ks[5], (DEPTH, CONV_CH), f32),
        "dt_bias": dt0 + jnp.log(-jnp.expm1(-dt0)),
        "a_log": jnp.log(jax.random.uniform(ks[8], (DEPTH, SSD_HEADS), f32, 1.0, 16.0)),
        "d_skip": 1.0 + 0.1 * jax.random.normal(ks[9], (DEPTH, SSD_HEADS), f32),
        "ssd_norm_g": 1.0 + 0.05 * jax.random.normal(ks[10], (DEPTH, D_SSD), f32),
        "w_br_attn": nrm(ks[11], (DEPTH, D_ATTN, D_MODEL), D_ATTN),
        "w_br_ssd": nrm(ks[12], (DEPTH, D_SSD, D_MODEL), D_SSD),
        "w_out": nrm(ks[13], (DEPTH, D_MODEL, D_MODEL), D_MODEL),
        "norm_ffn_g": 1.0 + 0.05 * jax.random.normal(ks[14], (DEPTH, D_MODEL), f32),
        "w_group_router": nrm(ks[15], (DEPTH, D_MODEL, N_EXPERT_GROUPS), D_MODEL),
        "b_group_router": 0.01 * jax.random.normal(ks[16], (DEPTH, N_EXPERT_GROUPS), f32),
        "w_expert_router": nrm(ks[17], (DEPTH, D_MODEL, N_EXPERTS), D_MODEL),
        "b_expert_router": 0.01 * jax.random.normal(ks[18], (DEPTH, N_EXPERTS), f32),
        "w1": nrm(ks[19], (DEPTH, N_EXPERTS, D_MODEL, EXPERT_FF), D_MODEL),
        "w3": nrm(ks[20], (DEPTH, N_EXPERTS, D_MODEL, EXPERT_FF), D_MODEL),
        "w2": nrm(ks[21], (DEPTH, N_EXPERTS, EXPERT_FF, D_MODEL), EXPERT_FF),
        "final_g": 1.0 + 0.05 * jax.random.normal(ks[22], (D_MODEL,), f32),
    }

def reference(x, norm_mix_g, w_in, b_f, conv_w, conv_b, dt_bias, a_log, d_skip, ssd_norm_g,
              w_br_attn, w_br_ssd, w_out, norm_ffn_g, w_group_router, b_group_router,
              w_expert_router, b_expert_router, w1, w3, w2, final_g):
    for l in range(DEPTH):
        h = rmsnorm(x, norm_mix_g[l])
        x = x + hybrid_mixer(h, w_in[l], b_f[l], conv_w[l], conv_b[l], dt_bias[l], a_log[l],
                             d_skip[l], ssd_norm_g[l], w_br_attn[l], w_br_ssd[l], w_out[l])
        h = rmsnorm(x, norm_ffn_g[l])
        x = x + hierarchical_moe(h, w_group_router[l], b_group_router[l], w_expert_router[l],
                                 b_expert_router[l], w1[l], w3[l], w2[l])
    return rmsnorm(x, final_g)


_drawn_inputs = setup_inputs


def setup_inputs(seed=0):
    import zlib

    import numpy as np

    out = dict(_drawn_inputs(seed))
    spreads = {}
    factors = {'conv_b': 2.938, 'b_group_router': 25.34, 'b_expert_router': 21.39}
    for name, (base, spread) in spreads.items():
        noise = np.random.default_rng([zlib.crc32(name.encode()), seed]).standard_normal(out[name].shape)
        drawn = base * np.exp(spread * noise) if base else spread * noise
        out[name] = __import__('jax').numpy.asarray(drawn.astype(out[name].dtype))
    for name, factor in factors.items():
        out[name] = (out[name] * factor).astype(out[name].dtype)
    return out
```

```python
from collections import namedtuple
from contextlib import ExitStack

import concourse.bass as bass
from concourse import mybir

F32 = mybir.dt.float32
F32R = mybir.dt.float32r
BF16 = mybir.dt.bfloat16
I32 = mybir.dt.int32
U32 = mybir.dt.uint32
ACT = mybir.ActivationFunctionType
ALU = mybir.AluOpType
AX = mybir.AxisListType
ds = bass.ds

P = 128
SEQ = 1024
D = 1024
KT = D // P
TT = SEQ // P
HALF = 512
RING = 2
DMA = 16
EPS = 1e-6

HEADS = 8
HD = 64
D_ATTN = HEADS * HD
SSD_HEADS = 16
SSD_HD = 64
D_SSD = SSD_HEADS * SSD_HD
GROUPS = 2
STATE = 128
CONV = 4
CONV_CH = D_SSD + 2 * GROUPS * STATE
CB = CONV_CH // P
XB = D_SSD // P

COL_Q = 0
COL_F = 3 * D_ATTN
COL_Z = COL_F + HEADS
COL_XBC = COL_Z + D_SSD
COL_DT = COL_XBC + CONV_CH
COL_GA = COL_DT + SSD_HEADS
COL_GS = COL_GA + D
DT_ROW = 32
SMALL = 64

N_GROUPS = 4
PER_GROUP = 8
NE = N_GROUPS * PER_GROUP
FF = 512
FT = FF // P
TOPK = 2
SLOTS = P
MAX_OVER = SEQ * TOPK // P
BLOCKS = NE + MAX_OVER
MASKED = -1.0e30


Constants = namedtuple("Constants", "ident ident_bf ones tri tri_after tri_before causal_bf")


def banks(ps, first, n):
    return ps[:, first:first + n, :].rearrange("p b c -> p (b c)")


def make_constants(nc, c):
    with ExitStack() as ctx:
        made = ctx.enter_context(nc.semaphore("const_filled"))
        selected = ctx.enter_context(nc.semaphore("const_selected"))
        block = ctx.enter_context(nc.Block())

        @block.gpsimd
        def _(pool):
            pool.memset(c.ident[:, :], 0.0)
            pool.memset(c.ident_bf[:, :], 0.0)
            pool.memset(c.ones[:, :], 1.0)
            pool.memset(c.tri[:, :], 1.0)
            pool.memset(c.tri_after[:, :], 1.0)
            pool.memset(c.tri_before[:, :], 1.0)
            pool.memset(c.causal_bf[:, :], 0.0).then_inc(made, 1)
            pool.wait_ge(made, 1)
            for m in (c.ident, c.ident_bf):
                pool.affine_select(out=m[:, :], in_=m[:, :], compare_op=ALU.not_equal, fill=1.0,
                                   base=0, pattern=[[-1, P]], channel_multiplier=1)
            pool.affine_select(out=c.tri[:, :], in_=c.tri[:, :], compare_op=ALU.is_ge, fill=0.0,
                               base=0, pattern=[[1, P]], channel_multiplier=-1)
            pool.affine_select(out=c.tri_after[:, :], in_=c.tri_after[:, :], compare_op=ALU.is_ge,
                               fill=0.0, base=-1, pattern=[[-1, P]], channel_multiplier=1)
            pool.affine_select(out=c.tri_before[:, :], in_=c.tri_before[:, :], compare_op=ALU.is_ge,
                               fill=0.0, base=-1, pattern=[[1, P]], channel_multiplier=-1)
            pool.affine_select(out=c.causal_bf[:, :], in_=c.causal_bf[:, :], compare_op=ALU.is_ge,
                               fill=MASKED, base=0, pattern=[[-1, P]],
                               channel_multiplier=1).then_inc(selected, 1)
            pool.wait_ge(selected, 1)


def normalise_input(nc, c, ps, x, gain, h_hi, h_lo):
    with ExitStack() as ctx:
        def sb(name, shape, dt=F32):
            return ctx.enter_context(nc.sbuf_tensor(name, shape, dt))

        def sem(name):
            return ctx.enter_context(nc.semaphore(name))

        x_all = sb("x_all", [P, TT, D])
        gain_row = sb("gain_row", [P, D])
        squares = sb("squares", [P, D])
        sum_sq = sb("sum_sq", [P, TT])
        mean_sq = sb("mean_sq", [P, TT])
        root = sb("root", [P, TT])
        rstd = sb("rstd", [P, TT])
        xn = sb("xn", [P, RING, D])
        x_loaded = [sem(f"x_loaded{n}") for n in range(4)]
        gain_loaded = sem("gain_loaded")
        squared = sem("squared")
        mean_done = sem("mean_done")
        root_done = sem("root_done")
        rstd_done = sem("rstd_done")
        xn_done = sem("xn_done")
        transposed = sem("transposed")
        hi_done = sem("hi_done")
        lo_done = sem("lo_done")
        x_tiles = x[0].rearrange("(t p) d -> p t d", p=P)
        block = ctx.enter_context(nc.Block())

        @block.sync
        def _(sp):
            for n in range(4):
                sp.dma_start(x_all[:, 2 * n:2 * n + 2, :], x_tiles[:, 2 * n:2 * n + 2, :]).then_inc(x_loaded[n], DMA)
            sp.dma_start(gain_row[:, :], gain.to_broadcast([P, D])).then_inc(gain_loaded, DMA)

        @block.scalar
        def _(act):
            for t in range(TT):
                if t % 2 == 0:
                    act.wait_ge(x_loaded[t // 2], DMA)
                if t > 0:
                    act.wait_ge(squared, t)
                act.activation(squares[:, :], x_all[:, t, :], ACT.Square,
                               accum_out=sum_sq[:, t:t + 1]).then_inc(squared, 1)
            act.wait_ge(mean_done, 1)
            act.activation(root[:, :], mean_sq[:, :], ACT.Sqrt).then_inc(root_done, 1)
            with act.Fori(0, TT // RING) as i:
                for s in range(RING):
                    act.wait_ge(transposed, RING + RING * i + s + 1)
                    act.activation(h_hi[:, :, ds(RING * P * i + s * P, P)],
                                   banks(ps, 2 * s, 2).rearrange("p (k t) -> p k t", k=KT),
                                   ACT.Copy).then_inc(hi_done, 1)

        @block.vector
        def _(dve):
            dve.wait_ge(squared, TT)
            dve.tensor_scalar(mean_sq[:, :], sum_sq[:, :], 1.0 / D, EPS, ALU.mult, ALU.add).then_inc(mean_done, 1)
            dve.wait_ge(root_done, 1)
            dve.reciprocal(rstd[:, :], root[:, :]).then_inc(rstd_done, 1)
            dve.wait_ge(rstd_done, 1)
            dve.wait_ge(gain_loaded, DMA)
            with dve.Fori(0, TT // RING) as i:
                for s in range(RING):
                    t = RING * i + s
                    dve.wait_ge(transposed, t + 1)
                    dve.scalar_tensor_tensor(out=xn[:, s, :], in0=x_all[:, ds(t, 1), :].rearrange("p a d -> p (a d)"),
                                             scalar=rstd[:, ds(t, 1)], in1=gain_row[:, :],
                                             op0=ALU.mult, op1=ALU.mult).then_inc(xn_done, 1)
                for s in range(RING):
                    dve.wait_ge(hi_done, RING * i + s + 1)
                    dst = ds(RING * P * i + s * P, P)
                    dve.tensor_tensor(h_lo[:, :, dst], banks(ps, 2 * s, 2).rearrange("p (k t) -> p k t", k=KT),
                                      h_hi[:, :, dst].bitcast(F32), ALU.subtract).then_inc(lo_done, 1)

        @block.tensor
        def _(pe):
            pe.sem_inc(transposed, RING)
            pe.sem_inc(lo_done, RING)
            with pe.Fori(0, TT // RING) as i:
                for s in range(RING):
                    pe.wait_ge(xn_done, RING * i + s + 1)
                    pe.wait_ge(lo_done, RING * i + s + 1)
                    for k in range(KT):
                        last = pe.transpose(banks(ps, 2 * s, 2)[:, k * P:(k + 1) * P],
                                            xn[:, s, k * P:(k + 1) * P], c.ident[:, :])
                    last.then_inc(transposed, 1)


def three_passes(pe, out, w_hi, w_lo, h_hi, h_lo, first, last):
    for a, b, opens, closes in ((w_hi, h_hi, first, False), (w_hi, h_lo, False, False), (w_lo, h_hi, False, last)):
        for n in range(len(out)):
            ins = pe.matmul(out[n], a, b[n], start=opens, stop=closes)
    return ins


def project(nc, ps, w_in, col, n_blocks, h_hi, h_lo, kind, dest, extra):
    with ExitStack() as ctx:
        def sb(name, shape, dt=F32):
            return ctx.enter_context(nc.sbuf_tensor(f"{name}_{col}", shape, dt))

        def sem(name):
            return ctx.enter_context(nc.semaphore(f"{name}_{col}"))

        w_raw = sb("w_raw", [P, RING, KT, P])
        w_hi = sb("w_hi", [P, RING, KT, P], F32R)
        w_lo = sb("w_lo", [P, RING, KT, P], F32R)
        w_loaded = [sem(f"w_loaded{s}") for s in range(RING)]
        w_hi_done = sem("w_hi_done")
        w_lo_done = sem("w_lo_done")
        projected = sem("projected")
        read_out = sem("read_out")
        if kind == "conv":
            taps, bias = extra
            padded = sb("padded", [P, RING, CONV - 1 + SEQ])
            mixed = sb("mixed", [P, RING, SEQ])
            pad_done = sem("pad_done")
            conv_done = sem("conv_done")
            tap_done = sem("tap_done")
            silu_done = sem("silu_done")
        if kind in ("silu", "sigmoid"):
            stage = sb("stage", [P, RING, SEQ])
            staged = sem("staged")
            stored = [sem(f"stored{s}") for s in range(RING)]
        w_cols = w_in.rearrange("(k p) c -> p k c", p=P)
        block = ctx.enter_context(nc.Block())

        @block.sync
        def _(sp):
            with sp.Fori(0, n_blocks // RING) as i:
                for s in range(RING):
                    sp.wait_ge(w_lo_done, RING * i + s + 1)
                    sp.dma_start(w_raw[:, s, :, :], w_cols[:, :, ds(col + RING * P * i + s * P, P)]).then_inc(w_loaded[s], DMA)

        if kind in ("silu", "sigmoid"):
            @block.gpsimd
            def _(pool):
                pool.sem_inc(w_lo_done, RING)
                for s in range(RING):
                    pool.sem_inc(stored[s], DMA)
                with pool.Fori(0, n_blocks // RING) as i:
                    for s in range(RING):
                        n = RING * i + s
                        pool.wait_ge(w_hi_done, n + 1)
                        pool.tensor_tensor(w_lo[:, s, :, :], w_raw[:, s, :, :], w_hi[:, s, :, :].bitcast(F32),
                                           ALU.subtract).then_inc(w_lo_done, 1)
        else:
            @block.gpsimd
            def _(pool):
                pool.sem_inc(w_lo_done, RING)
                if kind == "conv":
                    pool.memset(padded[:, :, 0:CONV - 1], 0.0).then_inc(pad_done, 1)
                with pool.Fori(0, n_blocks // RING) as i:
                    for s in range(RING):
                        pool.wait_ge(w_hi_done, RING * i + s + 1)
                        pool.tensor_tensor(w_lo[:, s, :, :], w_raw[:, s, :, :], w_hi[:, s, :, :].bitcast(F32),
                                           ALU.subtract).then_inc(w_lo_done, 1)

        @block.tensor
        def _(pe):
            pe.sem_inc(projected, RING)
            with pe.Fori(0, n_blocks // RING) as i:
                for s in range(RING):
                    n = RING * i + s
                    pe.wait_ge(w_lo_done, RING + n + 1)
                    pe.wait_ge(read_out, n + 1)
                    for k in range(KT):
                        last = three_passes(pe, [ps[:, 2 * s, :], ps[:, 2 * s + 1, :]], w_hi[:, s, k, :], w_lo[:, s, k, :],
                                            [h_hi[:, k, 0:HALF], h_hi[:, k, HALF:SEQ]],
                                            [h_lo[:, k, 0:HALF], h_lo[:, k, HALF:SEQ]], k == 0, k == KT - 1)
                    last.then_inc(projected, 1)

        @block.scalar
        def _(act):
            func = {"silu": ACT.Silu, "sigmoid": ACT.Sigmoid}.get(kind, ACT.Copy)
            if kind != "keep":
                act.sem_inc(read_out, RING)
            if kind == "conv":
                act.sem_inc(silu_done, RING)
                act.wait_ge(pad_done, 1)

            with act.Fori(0, n_blocks // RING) as i:
                for s in range(RING):
                    n = RING * i + s
                    act.wait_ge(w_loaded[s], DMA * i + DMA)
                    act.wait_ge(projected, n + 1)
                    act.activation(w_hi[:, s, :, :], w_raw[:, s, :, :], ACT.Copy).then_inc(w_hi_done, 1)
                for s in range(RING):
                    n = RING * i + s
                    if kind in ("silu", "sigmoid"):
                        act.wait_ge(projected, RING + n + 1)
                        act.wait_ge(stored[s], DMA * i + DMA)
                        act.activation(stage[:, s, :], banks(ps, 2 * s, 2), func).then_inc(read_out, 1)
                        act.wait_ge(read_out, RING + n + 1)
                        act.dma_start(dest[ds(n, 1)].rearrange("a p t -> p (a t)"), stage[:, s, :]).then_inc(stored[s], DMA)
                    if kind == "conv":
                        act.wait_ge(projected, RING + n + 1)
                        act.wait_ge(conv_done, n + 1)
                        act.activation(padded[:, s, CONV - 1:], banks(ps, 2 * s, 2), ACT.Copy).then_inc(read_out, 1)
                if kind == "conv":
                    for s in range(RING):
                        n = RING * i + s
                        act.wait_ge(conv_done, RING + n + 1)
                        act.activation(dest[:, ds(n, 1), :].rearrange("p a t -> p (a t)"), mixed[:, s, :],
                                       ACT.Silu).then_inc(silu_done, 1)
            if kind in ("silu", "sigmoid"):
                for s in range(RING):
                    act.wait_ge(stored[s], DMA * (n_blocks // RING) + DMA)

        @block.vector
        def _(dve):
            if kind == "keep":
                dve.sem_inc(read_out, RING)
                with dve.Fori(0, n_blocks // RING) as i:
                    for s in range(RING):
                        dve.wait_ge(projected, RING + RING * i + s + 1)
                        dve.tensor_copy(dest[:, ds(RING * i + s, 1), :].rearrange("p a t -> p (a t)"),
                                        banks(ps, 2 * s, 2)).then_inc(read_out, 1)
            if kind == "conv":
                dve.sem_inc(conv_done, RING)
                with dve.Fori(0, n_blocks // RING) as i:
                    for s in range(RING):
                        n = RING * i + s
                        dve.wait_ge(read_out, RING + n + 1)
                        dve.wait_ge(silu_done, n + 1)
                        dve.tensor_scalar(mixed[:, s, :], padded[:, s, 0:SEQ], taps[:, 0, ds(n, 1)], bias[:, ds(n, 1)],
                                          ALU.mult, ALU.add).then_inc(tap_done, 1)
                        for j in range(1, CONV):
                            dve.wait_ge(tap_done, (CONV - 1) * n + j)
                            dve.scalar_tensor_tensor(out=mixed[:, s, :], in0=padded[:, s, j:j + SEQ],
                                                     scalar=taps[:, j, ds(n, 1)], in1=mixed[:, s, :], op0=ALU.mult,
                                                     op1=ALU.add).then_inc(tap_done if j < CONV - 1 else conv_done, 1)


def decays(nc, c, ps, w_in, b_f, dt_bias, a_log, h_hi, h_lo, f_rows, dt_tok, a_tok):
    with ExitStack() as ctx:
        def sb(name, shape, dt=F32):
            return ctx.enter_context(nc.sbuf_tensor(name, shape, dt))

        def sem(name):
            return ctx.enter_context(nc.semaphore(name))

        w_raw = sb("small_raw", [P, KT, P])
        w_hi = sb("small_hi", [P, KT, P], F32R)
        w_lo = sb("small_lo", [P, KT, P], F32R)
        sign = sb("small_sign", [SMALL, 1])
        bias = sb("small_bias", [SMALL, 1])
        bias_signed = sb("small_bias_signed", [SMALL, 1])
        a_rate = sb("a_rate", [P, SSD_HEADS])
        a_exp = sb("a_exp", [P, SSD_HEADS])
        arg = sb("softplus_arg", [SMALL, SEQ])
        arg_abs = sb("softplus_abs", [SMALL, SEQ])
        expd = sb("softplus_exp", [SMALL, SEQ])
        logd = sb("softplus_log", [SMALL, SEQ])
        soft = sb("softplus", [SMALL, SEQ])
        one_row = sb("one_row", [HEADS, SEQ])
        neg_f = sb("neg_f", [HEADS, SEQ])
        cleared = sem("small_cleared")
        loaded = sem("small_loaded")
        a_loaded = sem("a_loaded")
        hi_done = sem("small_hi_done")
        lo_done = sem("small_lo_done")
        projected = sem("small_projected")
        vec = sem("decays_vec")
        abs_done = sem("softplus_abs_done")
        expd_done = sem("softplus_exp_done")
        logd_done = sem("softplus_log_done")
        a_exp_done = sem("a_exp_done")
        transposed = sem("dt_transposed")
        stored = sem("f_rows_stored")
        w_cols = w_in.rearrange("(k p) c -> p k c", p=P)
        dt_rows = slice(DT_ROW, DT_ROW + SSD_HEADS)
        block = ctx.enter_context(nc.Block())

        @block.gpsimd
        def _(pool):
            pool.memset(w_raw[:, :, :], 0.0)
            pool.memset(sign[:, :], 1.0)
            pool.memset(bias[:, :], 0.0)
            pool.memset(one_row[:, :], 1.0).then_inc(cleared, 1)
            pool.wait_ge(cleared, 1)
            pool.memset(sign[0:HEADS, :], -1.0).then_inc(cleared, 1)
            pool.wait_ge(hi_done, 1)
            pool.tensor_tensor(w_lo[:, :, :], w_raw[:, :, :], w_hi[:, :, :].bitcast(F32), ALU.subtract).then_inc(lo_done, 1)

        @block.sync
        def _(sp):
            sp.dma_start(a_rate[:, :], a_log.to_broadcast([P, SSD_HEADS])).then_inc(a_loaded, DMA)
            sp.wait_ge(cleared, 2)
            with nc.allow_non_contiguous_dma(reason="a few narrow columns"):
                sp.dma_start(w_raw[:, :, 0:HEADS], w_cols[:, :, COL_F:COL_F + HEADS]).then_inc(loaded, DMA)
                sp.dma_start(w_raw[:, :, dt_rows], w_cols[:, :, COL_DT:COL_DT + SSD_HEADS]).then_inc(loaded, DMA)
                sp.dma_start(bias[0:HEADS, :], b_f.rearrange("a h -> h a")).then_inc(loaded, DMA)
                sp.dma_start(bias[dt_rows, :], dt_bias.rearrange("a h -> h a")).then_inc(loaded, DMA)
            sp.wait_ge(vec, 4)
            sp.dma_start(f_rows, neg_f[:, :]).then_inc(stored, DMA)
            sp.wait_ge(stored, DMA)

        @block.scalar
        def _(act):
            act.wait_ge(loaded, 4 * DMA)
            act.activation(w_hi[:, :, :], w_raw[:, :, :], ACT.Copy).then_inc(hi_done, 1)
            act.wait_ge(a_loaded, DMA)
            act.activation(a_exp[:, :], a_rate[:, :], ACT.Exp).then_inc(a_exp_done, 1)
            act.wait_ge(vec, 2)
            act.activation(arg_abs[:, :], arg[:, :], ACT.Abs).then_inc(abs_done, 1)
            act.wait_ge(abs_done, 1)
            act.activation(expd[:, :], arg_abs[:, :], ACT.Exp, scale=-1.0).then_inc(expd_done, 1)
            act.wait_ge(expd_done, 1)
            act.activation(logd[:, :], expd[:, :], ACT.Ln, bias=1.0).then_inc(logd_done, 1)

        @block.tensor
        def _(pe):
            pe.wait_ge(lo_done, 1)
            for k in range(KT):
                last = three_passes(pe, [ps[:, 0, :], ps[:, 1, :]], w_hi[:, k, :], w_lo[:, k, :],
                                    [h_hi[:, k, 0:HALF], h_hi[:, k, HALF:SEQ]],
                                    [h_lo[:, k, 0:HALF], h_lo[:, k, HALF:SEQ]], k == 0, k == KT - 1)
            last.then_inc(projected, 1)
            pe.wait_ge(vec, 3)
            for t in range(TT):
                last = pe.transpose(ps[:, 2, t * SMALL:(t + 1) * SMALL], soft[:, t * P:(t + 1) * P],
                                    c.ident[0:SMALL, 0:SMALL])
            last.then_inc(transposed, 1)

        @block.vector
        def _(dve):
            dve.wait_ge(loaded, 4 * DMA)
            dve.tensor_tensor(bias_signed[:, :], bias[:, :], sign[:, :], ALU.mult).then_inc(vec, 1)
            dve.wait_ge(vec, 1)
            dve.wait_ge(projected, 1)
            dve.tensor_scalar(arg[:, :], banks(ps, 0, 2)[0:SMALL, :], sign[:, :], bias_signed[:, :],
                              ALU.mult, ALU.add).then_inc(vec, 1)
            dve.wait_ge(vec, 2)
            dve.wait_ge(logd_done, 1)
            dve.scalar_tensor_tensor(out=soft[:, :], in0=arg[:, :], scalar=0.0, in1=logd[:, :],
                                     op0=ALU.max, op1=ALU.add).then_inc(vec, 1)
            dve.wait_ge(vec, 3)
            dve.wait_ge(cleared, 2)
            dve.tensor_tensor_scan(neg_f[:, :], one_row[:, :], soft[0:HEADS, :], 0.0,
                                   ALU.mult, ALU.add).then_inc(vec, 1)
            dve.wait_ge(transposed, 1)
            dve.tensor_copy(dt_tok[:, :, :], ps[:, 2, :].rearrange("p (t r) -> p t r", t=TT)[:, :, dt_rows]).then_inc(vec, 1)
            dve.wait_ge(vec, 5)
            dve.wait_ge(a_exp_done, 1)
            for t in range(TT):
                dve.scalar_tensor_tensor(out=a_tok[:, t, :], in0=dt_tok[:, t, :], scalar=-1.0, in1=a_exp[:, :],
                                         op0=ALU.mult, op1=ALU.mult)


def attention(nc, c, ps, qkv, f_rows, y_hi, y_lo):
    PAIRS = HEADS // 2
    TILES = 2 * TT
    DT = HD + 1
    with ExitStack() as ctx:
        def sb(name, shape, dt=F32):
            return ctx.enter_context(nc.sbuf_tensor(name, shape, dt))

        def sem(name):
            return ctx.enter_context(nc.semaphore(name))

        q_cur = sb("q_cur", [DT, 2, SEQ])
        k_cur = sb("k_cur", [DT, 2, SEQ])
        v_cur = sb("v_cur", [P, SEQ])
        v_tok = sb("v_tok", [P, TT, P])
        probs = sb("probs", [P, RING, SEQ])
        probs_t = sb("probs_t", [P, RING, SEQ])
        neg_max = sb("neg_max", [P, TILES])
        row_sum = sb("row_sum", [P, TILES])
        inv_sum = sb("inv_sum", [P, TILES])
        y_pair = sb("y_pair", [P, TT, P])
        ones_set = sem("ones_set")
        f_loaded = [sem(f"f_loaded{s}") for s in range(2)]
        q_copied = sem("q_copied")
        k_copied = sem("k_copied")
        v_copied = sem("v_copied")
        v_turned = sem("v_turned")
        v_ready = sem("v_ready")
        scored = sem("scored")
        maxed = sem("maxed")
        expd = sem("expd")
        turned = sem("turned")
        evac_low = sem("evac_low")
        evac_high = sem("evac_high")
        weighed = sem("weighed")
        inverted = sem("inverted")
        normed = sem("normed")
        pair_turned = sem("pair_turned")
        hi_done = sem("attn_hi_done")
        lo_done = sem("attn_lo_done")
        order = [(0, t) for t in range(TT)] + [(1, TT - 1 - t) for t in range(TT)]
        block = ctx.enter_context(nc.Block())

        @block.sync
        def _(sp):
            with sp.Fori(0, PAIRS) as i:
                sp.wait_ge(pair_turned, i + 1)
                for s in range(2):
                    sp.dma_start(k_cur[HD:DT, s, :], f_rows[ds(2 * i + s, 1), :]).then_inc(f_loaded[s], DMA)

        @block.gpsimd
        def _(pool):
            pool.memset(q_cur[HD:DT, :, :], 1.0).then_inc(ones_set, 1)
            pool.wait_ge(ones_set, 1)
            with pool.Fori(0, PAIRS) as i:
                pool.wait_ge(pair_turned, i + 1)
                pool.tensor_copy(v_cur[:, :], qkv[:, ds(2 * PAIRS + i, 1), :].rearrange("p a t -> p (a t)")).then_inc(v_copied, 1)

        @block.vector
        def _(dve):
            dve.sem_inc(normed, RING)
            dve.sem_inc(evac_low, 1)
            dve.sem_inc(lo_done, 1)

            def row_max(i, n):
                s, t = order[n]
                dve.wait_ge(scored, TILES * i + n + 1)
                dve.tensor_reduce(neg_max[:, n:n + 1], banks(ps, 2 * (n % RING), 2)[:, 0:(t + 1) * P], AX.X, ALU.max,
                                  negate=True).then_inc(maxed, 1)

            def evacuate(i, n):
                s, t = order[n]
                width = min(t + 1, 4) * P
                dve.wait_ge(turned, RING + TILES * i + n + 1)
                dve.wait_ge(weighed, TILES * i + n + 1)
                dve.tensor_copy(probs_t[:, n % RING, 0:width], ps[:, 4, 0:width]).then_inc(evac_low, 1)
                dve.wait_ge(expd, RING + TILES * i + n + 1)
                dve.reciprocal(inv_sum[:, n:n + 1], row_sum[:, n:n + 1]).then_inc(inverted, 1)

            def normalise(i, n):
                s, t = order[n]
                dve.wait_ge(weighed, RING + TILES * i + n + 1)
                dve.wait_ge(inverted, TILES * i + n + 1)
                dve.tensor_scalar(y_pair[:, t, s * HD:(s + 1) * HD], ps[:, 6 + n % RING, 0:HD], inv_sum[:, n:n + 1],
                                  None, ALU.mult).then_inc(normed, 1)

            with dve.Fori(0, PAIRS) as i:
                dve.wait_ge(pair_turned, i + 1)
                for s in range(2):
                    dve.tensor_scalar(q_cur[0:HD, s, :], qkv[s * HD:(s + 1) * HD, ds(i, 1), :].rearrange("p a t -> p (a t)"),
                                      HD ** -0.5, None, ALU.mult).then_inc(q_copied, 1)
                dve.wait_ge(v_turned, i + 1)
                dve.tensor_copy(v_tok[:, :, :].rearrange("p t d -> p (t d)"), banks(ps, 4, 2)).then_inc(v_ready, 1)
                row_max(i, 0)
                for n in range(TILES):
                    if n + 1 < TILES:
                        row_max(i, n + 1)
                    evacuate(i, n)
                    if n > 0:
                        normalise(i, n - 1)
                normalise(i, TILES - 1)
                dve.wait_ge(hi_done, i + 1)
                dve.tensor_tensor(y_lo[:, ds(i, 1), :].rearrange("p a t -> p (a t)"), banks(ps, 4, 2),
                                  y_hi[:, ds(i, 1), :].rearrange("p a t -> p (a t)").bitcast(F32),
                                  ALU.subtract).then_inc(lo_done, 1)

        @block.scalar
        def _(act):
            act.sem_inc(expd, RING)
            act.sem_inc(evac_high, 1)

            def exponent(i, n):
                s, t = order[n]
                act.wait_ge(maxed, TILES * i + n + 1)
                act.wait_ge(turned, TILES * i + n + 1)
                width = (t + 1) * P
                act.activation(probs[:, n % RING, 0:width], banks(ps, 2 * (n % RING), 2)[:, 0:width], ACT.Exp,
                               bias=neg_max[:, n:n + 1], accum_out=row_sum[:, n:n + 1]).then_inc(expd, 1)

            def evacuate(i, n):
                s, t = order[n]
                act.wait_ge(turned, RING + TILES * i + n + 1)
                act.wait_ge(weighed, TILES * i + n + 1)
                act.activation(probs_t[:, n % RING, HALF:(t + 1) * P], ps[:, 5, 0:(t + 1) * P - HALF], ACT.Copy).then_inc(evac_high, 1)

            with act.Fori(0, PAIRS) as i:
                act.wait_ge(pair_turned, i + 1)
                for s in range(2):
                    act.activation(k_cur[0:HD, s, :], qkv[s * HD:(s + 1) * HD, ds(PAIRS + i, 1), :].rearrange("p a t -> p (a t)"),
                                   ACT.Copy).then_inc(k_copied, 1)
                exponent(i, 0)
                for n in range(TILES):
                    if n + 1 < TILES:
                        exponent(i, n + 1)
                    if order[n][1] >= 4:
                        evacuate(i, n)
                act.wait_ge(pair_turned, 1 + i + 1)
                act.activation(y_hi[:, ds(i, 1), :].rearrange("p a t -> p (a t)"), banks(ps, 4, 2), ACT.Copy).then_inc(hi_done, 1)

        @block.tensor
        def _(pe):
            pe.sem_inc(turned, RING)
            pe.sem_inc(weighed, RING)
            pe.sem_inc(pair_turned, 1)
            pe.wait_ge(ones_set, 1)

            def score(i, n):
                s, t = order[n]
                if n == 0 or n == TT:
                    pe.wait_ge(q_copied, 2 * i + s + 1)
                    pe.wait_ge(k_copied, 2 * i + s + 1)
                    pe.wait_ge(f_loaded[s], DMA * i + DMA)
                pe.wait_ge(expd, TILES * i + n + 1)
                for b in range(t // 4 + 1):
                    keys = min((t + 1) * P - b * HALF, HALF)
                    out = ps[:, 2 * (n % RING) + b, 0:keys]
                    last = pe.matmul(out, q_cur[:, s, t * P:(t + 1) * P], k_cur[:, s, b * HALF:b * HALF + keys],
                                     start=True, stop=True)
                    if b == t // 4:
                        last = pe.matmul(out[:, keys - P:keys], c.ident_bf[:, :], c.causal_bf[:, :], start=False, stop=True,
                                         skip_group_check=True)
                last.then_inc(scored, 1)

            def turn(i, n, high):
                s, t = order[n]
                pe.wait_ge(expd, RING + TILES * i + n + 1)
                pe.wait_ge(evac_low, 1 + TILES * i + n)
                pe.wait_ge(evac_high, 1 + 8 * i + high)
                for j in range(t + 1):
                    last = pe.transpose(ps[:, 4 + j // 4, (j % 4) * P:(j % 4 + 1) * P], probs[:, n % RING, j * P:(j + 1) * P],
                                        c.ident[:, :])
                last.then_inc(turned, 1)

            def weigh(i, n, high):
                s, t = order[n]
                pe.wait_ge(evac_low, 1 + TILES * i + n + 1)
                pe.wait_ge(evac_high, 1 + 8 * i + high)
                pe.wait_ge(normed, TILES * i + n + 1)
                for j in range(t + 1):
                    last = pe.matmul(ps[:, 6 + n % RING, 0:HD], probs_t[:, n % RING, j * P:(j + 1) * P],
                                     v_tok[:, j, s * HD:(s + 1) * HD], start=j == 0, stop=j == t)
                last.then_inc(weighed, 1)

            highs = [sum(t >= 4 for _, t in order[:n]) for n in range(TILES + 1)]
            with pe.Fori(0, PAIRS) as i:
                pe.wait_ge(v_copied, i + 1)
                pe.wait_ge(lo_done, i + 1)
                for t in range(TT):
                    last = pe.transpose(ps[:, 4 + t // 4, (t % 4) * P:(t % 4 + 1) * P], v_cur[:, t * P:(t + 1) * P], c.ident[:, :])
                last.then_inc(v_turned, 1)
                score(i, 0)
                pe.wait_ge(v_ready, i + 1)
                for n in range(TILES):
                    if n + 1 < TILES:
                        score(i, n + 1)
                    turn(i, n, highs[n])
                    if n > 0:
                        weigh(i, n - 1, highs[n])
                weigh(i, TILES - 1, highs[TILES])
                pe.wait_ge(normed, RING + TILES * i + TILES)
                for t in range(TT):
                    last = pe.transpose(ps[:, 4 + t // 4, (t % 4) * P:(t % 4 + 1) * P], y_pair[:, t, :], c.ident[:, :])
                last.then_inc(pair_turned, 1)


def spread(ap, shape, axis):
    return ap.unsqueeze(axis).to_broadcast(shape)


def state_space(nc, c, ps, xbc, dt_tok, a_tok, d_skip, silu_z, gated):
    CHUNKS = SEQ // P
    H, HP = SSD_HEADS, SSD_HD
    QUARTER = H // 4
    with ExitStack() as ctx:
        def sb(name, shape, dt=F32):
            return ctx.enter_context(nc.sbuf_tensor(name, shape, dt))

        def sem(name):
            return ctx.enter_context(nc.semaphore(name))

        d_col = sb("d_col", [P, XB])
        a_cs = sb("a_cs", [P, CHUNKS, H])
        a_total = sb("a_total", [P, CHUNKS, H])
        a_left = sb("a_left", [P, CHUNKS, H])
        grow_in = sb("grow_in", [P, CHUNKS, H])
        chunk_decay = sb("chunk_decay", [P, CHUNKS, H])
        to_end = sb("to_end", [P, CHUNKS, H])
        dt_to_end = sb("dt_to_end", [P, CHUNKS, H])
        chan = sb("chan", [P, RING, CB, P])
        a_spread = sb("a_spread", [P, RING, H, P])
        cb_masked = sb("cb_masked", [P, RING, GROUPS, P])
        b_tok = sb("b_tok", [P, RING, GROUPS, P])
        decay = sb("decay", [P, RING, H, P])
        x_dt = sb("x_dt", [P, RING, H, HP])
        x_end = sb("x_end", [P, RING, H, HP])
        y_tok = sb("y_tok", [P, H, HP])
        state = sb("state", [P, H, HP])
        skip = sb("skip", [P, XB, P])
        y_sum = sb("y_sum", [P, XB, P])
        z_chunk = sb("z_chunk", [P, RING, XB, P])

        d_loaded = sem("d_loaded")
        z_loaded = [sem(f"z_loaded{s}") for s in range(RING)]
        sums_ready = sem("sums_ready")
        pre = sem("ssd_prelude_vec")
        pre_exp = sem("ssd_prelude_exp")
        state_zero = sem("state_zero")
        copied = sem("chunk_copied")
        a_ready = sem("a_spread_ready")
        small_ready = sem("cb_and_b_ready")
        cb_done = sem("cb_masked_done")
        b_done = sem("b_tok_done")
        x_turned = sem("x_turned")
        x_scaled = sem("x_scaled")
        seg_done = sem("seg_done")
        decay_done = sem("decay_done")
        m_done = sem("m_done")
        y_parts = sem("y_parts")
        off_scaled = sem("off_scaled")
        y_added = sem("y_added")
        gain_ready = sem("state_gain_ready")
        state_scaled = sem("state_scaled")
        state_done = sem("state_done")
        y_turned = sem("y_turned")
        skip_done = sem("skip_done")
        y_done = sem("y_done")
        gated_done = sem("gated_done")
        held = sem("gated_held")
        z_cols = silu_z.rearrange("b p t -> p b t")
        block = ctx.enter_context(nc.Block())
        y_in = banks(ps, 4, 2)
        y_off = banks(ps, 6, 2)

        def steps(eng, step):
            with eng.Fori(0, CHUNKS // 2 - 1) as i:
                step(2 * i, 0, True)
                step(2 * i + 1, 1, True)
            step(CHUNKS - 2, 0, True)
            step(CHUNKS - 1, 1, False)

        @block.sync
        def _(sp):
            heads = d_skip.rearrange("a (b two) -> two a b", two=2)
            with nc.allow_non_contiguous_dma(reason="16 numbers"):
                for half in range(2):
                    sp.dma_start(d_col[half * HP:(half + 1) * HP, :], heads[half].to_broadcast([HP, XB])).then_inc(d_loaded, DMA)

            def step(n, s, more):
                sp.wait_ge(gated_done, n + 1)
                sp.dma_start(z_chunk[:, s, :, :], z_cols[:, :, ds(n * P, P)]).then_inc(z_loaded[s], DMA)

            steps(sp, step)

        @block.gpsimd
        def _(pool):
            pool.sem_inc(gated_done, RING)
            pool.memset(state[:, :, :], 0.0).then_inc(state_zero, 1)

            def front(n, s):
                pool.wait_ge(y_parts, n + 1)
                pool.tensor_copy(chan[:, s, :, :], xbc[:, :, ds(n * P, P)]).then_inc(copied, 1)
                pool.wait_ge(seg_done, 4 * n + 4)
                pool.tensor_tensor(a_spread[:, s, :, :],
                                   spread(a_tok[:, ds(n, 1), :].rearrange("p a h -> p (a h)"), [P, H, P], 2),
                                   spread(c.tri[:, :], [P, H, P], 1), ALU.mult).then_inc(a_ready, 1)

            def step(n, s, more):
                if more:
                    front(n + 1, 1 - s)
                pool.wait_ge(y_done, 1 + n)
                pool.wait_ge(copied, n + 1)
                pool.tensor_tensor(skip[:, :, :], chan[:, s, 0:XB, :], spread(d_col[:, :], [P, XB, P], 2),
                                   ALU.mult).then_inc(skip_done, 1)
                pool.wait_ge(y_done, 1 + n + 1)
                pool.wait_ge(z_loaded[s], DMA * (n // 2 if isinstance(n, int) else (n - s) // 2) + DMA)
                pool.sem_inc(held, 1)
                pool.tensor_tensor(gated[:, :, ds(n * P, P)], y_sum[:, :, :], z_chunk[:, s, :, :],
                                   ALU.mult).then_inc(gated_done, 1)

            pool.wait_ge(d_loaded, 2 * DMA)
            front(0, 0)
            steps(pool, step)

        @block.scalar
        def _(act):
            act.sem_inc(decay_done, 4)
            act.wait_ge(pre, 2)
            act.activation(grow_in[:, :, :], a_cs[:, :, :], ACT.Exp).then_inc(pre_exp, 1)
            act.activation(chunk_decay[:, :, :], a_total[:, :, :], ACT.Exp).then_inc(pre_exp, 1)
            act.wait_ge(pre, 3)
            act.activation(to_end[:, :, :], a_left[:, :, :], ACT.Exp).then_inc(pre_exp, 1)

            def front(n, s):
                act.wait_ge(small_ready, n + 1)
                act.wait_ge(cb_done, n + 1)
                act.activation(b_tok[:, s, :, :].rearrange("p g d -> p (g d)"), ps[:, 0, GROUPS * P:], ACT.Copy).then_inc(b_done, 1)
                for q in range(4):
                    act.wait_ge(seg_done, 4 * RING + 4 * n + q + 1)
                    if q == 0:
                        act.wait_ge(y_parts, n + 1)
                    act.activation(decay[:, s, q * QUARTER:(q + 1) * QUARTER, :].rearrange("p h l -> p (h l)"),
                                   ps[:, (q + 1) % 2, :], ACT.Exp).then_inc(decay_done, 1)

            front(0, 0)
            steps(act, lambda n, s, more: front(n + 1, 1 - s) if more else None)

        @block.vector
        def _(dve):
            for s in (y_done, x_scaled, state_done):
                dve.sem_inc(s, 1)
            dve.wait_ge(sums_ready, 1)
            dve.tensor_copy(a_cs[:, :, :].rearrange("p t h -> p (t h)"), ps[:, 0, 0:P]).then_inc(pre, 1)
            dve.tensor_copy(a_total[:, :, :].rearrange("p t h -> p (t h)"), ps[:, 0, P:2 * P]).then_inc(pre, 1)
            dve.wait_ge(pre, 2)
            dve.tensor_tensor(a_left[:, :, :], a_total[:, :, :], a_cs[:, :, :], ALU.subtract).then_inc(pre, 1)
            dve.wait_ge(pre_exp, 3)
            dve.tensor_tensor(dt_to_end[:, :, :], dt_tok[:, :, :], to_end[:, :, :], ALU.mult).then_inc(pre, 1)
            dve.wait_ge(pre, 4)
            dve.wait_ge(state_zero, 1)

            def per_head(t, n):
                return spread(t[:, ds(n, 1), :].rearrange("p a h -> p (a h)"), [P, H, HP], 2)

            def x_psum():
                return banks(ps, 2, 2).rearrange("p (h d) -> p h d", h=H)

            def front_x(n, s):
                dve.wait_ge(small_ready, n + 1)
                dve.tensor_tensor(cb_masked[:, s, :, :], ps[:, 0, 0:GROUPS * P].rearrange("p (g l) -> p g l", g=GROUPS),
                                  spread(c.tri[:, :], [P, GROUPS, P], 1), ALU.mult).then_inc(cb_done, 1)
                dve.wait_ge(x_turned, n + 1)
                dve.tensor_tensor(x_dt[:, s, :, :], x_psum(), per_head(dt_tok, n), ALU.mult)
                dve.tensor_tensor(x_end[:, s, :, :], x_psum(), per_head(dt_to_end, n), ALU.mult).then_inc(x_scaled, 1)

            def front_m(n, s):
                dve.wait_ge(cb_done, n + 1)
                for q in range(4):
                    dve.wait_ge(decay_done, 4 + 4 * n + q + 1)
                    heads = slice(q * QUARTER, (q + 1) * QUARTER)
                    dve.tensor_tensor(decay[:, s, heads, :], decay[:, s, heads, :],
                                      spread(cb_masked[:, s, q * GROUPS // 4, :], [P, QUARTER, P], 1), ALU.mult).then_inc(m_done, 1)

            def step(n, s, more):
                dve.wait_ge(y_parts, RING + n + 1)
                dve.tensor_tensor(y_tok[:, :, :], y_off.rearrange("p (h d) -> p h d", h=H), per_head(grow_in, n),
                                  ALU.mult).then_inc(off_scaled, 1)
                dve.wait_ge(off_scaled, n + 1)
                dve.tensor_tensor(y_tok[:, :, :].rearrange("p h d -> p (h d)"), y_in,
                                  y_tok[:, :, :].rearrange("p h d -> p (h d)"), ALU.add).then_inc(y_added, 1)
                if more:
                    front_x(n + 1, 1 - s)
                dve.tensor_tensor(state[:, :, :], state[:, :, :], per_head(chunk_decay, n), ALU.mult).then_inc(state_scaled, 1)
                dve.wait_ge(state_scaled, n + 1)
                dve.wait_ge(gain_ready, n + 1)
                dve.tensor_tensor(state[:, :, :].rearrange("p h d -> p (h d)"), y_off,
                                  state[:, :, :].rearrange("p h d -> p (h d)"), ALU.add).then_inc(state_done, 1)
                if more:
                    front_m(n + 1, 1 - s)
                dve.wait_ge(y_turned, n + 1)
                dve.wait_ge(skip_done, n + 1)
                dve.wait_ge(gated_done, RING + n)
                dve.tensor_tensor(y_sum[:, :, :].rearrange("p b l -> p (b l)"), y_in,
                                  skip[:, :, :].rearrange("p b l -> p (b l)"), ALU.add).then_inc(y_done, 1)

            front_x(0, 0)
            front_m(0, 0)
            steps(dve, step)

        @block.tensor
        def _(pe):
            pe.sem_inc(y_parts, RING)
            pe.sem_inc(seg_done, 4 * RING)
            flat = a_tok[:, :, :].rearrange("p t h -> p (t h)")
            pe.matmul(ps[:, 0, 0:P], c.tri[:, :], flat, start=True, stop=True)
            pe.matmul(ps[:, 0, P:2 * P], c.ones[:, :], flat, start=True, stop=True).then_inc(sums_ready, 1)

            def front_small(n, s):
                pe.wait_ge(copied, n + 1)
                pe.wait_ge(decay_done, 4 + 4 * n)
                for g in range(GROUPS):
                    pe.matmul(ps[:, 0, g * P:(g + 1) * P], chan[:, s, XB + g, :], chan[:, s, XB + GROUPS + g, :],
                              start=True, stop=True)
                for g in range(GROUPS):
                    last = pe.transpose(ps[:, 0, (GROUPS + g) * P:(GROUPS + g + 1) * P], chan[:, s, XB + g, :], c.ident[:, :])
                last.then_inc(small_ready, 1)
                pe.wait_ge(x_scaled, 1 + n)
                for b in range(XB):
                    last = pe.transpose(ps[:, 2 + b // 4, (b % 4) * P:(b % 4 + 1) * P], chan[:, s, b, :], c.ident[:, :])
                last.then_inc(x_turned, 1)

            def front_seg(n, s):
                pe.wait_ge(a_ready, n + 1)
                for q in range(4):
                    if q == 1:
                        pe.wait_ge(cb_done, n + 1)
                        pe.wait_ge(b_done, n + 1)
                    if q >= 2:
                        pe.wait_ge(decay_done, 4 + 4 * n + q - 1)
                    pe.matmul(ps[:, (q + 1) % 2, :], c.tri_after[:, :],
                              a_spread[:, s, q * QUARTER:(q + 1) * QUARTER, :].rearrange("p h l -> p (h l)"),
                              start=True, stop=True).then_inc(seg_done, 1)

            def step(n, s, more):
                pe.wait_ge(m_done, 4 * n + 4)
                pe.wait_ge(y_done, 1 + n)
                for h in range(H):
                    pe.matmul(y_in[:, h * HP:(h + 1) * HP], decay[:, s, h, :], x_dt[:, s, h, :], start=True, stop=True)
                pe.wait_ge(state_done, 1 + n)
                for g in range(GROUPS):
                    heads = slice(g * H // GROUPS, (g + 1) * H // GROUPS)
                    last = pe.matmul(ps[:, 6 + g, :], chan[:, s, XB + GROUPS + g, :],
                                     state[:, heads, :].rearrange("p h d -> p (h d)"), start=True, stop=True)
                last.then_inc(y_parts, 1)
                if more:
                    front_small(n + 1, 1 - s)
                pe.wait_ge(off_scaled, n + 1)
                for g in range(GROUPS):
                    heads = slice(g * H // GROUPS, (g + 1) * H // GROUPS)
                    last = pe.matmul(ps[:, 6 + g, :], b_tok[:, s, g, :],
                                     x_end[:, s, heads, :].rearrange("p h d -> p (h d)"), start=True, stop=True)
                last.then_inc(gain_ready, 1)
                if more:
                    front_seg(n + 1, 1 - s)
                pe.wait_ge(y_added, n + 1)
                for b in range(XB):
                    last = pe.transpose(ps[:, 4 + b // 4, (b % 4) * P:(b % 4 + 1) * P],
                                        y_tok[:, 2 * b:2 * b + 2, :].rearrange("p h d -> p (h d)"), c.ident[:, :])
                last.then_inc(y_turned, 1)

            pe.wait_ge(pre, 2)
            front_small(0, 0)
            front_seg(0, 0)
            steps(pe, step)


def normalise_ssd(nc, c, ps, gated, gain, y_hi, y_lo):
    with ExitStack() as ctx:
        def sb(name, shape, dt=F32):
            return ctx.enter_context(nc.sbuf_tensor(name, shape, dt))

        def sem(name):
            return ctx.enter_context(nc.semaphore(name))

        gain_col = sb("ssd_gain_col", [P, XB])
        squares = sb("ssd_squares", [P, RING, SEQ])
        mean_sq = sb("ssd_mean_sq", [P, SEQ])
        root = sb("ssd_root", [P, SEQ])
        rstd = sb("ssd_rstd", [P, SEQ])
        loaded = sem("ssd_gain_loaded")
        squared = sem("ssd_squared")
        summed = sem("ssd_summed")
        mean_done = sem("ssd_mean_done")
        root_done = sem("ssd_root_done")
        rstd_done = sem("ssd_rstd_done")
        scaled = sem("ssd_scaled")
        hi_done = sem("ssd_hi_done")
        lo_done = sem("ssd_lo_done")
        block = ctx.enter_context(nc.Block())

        def col(t, b):
            return t[:, ds(b, 1), :].rearrange("p a t -> p (a t)")

        @block.sync
        def _(sp):
            with nc.allow_non_contiguous_dma(reason="a gain per channel"):
                sp.dma_start(gain_col[:, :], gain.rearrange("a (b p) -> p (a b)", p=P)).then_inc(loaded, DMA)

        @block.scalar
        def _(act):
            with act.Fori(0, XB // RING) as i:
                for s in range(RING):
                    act.wait_ge(summed, RING * i + s + 1)
                    act.activation(squares[:, s, :], col(gated, RING * i + s), ACT.Square).then_inc(squared, 1)
            act.wait_ge(mean_done, 1)
            act.activation(root[:, :], mean_sq[:, :], ACT.Sqrt).then_inc(root_done, 1)
            with act.Fori(0, XB) as b:
                act.wait_ge(scaled, b + 1)
                act.activation(col(y_hi, b), col(gated, b), ACT.Copy).then_inc(hi_done, 1)

        @block.tensor
        def _(pe):
            pe.sem_inc(summed, RING)
            for b in range(XB):
                pe.wait_ge(squared, b + 1)
                for n in range(2):
                    last = pe.matmul(ps[:, n, :], c.ones[:, :], squares[:, b % RING, n * HALF:(n + 1) * HALF],
                                     start=b == 0, stop=b == XB - 1)
                last.then_inc(summed, 1)

        @block.vector
        def _(dve):
            dve.wait_ge(summed, RING + XB)
            dve.tensor_scalar(mean_sq[:, :], banks(ps, 0, 2), 1.0 / D_SSD, EPS, ALU.mult, ALU.add).then_inc(mean_done, 1)
            dve.wait_ge(root_done, 1)
            dve.reciprocal(rstd[:, :], root[:, :]).then_inc(rstd_done, 1)
            dve.wait_ge(rstd_done, 1)
            dve.wait_ge(loaded, DMA)

            def scale(b):
                dve.scalar_tensor_tensor(out=col(gated, b), in0=col(gated, b), scalar=gain_col[:, ds(b, 1)], in1=rstd[:, :],
                                         op0=ALU.mult, op1=ALU.mult).then_inc(scaled, 1)

            def rest(b):
                dve.wait_ge(hi_done, b + 1)
                dve.tensor_tensor(col(y_lo, b), col(gated, b), col(y_hi, b).bitcast(F32), ALU.subtract).then_inc(lo_done, 1)

            scale(0)
            with dve.Fori(0, XB - 1) as b:
                scale(b + 1)
                rest(b)
            rest(XB - 1)


def merge(nc, ps, w_attn, w_ssd, gates, ya_hi, ya_lo, ys_hi, ys_lo, merged):
    KA = D_ATTN // P
    KW = KA + XB
    NB = D // P
    with ExitStack() as ctx:
        def sb(name, shape, dt=F32):
            return ctx.enter_context(nc.sbuf_tensor(name, shape, dt))

        def sem(name):
            return ctx.enter_context(nc.semaphore(name))

        w_raw = sb("branch_raw", [P, RING, KW, P])
        w_hi = sb("branch_hi", [P, RING, KW, P], F32R)
        w_lo = sb("branch_lo", [P, RING, KW, P], F32R)
        gate = sb("gate", [P, RING, 2, SEQ])
        w_loaded = [sem(f"branch_loaded{s}") for s in range(RING)]
        g_loaded = [sem(f"gate_loaded{s}") for s in range(RING)]
        hi_done = sem("branch_hi_done")
        lo_done = sem("branch_lo_done")
        projected = sem("branch_projected")
        gated = sem("branch_gated")
        added = sem("branch_added")
        wa_cols = w_attn.rearrange("(k p) c -> p k c", p=P)
        ws_cols = w_ssd.rearrange("(k p) c -> p k c", p=P)
        block = ctx.enter_context(nc.Block())

        @block.sync
        def _(sp):
            with sp.Fori(0, NB // RING) as i:
                for s in range(RING):
                    n = RING * i + s
                    sp.wait_ge(lo_done, n + 1)
                    sp.dma_start(w_raw[:, s, 0:KA, :], wa_cols[:, :, ds(n * P, P)]).then_inc(w_loaded[s], DMA)
                    sp.dma_start(w_raw[:, s, KA:KW, :], ws_cols[:, :, ds(n * P, P)]).then_inc(w_loaded[s], DMA)
                    sp.wait_ge(added, n + 1)
                    sp.dma_start(gate[:, s, 0, :], gates[ds(n, 1)].rearrange("a p t -> p (a t)")).then_inc(g_loaded[s], DMA)
                    sp.dma_start(gate[:, s, 1, :], gates[ds(NB + n, 1)].rearrange("a p t -> p (a t)")).then_inc(g_loaded[s], DMA)

        @block.scalar
        def _(act):
            with act.Fori(0, NB // RING) as i:
                for s in range(RING):
                    act.wait_ge(w_loaded[s], 2 * DMA * i + 2 * DMA)
                    act.wait_ge(projected, RING * i + s + 1)
                    act.activation(w_hi[:, s, :, :], w_raw[:, s, :, :], ACT.Copy).then_inc(hi_done, 1)

        @block.gpsimd
        def _(pool):
            pool.sem_inc(lo_done, RING)
            with pool.Fori(0, NB // RING) as i:
                for s in range(RING):
                    pool.wait_ge(hi_done, RING * i + s + 1)
                    pool.tensor_tensor(w_lo[:, s, :, :], w_raw[:, s, :, :], w_hi[:, s, :, :].bitcast(F32),
                                       ALU.subtract).then_inc(lo_done, 1)

        @block.tensor
        def _(pe):
            pe.sem_inc(projected, RING)
            with pe.Fori(0, NB // RING) as i:
                for s in range(RING):
                    n = RING * i + s
                    pe.wait_ge(lo_done, RING + n + 1)
                    pe.wait_ge(added, n + 1)
                    for k in range(KW):
                        hi, lo, kk, b = (ya_hi, ya_lo, k, 4 * s) if k < KA else (ys_hi, ys_lo, k - KA, 4 * s + 2)
                        last = three_passes(pe, [ps[:, b, :], ps[:, b + 1, :]], w_hi[:, s, k, :], w_lo[:, s, k, :],
                                            [hi[:, kk, 0:HALF], hi[:, kk, HALF:SEQ]], [lo[:, kk, 0:HALF], lo[:, kk, HALF:SEQ]],
                                            kk == 0, k in (KA - 1, KW - 1))
                    last.then_inc(projected, 1)

        @block.vector
        def _(dve):
            dve.sem_inc(added, RING)
            with dve.Fori(0, NB // RING) as i:
                for s in range(RING):
                    n = RING * i + s
                    out = merged[:, ds(n, 1), :].rearrange("p a t -> p (a t)")
                    dve.wait_ge(projected, RING + n + 1)
                    dve.wait_ge(g_loaded[s], 2 * DMA * i + 2 * DMA)
                    for g in range(2):
                        dve.tensor_tensor(gate[:, s, g, :], banks(ps, 4 * s + 2 * g, 2), gate[:, s, g, :], ALU.mult).then_inc(gated, 1)
                    dve.wait_ge(gated, 2 * n + 2)
                    dve.tensor_tensor(out, gate[:, s, 0, :], gate[:, s, 1, :], ALU.add).then_inc(added, 1)


def project_out(nc, ps, w_out, x, merged, x2):
    with ExitStack() as ctx:
        def sb(name, shape, dt=F32):
            return ctx.enter_context(nc.sbuf_tensor(name, shape, dt))

        def sem(name):
            return ctx.enter_context(nc.semaphore(name))

        w_raw = sb("out_raw", [P, RING, D])
        w_hi = sb("out_hi", [P, KT, D], F32R)
        w_lo = sb("out_lo", [P, KT, D], F32R)
        m_hi = sb("merged_hi", [P, RING, KT, P], F32R)
        m_lo = sb("merged_lo", [P, RING, KT, P], F32R)
        x_tile = sb("x_tile", [P, RING, D])
        w_loaded = [sem(f"out_loaded{s}") for s in range(RING)]
        x_loaded = [sem(f"res_loaded{s}") for s in range(RING)]
        w_hi_done = sem("out_hi_done")
        w_lo_done = sem("out_lo_done")
        m_hi_done = sem("merged_hi_done")
        m_lo_done = sem("merged_lo_done")
        projected = sem("out_projected")
        added = sem("out_added")
        x_tiles = x[0].rearrange("(t p) d -> t p d", p=P)
        w_rows = w_out.rearrange("(k p) c -> k p c", p=P)
        block = ctx.enter_context(nc.Block())

        @block.sync
        def _(sp):
            for k in range(KT):
                sp.wait_ge(w_lo_done, k + 1)
                sp.dma_start(w_raw[:, k % RING, :], w_rows[k]).then_inc(w_loaded[k % RING], DMA)
            with sp.Fori(0, TT // RING) as i:
                for s in range(RING):
                    sp.wait_ge(added, RING * i + s + 1)
                    sp.dma_start(x_tile[:, s, :], x_tiles[ds(RING * i + s, 1)].rearrange("a p d -> p (a d)")).then_inc(x_loaded[s], DMA)

        @block.scalar
        def _(act):
            for k in range(KT):
                act.wait_ge(w_loaded[k % RING], DMA * (k // RING) + DMA)
                act.activation(w_hi[:, k, :], w_raw[:, k % RING, :], ACT.Copy).then_inc(w_hi_done, 1)
            with act.Fori(0, TT // RING) as i:
                for s in range(RING):
                    t = RING * i + s
                    act.wait_ge(projected, t + 1)
                    act.activation(m_hi[:, s, :, :], merged[:, :, ds(t * P, P)], ACT.Copy).then_inc(m_hi_done, 1)

        @block.tensor
        def _(pe):
            pe.sem_inc(projected, RING)
            pe.wait_ge(w_lo_done, RING + KT)
            with pe.Fori(0, TT // RING) as i:
                for s in range(RING):
                    t = RING * i + s
                    pe.wait_ge(m_lo_done, t + 1)
                    pe.wait_ge(added, t + 1)
                    for k in range(KT):
                        last = three_passes(pe, [ps[:, 2 * s, :], ps[:, 2 * s + 1, :]], m_hi[:, s, k, :], m_lo[:, s, k, :],
                                            [w_hi[:, k, 0:HALF], w_hi[:, k, HALF:D]], [w_lo[:, k, 0:HALF], w_lo[:, k, HALF:D]],
                                            k == 0, k == KT - 1)
                    last.then_inc(projected, 1)

        @block.vector
        def _(dve):
            dve.sem_inc(w_lo_done, RING)
            dve.sem_inc(added, RING)
            for k in range(KT):
                dve.wait_ge(w_hi_done, k + 1)
                dve.tensor_tensor(w_lo[:, k, :], w_raw[:, k % RING, :], w_hi[:, k, :].bitcast(F32), ALU.subtract).then_inc(w_lo_done, 1)
            def rest(t, s):
                dve.wait_ge(m_hi_done, t + 1)
                dve.tensor_tensor(m_lo[:, s, :, :], merged[:, :, ds(t * P, P)], m_hi[:, s, :, :].bitcast(F32),
                                  ALU.subtract).then_inc(m_lo_done, 1)

            with dve.Fori(0, TT // RING) as i:
                for s in range(RING):
                    rest(RING * i + s, s)
                for s in range(RING):
                    t = RING * i + s
                    dve.wait_ge(projected, RING + t + 1)
                    dve.wait_ge(x_loaded[s], DMA * i + DMA)
                    dve.tensor_tensor(x2[:, ds(t, 1), :].rearrange("p a d -> p (a d)"), banks(ps, 2 * s, 2), x_tile[:, s, :],
                                      ALU.add).then_inc(added, 1)


def router_logits(nc, c, ps, x2, gain, w_group, b_group, w_expert, b_expert, h2_rows, logits):
    NL = N_GROUPS + NE
    with ExitStack() as ctx:
        def sb(name, shape, dt=F32):
            return ctx.enter_context(nc.sbuf_tensor(name, shape, dt))

        def sem(name):
            return ctx.enter_context(nc.semaphore(name))

        w_router = sb("w_router", [P, KT, NL])
        b_router = sb("b_router", [P, NL])
        gain_row = sb("gain2_row", [P, D])
        squares = sb("squares2", [P, D])
        sum_sq = sb("sum_sq2", [P, TT])
        mean_sq = sb("mean_sq2", [P, TT])
        root = sb("root2", [P, TT])
        rstd = sb("rstd2", [P, TT])
        h2 = sb("h2", [P, RING, D])
        h2_t = sb("h2_t", [P, RING, KT, P])
        loaded = sem("router_loaded")
        squared = sem("squared2")
        mean_done = sem("mean_done2")
        root_done = sem("root_done2")
        rstd_done = sem("rstd_done2")
        h2_done = sem("h2_done")
        stored = [sem(f"h2_stored{s}") for s in range(RING)]
        turned = sem("h2_turned")
        t_done = sem("h2_t_done")
        routed = sem("routed")
        logit_done = sem("logit_done")
        h2_tiles = h2_rows.rearrange("(t p) d -> t p d", p=P)
        block = ctx.enter_context(nc.Block())

        @block.sync
        def _(sp):
            with nc.allow_non_contiguous_dma(reason="narrow router weights"):
                sp.dma_start(w_router[:, :, 0:N_GROUPS], w_group.rearrange("(k p) g -> p k g", p=P)).then_inc(loaded, DMA)
                sp.dma_start(w_router[:, :, N_GROUPS:NL], w_expert.rearrange("(k p) g -> p k g", p=P)).then_inc(loaded, DMA)
                sp.dma_start(b_router[:, 0:N_GROUPS], b_group.to_broadcast([P, N_GROUPS])).then_inc(loaded, DMA)
                sp.dma_start(b_router[:, N_GROUPS:NL], b_expert.to_broadcast([P, NE])).then_inc(loaded, DMA)
            sp.dma_start(gain_row[:, :], gain.to_broadcast([P, D])).then_inc(loaded, DMA)
            for s in range(RING):
                sp.sem_inc(stored[s], DMA)
            with sp.Fori(0, TT // RING) as i:
                for s in range(RING):
                    sp.wait_ge(h2_done, RING * i + s + 1)
                    sp.dma_start(h2_tiles[ds(RING * i + s, 1)].rearrange("a p d -> p (a d)"), h2[:, s, :]).then_inc(stored[s], DMA)
            for s in range(RING):
                sp.wait_ge(stored[s], DMA * (TT // RING) + DMA)

        @block.scalar
        def _(act):
            act.sem_inc(squared, 1)
            with act.Fori(0, TT) as t:
                act.wait_ge(squared, 1 + t)
                act.activation(squares[:, :], x2[:, ds(t, 1), :].rearrange("p a d -> p (a d)"), ACT.Square,
                               accum_out=sum_sq[:, ds(t, 1)]).then_inc(squared, 1)
            act.wait_ge(mean_done, 1)
            act.activation(root[:, :], mean_sq[:, :], ACT.Sqrt).then_inc(root_done, 1)
            with act.Fori(0, TT // RING) as i:
                for s in range(RING):
                    t = RING * i + s
                    act.wait_ge(turned, RING + t + 1)
                    act.wait_ge(routed, t + 1)
                    act.activation(h2_t[:, s, :, :].rearrange("p k t -> p (k t)"), banks(ps, 2 * s, 2), ACT.Copy).then_inc(t_done, 1)

        @block.vector
        def _(dve):
            dve.sem_inc(logit_done, RING)
            dve.wait_ge(squared, 1 + TT)
            dve.tensor_scalar(mean_sq[:, :], sum_sq[:, :], 1.0 / D, EPS, ALU.mult, ALU.add).then_inc(mean_done, 1)
            dve.wait_ge(root_done, 1)
            dve.reciprocal(rstd[:, :], root[:, :]).then_inc(rstd_done, 1)
            dve.wait_ge(rstd_done, 1)
            dve.wait_ge(loaded, 5 * DMA)
            with dve.Fori(0, TT // RING) as i:
                for s in range(RING):
                    t = RING * i + s
                    dve.wait_ge(turned, t + 1)
                    dve.wait_ge(stored[s], DMA * i + DMA)
                    dve.scalar_tensor_tensor(out=h2[:, s, :], in0=x2[:, ds(t, 1), :].rearrange("p a d -> p (a d)"),
                                             scalar=rstd[:, ds(t, 1)], in1=gain_row[:, :], op0=ALU.mult,
                                             op1=ALU.mult).then_inc(h2_done, 1)
                for s in range(RING):
                    t = RING * i + s
                    dve.wait_ge(routed, RING + t + 1)
                    dve.tensor_tensor(logits[:, ds(t, 1), :].rearrange("p a l -> p (a l)"), ps[:, 4 + s, 0:NL], b_router[:, :],
                                      ALU.add).then_inc(logit_done, 1)

        @block.tensor
        def _(pe):
            pe.sem_inc(turned, RING)
            pe.sem_inc(routed, RING)
            pe.wait_ge(loaded, 5 * DMA)
            with pe.Fori(0, TT // RING) as i:
                for s in range(RING):
                    t = RING * i + s
                    pe.wait_ge(h2_done, t + 1)
                    for k in range(KT):
                        last = pe.transpose(banks(ps, 2 * s, 2)[:, k * P:(k + 1) * P], h2[:, s, k * P:(k + 1) * P], c.ident[:, :])
                    last.then_inc(turned, 1)
                for s in range(RING):
                    t = RING * i + s
                    pe.wait_ge(t_done, t + 1)
                    pe.wait_ge(logit_done, t + 1)
                    for k in range(KT):
                        last = pe.matmul(ps[:, 4 + s, 0:NL], h2_t[:, s, k, :], w_router[:, k, :], start=k == 0, stop=k == KT - 1)
                    last.then_inc(routed, 1)


def route(nc, c, ps, logits, gates, slot_table, gather_src, scatter_dst, over_expert):
    with ExitStack() as ctx:
        def sb(name, shape, dt=F32):
            return ctx.enter_context(nc.sbuf_tensor(name, shape, dt))

        def sem(name):
            return ctx.enter_context(nc.semaphore(name))

        unused = sb("unused", [P, BLOCKS], I32)
        source = sb("source", [P, TOPK, TT], I32)
        expert_no = sb("expert_no", [P, NE])
        expert_base = sb("expert_base", [P, NE])
        block_no = sb("block_no", [P, MAX_OVER])
        limits = sb("limits", [P, TT - 1])
        group_logits = sb("group_logits", [P, TT, 8])
        group_top = sb("group_top", [P, TT, 8])
        group_at = sb("group_at", [P, TT, 8], U32)
        group_index = sb("group_index", [P, TT])
        group_less = sb("group_less", [P, TT, N_GROUPS])
        group_exp = sb("group_exp", [P, TT, N_GROUPS])
        group_sum = sb("group_sum", [P, TT])
        penalty = sb("penalty", [P, TT, N_GROUPS])
        expert_logits = sb("expert_logits", [P, TT, NE])
        expert_top = sb("expert_top", [P, TT, 8])
        expert_at = sb("expert_at", [P, TT, 8], U32)
        choice = sb("choice", [P, TOPK, TT])
        expert_less = sb("expert_less", [P, TT, NE])
        expert_exp = sb("expert_exp", [P, TT, NE])
        expert_sum = sb("expert_sum", [P, TT])
        second_less = sb("second_less", [P, TT])
        second_exp = sb("second_exp", [P, TT])
        denominator = sb("denominator", [P, TT])
        picked = sb("picked", [P, TOPK, TT, NE])
        either = sb("either", [P, TT, NE])
        running = sb("running", [P, TT + 1, NE])
        position = sb("position", [P, TT, NE])
        count = sb("count", [P, NE])
        above = sb("above", [P, NE, TT - 1])
        over = sb("over", [P, NE])
        over_upto = sb("over_upto", [P, NE])
        ones_row = sb("ones_row", [P, NE])
        over_base = sb("over_base", [P, NE])
        base_gap = sb("base_gap", [P, NE])
        low = sb("low", [P, TT, NE])
        slot_of = sb("slot_of", [P, TT, NE])
        slot_pick = sb("slot_pick", [P, TOPK, TT, NE])
        slot_f = sb("slot_f", [P, TOPK, TT])
        slot_i = sb("slot_i", [P, TOPK, TT], I32)
        passed = sb("passed", [P, MAX_OVER, NE])
        over_f = sb("over_f", [P, MAX_OVER + 1])
        table = sb("table", [P, BLOCKS], I32)
        made = sem("route_constants")
        cleared = sem("table_cleared")
        vec = sem("route_vec")
        expd = sem("route_exp")
        placed = sem("route_placed")
        slots_done = sem("slots_done")
        scattered = sem("table_scattered")
        table_loaded = sem("table_loaded")
        block = ctx.enter_context(nc.Block())
        steps = [0]

        def bc(ap, shape, axis):
            return spread(ap, shape, axis)

        @block.gpsimd
        def _(pool):
            pool.memset(group_logits[:, :, :], MASKED)
            pool.memset(ones_row[:, :], 1.0)
            pool.memset(running[:, 0, :], 0.0)
            pool.iota(unused[:, :], pattern=[[1, BLOCKS]], base=TOPK * SEQ, channel_multiplier=BLOCKS)
            pool.iota(source[:, :, :], pattern=[[SEQ, TOPK], [P, TT]], base=0, channel_multiplier=1)
            f = {"allow_small_or_imprecise_dtypes": True}
            pool.iota(expert_no[:, :], pattern=[[1, NE]], base=0, channel_multiplier=0, **f)
            pool.iota(expert_base[:, :], pattern=[[P, NE]], base=0, channel_multiplier=0, **f)
            pool.iota(block_no[:, :], pattern=[[1, MAX_OVER]], base=0, channel_multiplier=0, **f)
            pool.iota(limits[:, :], pattern=[[P, TT - 1]], base=P, channel_multiplier=0, **f).then_inc(made, 1)
            pool.wait_ge(made, 1)
            pool.dma_start(slot_table.rearrange("(p b) a -> p (b a)", p=P), unused[:, :]).then_inc(cleared, DMA)
            pool.wait_ge(cleared, DMA)
            pool.wait_ge(slots_done, 1)
            for k in range(TOPK):
                for t in range(TT):
                    pool.indirect_dma_start(out=slot_table, out_offset=bass.IndirectOffsetOnAxis(ap=slot_i[:, k, t:t + 1], axis=0),
                                            in_=source[:, k, t:t + 1], in_offset=None).then_inc(scattered, DMA)
            pool.wait_ge(scattered, TOPK * TT * DMA)
            pool.dma_start(table[:, :], slot_table.rearrange("(b p) a -> p (b a)", p=P),
                           allow_slow_non_contiguous=True).then_inc(table_loaded, DMA)

        @block.scalar
        def _(act):
            act.wait_ge(expd, 1)
            act.activation(group_exp[:, :, :], group_less[:, :, :], ACT.Exp).then_inc(expd, 1)
            act.wait_ge(expd, 3)
            act.activation(expert_exp[:, :, :], expert_less[:, :, :], ACT.Exp)
            act.activation(second_exp[:, :], second_less[:, :], ACT.Exp).then_inc(expd, 1)

        @block.tensor
        def _(pe):
            pe.wait_ge(placed, 1)
            flat = ps[:, 0, 0:TT * NE]
            pe.matmul(flat, c.tri_before[:, :], either[:, :, :].rearrange("p t e -> p (t e)"), start=True, stop=False)
            pe.matmul(flat, c.ones[:, :], running[:, 0:TT, :].rearrange("p t e -> p (t e)"), start=False, stop=True)
            pe.matmul(ps[:, 1, 0:NE], c.ones[:, :], running[:, TT, :], start=True, stop=True).then_inc(placed, 1)

        @block.vector
        def _(dve):
            def then(ins):
                steps[0] += 1
                ins.then_inc(vec, 1)
                dve.wait_ge(vec, steps[0])

            dve.wait_ge(made, 1)
            then(dve.tensor_copy(group_logits[:, :, 0:N_GROUPS], logits[:, :, 0:N_GROUPS]))
            for t in range(TT):
                ins = dve.max(group_top[:, t, :], group_logits[:, t, :])
            then(ins)
            for t in range(TT):
                ins = dve.max_index(group_at[:, t, :], group_top[:, t, :], group_logits[:, t, :])
            then(ins)
            dve.tensor_tensor(group_less[:, :, :], logits[:, :, 0:N_GROUPS],
                              group_top[:, :, 0:1].to_broadcast([P, TT, N_GROUPS]), ALU.subtract).then_inc(expd, 1)
            then(dve.tensor_copy(group_index[:, :], group_at[:, :, 0]))
            then(dve.tensor_tensor(penalty[:, :, :], bc(expert_no[:, 0:N_GROUPS], [P, TT, N_GROUPS], 1),
                                   bc(group_index[:, :], [P, TT, N_GROUPS], 2), ALU.is_equal))
            then(dve.tensor_scalar(penalty[:, :, :], penalty[:, :, :], -MASKED, MASKED, ALU.mult, ALU.add))
            then(dve.tensor_tensor(expert_logits[:, :, :].rearrange("p t (g e) -> p t g e", g=N_GROUPS),
                                   logits[:, :, N_GROUPS:].rearrange("p t (g e) -> p t g e", g=N_GROUPS),
                                   bc(penalty[:, :, :], [P, TT, N_GROUPS, PER_GROUP], 3), ALU.add))
            for t in range(TT):
                ins = dve.max(expert_top[:, t, :], expert_logits[:, t, :])
            then(ins)
            for t in range(TT):
                ins = dve.max_index(expert_at[:, t, :], expert_top[:, t, :], expert_logits[:, t, :])
            then(ins)
            dve.wait_ge(expd, 2)
            dve.tensor_tensor(expert_less[:, :, :], expert_logits[:, :, :], expert_top[:, :, 0:1].to_broadcast([P, TT, NE]),
                              ALU.subtract)
            dve.tensor_tensor(second_less[:, :], expert_top[:, :, 1], expert_top[:, :, 0], ALU.subtract).then_inc(expd, 1)
            dve.tensor_reduce(group_sum[:, :], group_exp[:, :, :], AX.X, ALU.add)
            for k in range(TOPK):
                ins = dve.tensor_copy(choice[:, k, :], expert_at[:, :, k])
            then(ins)
            for k in range(TOPK):
                ins = dve.tensor_tensor(picked[:, k, :, :], bc(expert_no[:, :], [P, TT, NE], 1),
                                        bc(choice[:, k, :], [P, TT, NE], 2), ALU.is_equal)
            then(ins)
            then(dve.tensor_tensor(either[:, :, :], picked[:, 0, :, :], picked[:, 1, :, :], ALU.add))
            for t in range(TT):
                then(dve.tensor_tensor(running[:, t + 1, :], running[:, t, :], either[:, t, :], ALU.add))
            dve.sem_inc(placed, 1)
            dve.wait_ge(expd, 4)
            then(dve.tensor_reduce(expert_sum[:, :], expert_exp[:, :, :], AX.X, ALU.add))
            then(dve.tensor_tensor(denominator[:, :], group_sum[:, :], expert_sum[:, :], ALU.mult))
            then(dve.reciprocal(gates[:, 0, :], denominator[:, :]))
            dve.tensor_tensor(gates[:, 1, :], gates[:, 0, :], second_exp[:, :], ALU.mult)
            dve.wait_ge(placed, 2)
            dve.tensor_copy(position[:, :, :].rearrange("p t e -> p (t e)"), ps[:, 0, 0:TT * NE])
            then(dve.tensor_copy(count[:, :], ps[:, 1, 0:NE]))
            then(dve.tensor_tensor(above[:, :, :], bc(count[:, :], [P, NE, TT - 1], 2), bc(limits[:, :], [P, NE, TT - 1], 1), ALU.is_gt))
            then(dve.tensor_reduce(over[:, :], above[:, :, :], AX.X, ALU.add))
            then(dve.tensor_tensor_scan(over_upto[:, :], ones_row[:, :], over[:, :], 0.0, ALU.mult, ALU.add))
            then(dve.tensor_tensor(over_base[:, :], over_upto[:, :], over[:, :], ALU.subtract))
            then(dve.tensor_scalar(over_base[:, :], over_base[:, :], float(NE - 1), float(P), ALU.add, ALU.mult))
            dve.tensor_tensor(base_gap[:, :], expert_base[:, :], over_base[:, :], ALU.subtract)
            then(dve.tensor_scalar(low[:, :, :], position[:, :, :], float(P), None, ALU.is_lt))
            then(dve.tensor_tensor(slot_of[:, :, :], low[:, :, :], bc(base_gap[:, :], [P, TT, NE], 1), ALU.mult))
            then(dve.tensor_tensor(slot_of[:, :, :], slot_of[:, :, :], bc(over_base[:, :], [P, TT, NE], 1), ALU.add))
            then(dve.tensor_tensor(slot_of[:, :, :], slot_of[:, :, :], position[:, :, :], ALU.add))
            for k in range(TOPK):
                ins = dve.tensor_tensor(slot_pick[:, k, :, :], picked[:, k, :, :], slot_of[:, :, :], ALU.mult)
            then(ins)
            then(dve.tensor_reduce(slot_f[:, :, :], slot_pick[:, :, :, :], AX.X, ALU.add))
            dve.tensor_copy(slot_i[:, :, :], slot_f[:, :, :]).then_inc(slots_done, 1)
            then(dve.tensor_tensor(passed[:, :, :], bc(over_upto[:, :], [P, MAX_OVER, NE], 1),
                                   bc(block_no[:, :], [P, MAX_OVER, NE], 2), ALU.is_le))
            then(dve.tensor_reduce(over_f[:, 0:MAX_OVER], passed[:, :, :], AX.X, ALU.add))
            then(dve.tensor_scalar(over_f[:, 0:MAX_OVER], over_f[:, 0:MAX_OVER], float(NE - 1), None, ALU.min))
            then(dve.tensor_copy(over_f[:, MAX_OVER:], over_upto[:, NE - 1:NE]))
            dve.tensor_copy(over_expert[:, :], over_f[:, :])
            dve.wait_ge(table_loaded, DMA)
            dve.tensor_copy(scatter_dst[:, :], table[:, :])
            dve.tensor_scalar(gather_src[:, :], table[:, :], SEQ - 1, None, ALU.bitwise_and)


def experts(nc, c, ps, w1, w3, w2, h2_rows, y_rows, gather_src, scatter_dst):
    with ExitStack() as ctx:
        def sb(name, shape, dt=F32):
            return ctx.enter_context(nc.sbuf_tensor(name, shape, dt))

        def sem(name):
            return ctx.enter_context(nc.semaphore(name))

        w1_sb = sb("w1_sb", [P, RING, KT, FF])
        w3_sb = sb("w3_sb", [P, RING, KT, FF])
        w2_sb = sb("w2_sb", [P, RING, FT, D])
        index = sb("index", [P, RING, 2], I32)
        x_rows = sb("x_rows", [P, RING, D])
        x_t = sb("x_t", [P, RING, KT, P])
        act_up = sb("act_up", [P, FF])
        g_tok = sb("g_tok", [P, RING, FF])
        g_t = sb("g_t", [P, RING, FT, P])
        y_out = sb("y_out", [P, RING, D])
        w1_loaded = [sem(f"w1_loaded{s}") for s in range(RING)]
        w3_loaded = [sem(f"w3_loaded{s}") for s in range(RING)]
        w2_loaded = [sem(f"w2_loaded{s}") for s in range(RING)]
        held = sem("experts_held")
        indexed = sem("indexed")
        aimed = sem("aimed")
        gathered = [sem(f"gathered{s}") for s in range(RING)]
        scattered = [sem(f"scattered{s}") for s in range(RING)]
        x_turned = sem("moe_x_turned")
        x_ready = sem("moe_x_ready")
        up_done = sem("up_done")
        silu_done = sem("moe_silu_done")
        g_done = sem("g_done")
        g_turned = sem("g_turned")
        g_ready = sem("g_ready")
        down_done = sem("down_done")
        y_ready = sem("y_ready")
        y_free = sem("y_free")
        w1_rows = w1.rearrange("e (k p) f -> e p k f", p=P)
        w3_rows = w3.rearrange("e (k p) f -> e p k f", p=P)
        w2_rows = w2.rearrange("e (k p) f -> e p k f", p=P)
        block = ctx.enter_context(nc.Block())

        def of(ap, n):
            return ap[ds(n, 1)].rearrange("e p k f -> p (e k) f")

        @block.sync
        def _(sp):
            with sp.Fori(0, NE // RING) as i:
                for s in range(RING):
                    n = RING * i + s
                    sp.wait_ge(up_done, n + 1)
                    sp.dma_start(w1_sb[:, s, :, :], of(w1_rows, n)).then_inc(w1_loaded[s], DMA)
                    sp.dma_start(w3_sb[:, s, :, :], of(w3_rows, n)).then_inc(w3_loaded[s], DMA)
                    sp.wait_ge(down_done, n + 1)
                    sp.dma_start(w2_sb[:, s, :, :], of(w2_rows, n)).then_inc(w2_loaded[s], DMA)

        @block.gpsimd
        def _(pool):
            def gather(n, s):
                pool.wait_ge(x_turned, n + 1)
                pool.tensor_copy(index[:, s, 0:1], gather_src[:, ds(n, 1)]).then_inc(indexed, 1)
                pool.wait_ge(indexed, n + 1)
                pool.sem_inc(held, 1)
                pool.indirect_dma_start(out=x_rows[:, s, :], out_offset=None, in_=h2_rows,
                                        in_offset=bass.IndirectOffsetOnAxis(ap=index[:, s, 0:1], axis=0)).then_inc(gathered[s], DMA)

            def scatter(n, s, i):
                if i is not None:
                    pool.wait_ge(scattered[s], DMA * i)
                    pool.sem_inc(y_free, 1)
                pool.tensor_copy(index[:, s, 1:2], scatter_dst[:, ds(n, 1)]).then_inc(aimed, 1)
                pool.wait_ge(aimed, n + 1)
                pool.wait_ge(y_ready, 1 + n + 1)
                pool.sem_inc(held, 1)
                pool.indirect_dma_start(out=y_rows, out_offset=bass.IndirectOffsetOnAxis(ap=index[:, s, 1:2], axis=0),
                                        in_=y_out[:, s, :], in_offset=None).then_inc(scattered[s], DMA)

            pool.sem_inc(y_free, RING)
            for s in range(RING):
                gather(s, s)
            for s in range(RING):
                gather(RING + s, s)
                scatter(s, s, None)
            with pool.Fori(0, NE // RING - 2) as i:
                for s in range(RING):
                    gather(RING * i + s + 2 * RING, s)
                    scatter(RING * i + s + RING, s, i + 1)
            for s in range(RING):
                scatter(NE - RING + s, s, NE // RING - 1)
            for s in range(RING):
                pool.wait_ge(scattered[s], DMA * (NE // RING))

        @block.scalar
        def _(act):
            act.sem_inc(x_ready, 1)

            def x_out(n, s):
                act.wait_ge(x_turned, RING + n + 1)
                act.wait_ge(up_done, n + 1)
                act.activation(x_t[:, s, :, :].rearrange("p k t -> p (k t)"), banks(ps, 0, 2), ACT.Copy).then_inc(x_ready, 1)

            def silu(n):
                act.wait_ge(up_done, RING + n + 1)
                act.wait_ge(g_done, 1 + n)
                act.activation(act_up[:, :], ps[:, 2, :], ACT.Silu).then_inc(silu_done, 1)

            x_out(0, 0)
            with act.Fori(0, NE // RING - 1) as i:
                for s in range(RING):
                    x_out(RING * i + s + 1, 1 - s)
                    silu(RING * i + s)
            x_out(NE - 1, 1)
            silu(NE - 2)
            silu(NE - 1)

        @block.vector
        def _(dve):
            for ready in (g_done, g_ready, y_ready):
                dve.sem_inc(ready, 1)

            def step(n, s):
                dve.wait_ge(silu_done, n + 1)
                dve.wait_ge(g_turned, 1 + n)
                dve.tensor_tensor(g_tok[:, s, :], ps[:, 3, :], act_up[:, :], ALU.mult).then_inc(g_done, 1)

            def g_out(n, s):
                dve.wait_ge(g_turned, 1 + n + 1)
                dve.wait_ge(down_done, n + 1)
                dve.tensor_copy(g_t[:, s, :, :].rearrange("p k t -> p (k t)"), ps[:, 4, :]).then_inc(g_ready, 1)

            def y_copy(n, s):
                dve.wait_ge(down_done, RING + n + 1)
                dve.wait_ge(y_free, n + 1)
                dve.tensor_copy(y_out[:, s, :], banks(ps, 5, 2)).then_inc(y_ready, 1)

            step(0, 0)
            with dve.Fori(0, NE // RING - 1) as i:
                for s in range(RING):
                    n = RING * i + s
                    g_out(n, s)
                    step(n + 1, 1 - s)
                    y_copy(n, s)
            g_out(NE - 2, 0)
            step(NE - 1, 1)
            y_copy(NE - 2, 0)
            g_out(NE - 1, 1)
            y_copy(NE - 1, 1)

        @block.tensor
        def _(pe):
            pe.sem_inc(x_turned, RING)
            pe.sem_inc(up_done, RING)
            pe.sem_inc(down_done, RING)
            pe.sem_inc(g_turned, 1)

            def turn_x(n, s, i):
                pe.wait_ge(gathered[s], DMA * i + DMA)
                pe.wait_ge(x_ready, 1 + n)
                for k in range(KT):
                    last = pe.transpose(ps[:, k // 4, (k % 4) * P:(k % 4 + 1) * P], x_rows[:, s, k * P:(k + 1) * P], c.ident[:, :])
                last.then_inc(x_turned, 1)

            def turn_g(n, s):
                pe.wait_ge(g_done, 1 + n + 1)
                pe.wait_ge(g_ready, 1 + n)
                for k in range(FT):
                    last = pe.transpose(ps[:, 4, k * P:(k + 1) * P], g_tok[:, s, k * P:(k + 1) * P], c.ident[:, :])
                last.then_inc(g_turned, 1)

            def up(n, s, i):
                pe.wait_ge(x_ready, 1 + n + 1)
                pe.wait_ge(g_done, 1 + n)
                pe.wait_ge(w1_loaded[s], DMA * i + DMA)
                for k in range(KT):
                    pe.matmul(ps[:, 2, :], x_t[:, s, k, :], w1_sb[:, s, k, :], start=k == 0, stop=k == KT - 1)
                pe.wait_ge(w3_loaded[s], DMA * i + DMA)
                for k in range(KT):
                    last = pe.matmul(ps[:, 3, :], x_t[:, s, k, :], w3_sb[:, s, k, :], start=k == 0, stop=k == KT - 1)
                last.then_inc(up_done, 1)

            def down(n, s, i):
                pe.wait_ge(g_ready, 1 + n + 1)
                pe.wait_ge(y_ready, 1 + n)
                pe.wait_ge(w2_loaded[s], DMA * i + DMA)
                for k in range(FT):
                    for h in range(2):
                        last = pe.matmul(ps[:, 5 + h, :], g_t[:, s, k, :], w2_sb[:, s, k, h * HALF:(h + 1) * HALF],
                                         start=k == 0, stop=k == FT - 1)
                last.then_inc(down_done, 1)

            turn_x(0, 0, 0)
            turn_x(1, 1, 0)
            up(0, 0, 0)
            with pe.Fori(0, NE // RING - 1) as i:
                turn_x(2 * i + 2, 0, i + 1)
                turn_g(2 * i, 0)
                up(2 * i + 1, 1, i)
                down(2 * i, 0, i)
                turn_x(2 * i + 3, 1, i + 1)
                turn_g(2 * i + 1, 1)
                up(2 * i + 2, 0, i + 1)
                down(2 * i + 1, 1, i)
            turn_g(NE - 2, 0)
            up(NE - 1, 1, NE // RING - 1)
            down(NE - 2, 0, NE // RING - 1)
            turn_g(NE - 1, 1)
            down(NE - 1, 1, NE // RING - 1)


def overflow(nc, c, ps, w1, w3, w2, h2_rows, y_rows, gather_src, scatter_dst, over_expert):
    with ExitStack() as ctx:
        def sb(name, shape, dt=F32):
            return ctx.enter_context(nc.sbuf_tensor(name, shape, dt))

        def sem(name):
            return ctx.enter_context(nc.semaphore(name))

        w1_sb = sb("over_w1", [P, KT, FF])
        w3_sb = sb("over_w3", [P, KT, FF])
        w2_sb = sb("over_w2", [P, FT, D])
        index = sb("over_index", [P, 2], I32)
        x_rows = sb("over_x", [P, D])
        x_t = sb("over_x_t", [P, KT, P])
        act_up = sb("over_act_up", [P, FF])
        g_tok = sb("over_g", [P, FF])
        g_t = sb("over_g_t", [P, FT, P])
        y_out = sb("over_y", [P, D])
        loaded = sem("over_loaded")
        held = sem("over_held")
        indexed = sem("over_indexed")
        gathered = sem("over_gathered")
        x_turned = sem("over_x_turned")
        x_ready = sem("over_x_ready")
        up_done = sem("over_up_done")
        silu_done = sem("over_silu_done")
        g_done = sem("over_g_done")
        g_turned = sem("over_g_turned")
        g_ready = sem("over_g_ready")
        down_done = sem("over_down_done")
        y_ready = sem("over_y_ready")
        scattered = sem("over_scattered")
        w1_rows = w1.rearrange("e (k p) f -> e p k f", p=P)
        w3_rows = w3.rearrange("e (k p) f -> e p k f", p=P)
        w2_rows = w2.rearrange("e (k p) f -> e p k f", p=P)
        block = ctx.enter_context(nc.Block())

        def each(eng, body):
            blocks = eng.value_load(over_expert[0:1, MAX_OVER:MAX_OVER + 1], min_val=0, max_val=MAX_OVER)
            with eng.If(blocks > 0):
                with eng.Fori(0, MAX_OVER) as b:
                    with eng.If(b < blocks):
                        body(b)

        @block.sync
        def _(sp):
            def body(b):
                e = sp.value_load(over_expert[0:1, ds(b, 1)], min_val=0, max_val=NE - 1)
                sp.wait_ge(down_done, 1 + b)
                for dst, src in ((w1_sb, w1_rows), (w3_sb, w3_rows), (w2_sb, w2_rows)):
                    sp.dma_start(dst[:, :, :], src[ds(e, 1)].rearrange("e p k f -> p (e k) f")).then_inc(loaded, DMA)

            each(sp, body)

        @block.gpsimd
        def _(pool):
            def body(b):
                pool.tensor_copy(index[:, 0:1], gather_src[:, ds(NE + b, 1)])
                pool.tensor_copy(index[:, 1:2], scatter_dst[:, ds(NE + b, 1)]).then_inc(indexed, 1)
                pool.wait_ge(indexed, b + 1)
                pool.sem_inc(held, 1)
                pool.indirect_dma_start(out=x_rows[:, :], out_offset=None, in_=h2_rows,
                                        in_offset=bass.IndirectOffsetOnAxis(ap=index[:, 0:1], axis=0)).then_inc(gathered, DMA)
                pool.wait_ge(y_ready, 1 + b + 1)
                pool.sem_inc(held, 1)
                pool.indirect_dma_start(out=y_rows, out_offset=bass.IndirectOffsetOnAxis(ap=index[:, 1:2], axis=0),
                                        in_=y_out[:, :], in_offset=None).then_inc(scattered, DMA)
                pool.wait_ge(scattered, DMA * b + DMA)

            each(pool, body)

        @block.scalar
        def _(act):
            def body(b):
                act.wait_ge(x_turned, b + 1)
                act.activation(x_t[:, :, :].rearrange("p k t -> p (k t)"), banks(ps, 0, 2), ACT.Copy).then_inc(x_ready, 1)
                act.wait_ge(up_done, b + 1)
                act.activation(act_up[:, :], ps[:, 2, :], ACT.Silu).then_inc(silu_done, 1)

            each(act, body)

        @block.vector
        def _(dve):
            dve.sem_inc(y_ready, 1)

            def body(b):
                dve.wait_ge(silu_done, b + 1)
                dve.tensor_tensor(g_tok[:, :], ps[:, 3, :], act_up[:, :], ALU.mult).then_inc(g_done, 1)
                dve.wait_ge(g_turned, b + 1)
                dve.tensor_copy(g_t[:, :, :].rearrange("p k t -> p (k t)"), ps[:, 4, :]).then_inc(g_ready, 1)
                dve.wait_ge(down_done, 1 + b + 1)
                dve.tensor_copy(y_out[:, :], banks(ps, 5, 2)).then_inc(y_ready, 1)

            each(dve, body)

        @block.tensor
        def _(pe):
            pe.sem_inc(down_done, 1)

            def body(b):
                pe.wait_ge(gathered, DMA * b + DMA)
                for k in range(KT):
                    last = pe.transpose(ps[:, k // 4, (k % 4) * P:(k % 4 + 1) * P], x_rows[:, k * P:(k + 1) * P], c.ident[:, :])
                last.then_inc(x_turned, 1)
                pe.wait_ge(x_ready, b + 1)
                pe.wait_ge(loaded, 3 * DMA * b + 3 * DMA)
                for n, w in ((2, w1_sb), (3, w3_sb)):
                    for k in range(KT):
                        last = pe.matmul(ps[:, n, :], x_t[:, k, :], w[:, k, :], start=k == 0, stop=k == KT - 1)
                last.then_inc(up_done, 1)
                pe.wait_ge(g_done, b + 1)
                for k in range(FT):
                    last = pe.transpose(ps[:, 4, k * P:(k + 1) * P], g_tok[:, k * P:(k + 1) * P], c.ident[:, :])
                last.then_inc(g_turned, 1)
                pe.wait_ge(g_ready, b + 1)
                pe.wait_ge(y_ready, 1 + b)
                for k in range(FT):
                    for h in range(2):
                        last = pe.matmul(ps[:, 5 + h, :], g_t[:, k, :], w2_sb[:, k, h * HALF:(h + 1) * HALF],
                                         start=k == 0, stop=k == FT - 1)
                last.then_inc(down_done, 1)

            each(pe, body)


def finish(nc, x2, gates, y_rows, gain, out):
    with ExitStack() as ctx:
        def sb(name, shape, dt=F32):
            return ctx.enter_context(nc.sbuf_tensor(name, shape, dt))

        def sem(name):
            return ctx.enter_context(nc.semaphore(name))

        gain_row = sb("final_row", [P, D])
        y_tile = sb("y_tile", [P, RING, TOPK, D])
        total = sb("total", [P, RING, D])
        squares = sb("final_squares", [P, D])
        sum_sq = sb("final_sum", [P, TT])
        mean_sq = sb("final_mean", [P, TT])
        root = sb("final_root", [P, TT])
        rstd = sb("final_rstd", [P, TT])
        result = sb("result", [P, RING, D])
        gain_loaded = sem("final_gain_loaded")
        y_loaded = [sem(f"y_loaded{s}") for s in range(RING)]
        first_added = sem("first_added")
        summed = sem("final_summed")
        squared = sem("final_squared")
        mean_done = sem("final_mean_done")
        root_done = sem("final_root_done")
        rstd_done = sem("final_rstd_done")
        scaled = sem("final_scaled")
        stored = [sem(f"out_stored{s}") for s in range(RING)]
        y_tiles = y_rows[0:TOPK * SEQ].rearrange("(k t p) d -> t p k d", k=TOPK, p=P)
        out_tiles = out[0].rearrange("(t p) d -> t p d", p=P)
        block = ctx.enter_context(nc.Block())

        @block.sync
        def _(sp):
            sp.dma_start(gain_row[:, :], gain.rearrange("(a d) -> a d", a=1).to_broadcast([P, D])).then_inc(gain_loaded, DMA)
            with sp.Fori(0, TT // RING) as i:
                for s in range(RING):
                    sp.wait_ge(summed, RING * i + s + 1)
                    sp.dma_start(y_tile[:, s, :, :], y_tiles[ds(RING * i + s, 1)].rearrange("a p k d -> p (a k) d")).then_inc(y_loaded[s], DMA)

        @block.scalar
        def _(act):
            act.sem_inc(squared, RING)
            for s in range(RING):
                act.sem_inc(stored[s], DMA)
            with act.Fori(0, TT // RING) as i:
                for s in range(RING):
                    t = RING * i + s
                    act.wait_ge(summed, RING + t + 1)
                    act.wait_ge(squared, RING + t)
                    act.activation(squares[:, :], total[:, s, :], ACT.Square, accum_out=sum_sq[:, ds(t, 1)]).then_inc(squared, 1)
                    act.wait_ge(mean_done, t + 1)
                    act.activation(root[:, ds(t, 1)], mean_sq[:, ds(t, 1)], ACT.Sqrt).then_inc(root_done, 1)
                    act.wait_ge(scaled, t + 1)
                    act.dma_start(out_tiles[ds(t, 1)].rearrange("a p d -> p (a d)"), result[:, s, :]).then_inc(stored[s], DMA)
            for s in range(RING):
                act.wait_ge(stored[s], DMA * (TT // RING) + DMA)

        @block.vector
        def _(dve):
            dve.sem_inc(summed, RING)
            dve.wait_ge(gain_loaded, DMA)
            with dve.Fori(0, TT // RING) as i:
                for s in range(RING):
                    t = RING * i + s
                    dve.wait_ge(y_loaded[s], DMA * i + DMA)
                    dve.scalar_tensor_tensor(out=total[:, s, :], in0=y_tile[:, s, 0, :], scalar=gates[:, 0, ds(t, 1)],
                                             in1=x2[:, ds(t, 1), :].rearrange("p a d -> p (a d)"), op0=ALU.mult,
                                             op1=ALU.add).then_inc(first_added, 1)
                    dve.wait_ge(first_added, t + 1)
                    dve.scalar_tensor_tensor(out=total[:, s, :], in0=y_tile[:, s, 1, :], scalar=gates[:, 1, ds(t, 1)],
                                             in1=total[:, s, :], op0=ALU.mult, op1=ALU.add).then_inc(summed, 1)
                for s in range(RING):
                    t = RING * i + s
                    dve.wait_ge(squared, RING + t + 1)
                    dve.tensor_scalar(mean_sq[:, ds(t, 1)], sum_sq[:, ds(t, 1)], 1.0 / D, EPS, ALU.mult, ALU.add).then_inc(mean_done, 1)
                    dve.wait_ge(root_done, t + 1)
                    dve.reciprocal(rstd[:, ds(t, 1)], root[:, ds(t, 1)]).then_inc(rstd_done, 1)
                    dve.wait_ge(rstd_done, t + 1)
                    dve.wait_ge(stored[s], DMA * i + DMA)
                    dve.scalar_tensor_tensor(out=result[:, s, :], in0=total[:, s, :], scalar=rstd[:, ds(t, 1)], in1=gain_row[:, :],
                                             op0=ALU.mult, op1=ALU.mult).then_inc(scaled, 1)


def clear_semaphores(nc):
    used = sorted(nc.released_uncleared_semaphores)
    nc.gpsimd.sem_clear(range(used[0], used[-1] + 1))
    nc.all_engine_barrier()


def load_taps(nc, conv_w, conv_b, taps, bias):
    with ExitStack() as ctx:
        loaded = ctx.enter_context(nc.semaphore("taps_loaded"))
        block = ctx.enter_context(nc.Block())

        @block.sync
        def _(sp):
            with nc.allow_non_contiguous_dma(reason="five numbers a channel"):
                for j in range(CONV):
                    sp.dma_start(taps[:, j, :], conv_w[0][j].rearrange("(b p) -> p b", p=P)).then_inc(loaded, DMA)
                sp.dma_start(bias[:, :], conv_b[0].rearrange("(b p) -> p b", p=P)).then_inc(loaded, DMA)
            sp.wait_ge(loaded, (CONV + 1) * DMA)


def trunk(nc, x, norm_mix_g, w_in, b_f, conv_w, conv_b, dt_bias, a_log, d_skip, ssd_norm_g, w_br_attn, w_br_ssd,
          w_out, norm_ffn_g, w_group_router, b_group_router, w_expert_router, b_expert_router, w1, w3, w2, final_g, out):
    with ExitStack() as ctx:
        def sb(name, shape, dt=F32):
            return ctx.enter_context(nc.sbuf_tensor(name, shape, dt))

        def dram(name, shape, dt=F32):
            return nc.dram_tensor(name, shape, dt, kind="Internal").ap()

        ps = ctx.enter_context(nc.psum_tensor("ps", [P, 8, HALF], F32))
        c = Constants(ident=sb("ident", [P, P]), ident_bf=sb("ident_bf", [P, P], BF16), ones=sb("ones", [P, P]),
                            tri=sb("tri", [P, P]), tri_after=sb("tri_after", [P, P]), tri_before=sb("tri_before", [P, P]),
                            causal_bf=sb("causal_bf", [P, P], BF16))
        dt_tok = sb("dt_tok", [P, TT, SSD_HEADS])
        a_tok = sb("a_tok", [P, TT, SSD_HEADS])
        gates = sb("gates", [P, TOPK, TT])
        logits = sb("logits", [P, TT, N_GROUPS + NE])
        gather_src = sb("gather_src", [P, BLOCKS], I32)
        scatter_dst = sb("scatter_dst", [P, BLOCKS], I32)
        over_expert = sb("over_expert", [P, MAX_OVER + 1], I32)
        f_rows = dram("f_rows", (HEADS, SEQ))
        silu_z = dram("silu_z", (XB, P, SEQ))
        gate_rows = dram("gate_rows", (2 * KT, P, SEQ))
        h2_rows = dram("h2_rows", (SEQ, D))
        y_rows = dram("y_rows", (TOPK * SEQ + BLOCKS * P, D))
        slot_table = dram("slot_table", (BLOCKS * P, 1), I32)
        make_constants(nc, c)

        held_at = (nc.sbuf_base + 31) // 32 * 32
        sb("held", [P, TT * D + 8])
        size = (D_ATTN // P) * SEQ * 4
        ya_hi = nc.alloc_sbuf_tensor_at("ya_hi", [P, D_ATTN // P, SEQ], F32R, offset=held_at)
        ya_lo = nc.alloc_sbuf_tensor_at("ya_lo", [P, D_ATTN // P, SEQ], F32R, offset=held_at + size)
        x2 = nc.alloc_sbuf_tensor_at("x2", [P, TT, D], F32, offset=held_at)
        with ExitStack() as mixer:
            xbc = mixer.enter_context(nc.sbuf_tensor("xbc", [P, CB, SEQ], F32))
            gated = xbc[:, 0:XB, :]
            merged = xbc[:, 0:KT, :]
            with ExitStack() as proj:
                h_hi = proj.enter_context(nc.sbuf_tensor("h_hi", [P, KT, SEQ], F32R))
                h_lo = proj.enter_context(nc.sbuf_tensor("h_lo", [P, KT, SEQ], F32R))
                taps = proj.enter_context(nc.sbuf_tensor("taps", [P, CONV, CB], F32))
                bias = proj.enter_context(nc.sbuf_tensor("conv_bias", [P, CB], F32))
                normalise_input(nc, c, ps, x, norm_mix_g, h_hi, h_lo)
                load_taps(nc, conv_w, conv_b, taps, bias)
                decays(nc, c, ps, w_in[0], b_f, dt_bias, a_log, h_hi, h_lo, f_rows, dt_tok, a_tok)
                project(nc, ps, w_in[0], COL_Q, CB, h_hi, h_lo, "keep", xbc, None)
                attention(nc, c, ps, xbc, f_rows, ya_hi, ya_lo)
                project(nc, ps, w_in[0], COL_Z, XB, h_hi, h_lo, "silu", silu_z, None)
                project(nc, ps, w_in[0], COL_GA, 2 * KT, h_hi, h_lo, "sigmoid", gate_rows, None)
                project(nc, ps, w_in[0], COL_XBC, CB, h_hi, h_lo, "conv", xbc, (taps, bias))
            state_space(nc, c, ps, xbc, dt_tok, a_tok, d_skip, silu_z, gated)
            with ExitStack() as branch:
                ys_hi = branch.enter_context(nc.sbuf_tensor("ys_hi", [P, XB, SEQ], F32R))
                ys_lo = branch.enter_context(nc.sbuf_tensor("ys_lo", [P, XB, SEQ], F32R))
                normalise_ssd(nc, c, ps, gated, ssd_norm_g, ys_hi, ys_lo)
                merge(nc, ps, w_br_attn[0], w_br_ssd[0], gate_rows, ya_hi, ya_lo, ys_hi, ys_lo, merged)
            project_out(nc, ps, w_out[0], x, merged, x2)
        clear_semaphores(nc)
        router_logits(nc, c, ps, x2, norm_ffn_g, w_group_router[0], b_group_router, w_expert_router[0], b_expert_router,
                      h2_rows, logits)
        route(nc, c, ps, logits, gates, slot_table, gather_src, scatter_dst, over_expert)
        experts(nc, c, ps, w1[0], w3[0], w2[0], h2_rows, y_rows, gather_src, scatter_dst)
        overflow(nc, c, ps, w1[0], w3[0], w2[0], h2_rows, y_rows, gather_src, scatter_dst, over_expert)
        finish(nc, x2, gates, y_rows, final_g, out)


_INS = ["x", "norm_mix_g", "w_in", "b_f", "conv_w", "conv_b", "dt_bias", "a_log", "d_skip", "ssd_norm_g", "w_br_attn",
        "w_br_ssd", "w_out", "norm_ffn_g", "w_group_router", "b_group_router", "w_expert_router", "b_expert_router",
        "w1", "w3", "w2", "final_g"]


def kernel(**inputs):
    import numpy as np
    import concourse.bacc as bacc
    from concourse.bass_utils import run_bass_kernel_spmd

    nc = bacc.Bacc("TRN2", target_bir_lowering=False, num_devices=1)
    arrays, args = {}, []
    for name in _INS:
        a = np.ascontiguousarray(inputs[name])
        arrays[f"in_{name}"] = a
        args.append(nc.dram_tensor(f"in_{name}", a.shape, mybir.dt.from_np(a.dtype), kind="ExternalInput").ap())
    args.append(nc.dram_tensor("result_dram", (1, SEQ, D), F32, kind="ExternalOutput").ap())
    trunk(nc, *args)
    nc.compile()
    r = run_bass_kernel_spmd(nc, [arrays], core_ids=[0])
    return r.results[0]["result_dram"]
```

```python
from collections import namedtuple
from contextlib import ExitStack

import concourse.bass as bass
from concourse import mybir

F32 = mybir.dt.float32
F32R = mybir.dt.float32r
BF16 = mybir.dt.bfloat16
I32 = mybir.dt.int32
U32 = mybir.dt.uint32
ACT = mybir.ActivationFunctionType
ALU = mybir.AluOpType
AX = mybir.AxisListType
ds = bass.ds

P = 128
SEQ = 1024
D = 1024
KT = D // P
TT = SEQ // P
HALF = 512
RING = 2
DMA = 16
EPS = 1e-6

HEADS = 8
HD = 64
D_ATTN = HEADS * HD
SSD_HEADS = 16
SSD_HD = 64
D_SSD = SSD_HEADS * SSD_HD
GROUPS = 2
STATE = 128
CONV = 4
CONV_CH = D_SSD + 2 * GROUPS * STATE
CB = CONV_CH // P
XB = D_SSD // P

COL_Q = 0
COL_F = 3 * D_ATTN
COL_Z = COL_F + HEADS
COL_XBC = COL_Z + D_SSD
COL_DT = COL_XBC + CONV_CH
COL_GA = COL_DT + SSD_HEADS
COL_GS = COL_GA + D
DT_ROW = 32
SMALL = 64

N_GROUPS = 4
PER_GROUP = 8
NE = N_GROUPS * PER_GROUP
FF = 512
FT = FF // P
TOPK = 2
SLOTS = P
MAX_OVER = SEQ * TOPK // P
BLOCKS = NE + MAX_OVER
MASKED = -1.0e30


Constants = namedtuple("Constants", "ident ident_bf ones tri tri_after tri_before causal_bf")


def region(nc, ctx, name, size):
    at = (nc.sbuf_base + 31) // 32 * 32
    ctx.enter_context(nc.sbuf_tensor(name, [P, size // 4 + 8], F32))
    return at


def banks(ps, first, n):
    return ps[:, first:first + n, :].rearrange("p b c -> p (b c)")


def make_constants(nc, c):
    with ExitStack() as ctx:
        made = ctx.enter_context(nc.semaphore("const_filled"))
        selected = ctx.enter_context(nc.semaphore("const_selected"))
        block = ctx.enter_context(nc.Block())

        @block.gpsimd
        def _(pool):
            pool.memset(c.ident[:, :], 0.0)
            pool.memset(c.ident_bf[:, :], 0.0)
            pool.memset(c.ones[:, :], 1.0)
            pool.memset(c.tri[:, :], 1.0)
            pool.memset(c.tri_after[:, :], 1.0)
            pool.memset(c.tri_before[:, :], 1.0)
            pool.memset(c.causal_bf[:, :], 0.0).then_inc(made, 1)
            pool.wait_ge(made, 1)
            for m in (c.ident, c.ident_bf):
                pool.affine_select(out=m[:, :], in_=m[:, :], compare_op=ALU.not_equal, fill=1.0,
                                   base=0, pattern=[[-1, P]], channel_multiplier=1)
            pool.affine_select(out=c.tri[:, :], in_=c.tri[:, :], compare_op=ALU.is_ge, fill=0.0,
                               base=0, pattern=[[1, P]], channel_multiplier=-1)
            pool.affine_select(out=c.tri_after[:, :], in_=c.tri_after[:, :], compare_op=ALU.is_ge,
                               fill=0.0, base=-1, pattern=[[-1, P]], channel_multiplier=1)
            pool.affine_select(out=c.tri_before[:, :], in_=c.tri_before[:, :], compare_op=ALU.is_ge,
                               fill=0.0, base=-1, pattern=[[1, P]], channel_multiplier=-1)
            pool.affine_select(out=c.causal_bf[:, :], in_=c.causal_bf[:, :], compare_op=ALU.is_ge,
                               fill=MASKED, base=0, pattern=[[-1, P]],
                               channel_multiplier=1).then_inc(selected, 1)
            pool.wait_ge(selected, 1)


def normalise_input(nc, c, ps, x, gain, h_hi, h_lo):
    with ExitStack() as ctx:
        def sb(name, shape, dt=F32):
            return ctx.enter_context(nc.sbuf_tensor(name, shape, dt))

        def sem(name):
            return ctx.enter_context(nc.semaphore(name))

        x_all = sb("x_all", [P, TT, D])
        gain_row = sb("gain_row", [P, D])
        squares = sb("squares", [P, D])
        sum_sq = sb("sum_sq", [P, TT])
        mean_sq = sb("mean_sq", [P, TT])
        root = sb("root", [P, TT])
        rstd = sb("rstd", [P, TT])
        xn = sb("xn", [P, RING, D])
        x_loaded = [sem(f"x_loaded{n}") for n in range(4)]
        gain_loaded = sem("gain_loaded")
        squared = sem("squared")
        mean_done = sem("mean_done")
        root_done = sem("root_done")
        rstd_done = sem("rstd_done")
        xn_done = sem("xn_done")
        transposed = sem("transposed")
        hi_done = sem("hi_done")
        lo_done = sem("lo_done")
        x_tiles = x[0].rearrange("(t p) d -> p t d", p=P)
        block = ctx.enter_context(nc.Block())

        @block.sync
        def _(sp):
            for n in range(4):
                sp.dma_start(x_all[:, 2 * n:2 * n + 2, :], x_tiles[:, 2 * n:2 * n + 2, :]).then_inc(x_loaded[n], DMA)
            sp.dma_start(gain_row[:, :], gain.to_broadcast([P, D])).then_inc(gain_loaded, DMA)

        @block.scalar
        def _(act):
            for t in range(TT):
                if t % 2 == 0:
                    act.wait_ge(x_loaded[t // 2], DMA)
                if t > 0:
                    act.wait_ge(squared, t)
                act.activation(squares[:, :], x_all[:, t, :], ACT.Square,
                               accum_out=sum_sq[:, t:t + 1]).then_inc(squared, 1)
            act.wait_ge(mean_done, 1)
            act.activation(root[:, :], mean_sq[:, :], ACT.Sqrt).then_inc(root_done, 1)
            with act.Fori(0, TT // RING) as i:
                for s in range(RING):
                    act.wait_ge(transposed, RING + RING * i + s + 1)
                    act.activation(h_hi[:, :, ds(RING * P * i + s * P, P)],
                                   banks(ps, 2 * s, 2).rearrange("p (k t) -> p k t", k=KT),
                                   ACT.Copy).then_inc(hi_done, 1)

        @block.vector
        def _(dve):
            dve.wait_ge(squared, TT)
            dve.tensor_scalar(mean_sq[:, :], sum_sq[:, :], 1.0 / D, EPS, ALU.mult, ALU.add).then_inc(mean_done, 1)
            dve.wait_ge(root_done, 1)
            dve.reciprocal(rstd[:, :], root[:, :]).then_inc(rstd_done, 1)
            dve.wait_ge(rstd_done, 1)
            dve.wait_ge(gain_loaded, DMA)
            with dve.Fori(0, TT // RING) as i:
                for s in range(RING):
                    t = RING * i + s
                    dve.wait_ge(transposed, t + 1)
                    dve.scalar_tensor_tensor(out=xn[:, s, :], in0=x_all[:, ds(t, 1), :].rearrange("p a d -> p (a d)"),
                                             scalar=rstd[:, ds(t, 1)], in1=gain_row[:, :],
                                             op0=ALU.mult, op1=ALU.mult).then_inc(xn_done, 1)
                for s in range(RING):
                    dve.wait_ge(hi_done, RING * i + s + 1)
                    dst = ds(RING * P * i + s * P, P)
                    dve.tensor_tensor(h_lo[:, :, dst], banks(ps, 2 * s, 2).rearrange("p (k t) -> p k t", k=KT),
                                      h_hi[:, :, dst].bitcast(F32), ALU.subtract).then_inc(lo_done, 1)

        @block.tensor
        def _(pe):
            pe.sem_inc(transposed, RING)
            pe.sem_inc(lo_done, RING)
            with pe.Fori(0, TT // RING) as i:
                for s in range(RING):
                    pe.wait_ge(xn_done, RING * i + s + 1)
                    pe.wait_ge(lo_done, RING * i + s + 1)
                    for k in range(KT):
                        last = pe.transpose(banks(ps, 2 * s, 2)[:, k * P:(k + 1) * P],
                                            xn[:, s, k * P:(k + 1) * P], c.ident[:, :])
                    last.then_inc(transposed, 1)


def three_passes(pe, out, w_hi, w_lo, h_hi, h_lo, first, last):
    for a, b, opens, closes in ((w_hi, h_hi, first, False), (w_hi, h_lo, False, False), (w_lo, h_hi, False, last)):
        for n in range(len(out)):
            ins = pe.matmul(out[n], a, b[n], start=opens, stop=closes)
    return ins


def project(nc, ps, w_in, parts, h_hi, h_lo, taps, bias):
    kinds = [kind for _, _, kind, _ in parts]
    total = sum(blocks for _, blocks, _, _ in parts)
    firsts = [sum(blocks for _, blocks, _, _ in parts[:k]) for k in range(len(parts))]
    n_staged = sum(blocks for _, blocks, kind, _ in parts if kind in ("silu", "sigmoid"))
    with ExitStack() as ctx:
        def sb(name, shape, dt=F32):
            return ctx.enter_context(nc.sbuf_tensor(f"{name}_{kinds[0]}", shape, dt))

        def sem(name):
            return ctx.enter_context(nc.semaphore(f"{name}_{kinds[0]}"))

        w_raw = sb("w_raw", [P, RING, KT, P])
        w_hi = sb("w_hi", [P, RING, KT, P], F32R)
        w_lo = sb("w_lo", [P, RING, KT, P], F32R)
        w_loaded = [sem(f"w_loaded{s}") for s in range(RING)]
        w_hi_done = sem("w_hi_done")
        w_lo_done = sem("w_lo_done")
        projected = sem("projected")
        read_out = sem("read_out")
        if "conv" in kinds:
            padded = sb("padded", [P, RING, CONV - 1 + SEQ])
            mixed = sb("mixed", [P, RING, SEQ])
            pad_done = sem("pad_done")
            tap_done = sem("tap_done")
            conv_done = sem("conv_done")
            silu_done = sem("silu_done")
        if n_staged:
            stage = sb("stage", [P, RING, SEQ])
            stored = [sem(f"stored{s}") for s in range(RING)]
        w_cols = w_in.rearrange("(k p) c -> p k c", p=P)
        block = ctx.enter_context(nc.Block())

        def flat(t, n):
            return t[:, ds(n, 1), :].rearrange("p a t -> p (a t)")

        @block.sync
        def _(sp):
            for (col, blocks, _, _), first in zip(parts, firsts):
                with sp.Fori(0, blocks // RING) as i:
                    for s in range(RING):
                        sp.wait_ge(w_lo_done, first + RING * i + s + 1)
                        sp.dma_start(w_raw[:, s, :, :], w_cols[:, :, ds(col + RING * P * i + s * P, P)]).then_inc(w_loaded[s], DMA)

        @block.gpsimd
        def _(pool):
            pool.sem_inc(w_lo_done, RING)
            if "conv" in kinds:
                pool.memset(padded[:, :, 0:CONV - 1], 0.0).then_inc(pad_done, 1)
            with pool.Fori(0, total // RING) as i:
                for s in range(RING):
                    pool.wait_ge(w_hi_done, RING * i + s + 1)
                    pool.tensor_tensor(w_lo[:, s, :, :], w_raw[:, s, :, :], w_hi[:, s, :, :].bitcast(F32),
                                       ALU.subtract).then_inc(w_lo_done, 1)

        @block.tensor
        def _(pe):
            pe.sem_inc(projected, RING)
            with pe.Fori(0, total // RING) as i:
                for s in range(RING):
                    n = RING * i + s
                    pe.wait_ge(w_lo_done, RING + n + 1)
                    pe.wait_ge(read_out, n + 1)
                    for k in range(KT):
                        last = three_passes(pe, [ps[:, 2 * s, :], ps[:, 2 * s + 1, :]], w_hi[:, s, k, :], w_lo[:, s, k, :],
                                            [h_hi[:, k, 0:HALF], h_hi[:, k, HALF:SEQ]],
                                            [h_lo[:, k, 0:HALF], h_lo[:, k, HALF:SEQ]], k == 0, k == KT - 1)
                    last.then_inc(projected, 1)

        @block.scalar
        def _(act):
            def high(n, s, round_):
                act.wait_ge(w_loaded[s], DMA * round_ + DMA)
                act.wait_ge(projected, n + 1)
                act.activation(w_hi[:, s, :, :], w_raw[:, s, :, :], ACT.Copy).then_inc(w_hi_done, 1)

            def evacuate(n, s, own, kind, dest):
                act.wait_ge(projected, RING + n + 1)
                if kind == "conv":
                    act.wait_ge(conv_done, own + 1)
                    act.activation(padded[:, s, CONV - 1:], banks(ps, 2 * s, 2), ACT.Copy).then_inc(read_out, 1)
                else:
                    round_ = (n - s) * (DMA // RING)
                    act.wait_ge(stored[s], round_ + DMA)
                    act.activation(stage[:, s, :], banks(ps, 2 * s, 2),
                                   ACT.Silu if kind == "silu" else ACT.Sigmoid).then_inc(read_out, 1)
                    act.wait_ge(read_out, RING + n + 1)
                    act.dma_start(dest[ds(own, 1)].rearrange("a p t -> p (a t)"), stage[:, s, :]).then_inc(stored[s], DMA)

            def silu(own, s, dest):
                act.wait_ge(conv_done, RING + own + 1)
                act.activation(flat(dest, own), mixed[:, s, :], ACT.Silu).then_inc(silu_done, 1)

            if n_staged:
                for s in range(RING):
                    act.sem_inc(stored[s], DMA)
            if kinds[0] != "keep":
                act.sem_inc(read_out, RING)
            if "conv" in kinds:
                act.sem_inc(silu_done, RING)
                act.wait_ge(pad_done, 1)
            high(0, 0, 0)
            for (_, blocks, kind, dest), first in zip(parts, firsts):
                def pair(i, first_pair, last_pair):
                    for s in range(RING):
                        own = RING * i + s
                        n = first + own
                        if s == 0:
                            high(n + 1, 1, first // RING + i)
                        elif not last_pair:
                            high(n + 1, 0, first // RING + i + 1)
                        if kind != "keep":
                            evacuate(n, s, own, kind, dest)
                        if kind == "conv" and not (first_pair and s == 0):
                            silu(own - 1, 1 - s, dest)

                pair(0, True, False)
                with act.Fori(0, blocks // RING - 2) as i:
                    pair(i + 1, False, False)
                pair(blocks // RING - 1, False, first + blocks == total)
                if kind == "conv":
                    silu(blocks - 1, 1, dest)
            if n_staged:
                for s in range(RING):
                    act.wait_ge(stored[s], DMA * (n_staged // RING) + DMA)

        @block.vector
        def _(dve):
            if kinds[0] == "keep":
                dve.sem_inc(read_out, RING)
            if "conv" in kinds:
                dve.sem_inc(conv_done, RING)
            for (_, blocks, kind, dest), first in zip(parts, firsts):
                if kind == "keep":
                    with dve.Fori(0, blocks // RING) as i:
                        for s in range(RING):
                            own = RING * i + s
                            dve.wait_ge(projected, RING + first + own + 1)
                            dve.tensor_copy(flat(dest, own), banks(ps, 2 * s, 2)).then_inc(read_out, 1)
                if kind == "conv":
                    with dve.Fori(0, blocks // RING) as i:
                        for s in range(RING):
                            own = RING * i + s
                            dve.wait_ge(read_out, RING + first + own + 1)
                            dve.wait_ge(silu_done, own + 1)
                            dve.tensor_scalar(mixed[:, s, :], padded[:, s, 0:SEQ], taps[:, 0, ds(own, 1)], bias[:, ds(own, 1)],
                                              ALU.mult, ALU.add).then_inc(tap_done, 1)
                            for j in range(1, CONV):
                                dve.wait_ge(tap_done, (CONV - 1) * own + j)
                                dve.scalar_tensor_tensor(out=mixed[:, s, :], in0=padded[:, s, j:j + SEQ],
                                                         scalar=taps[:, j, ds(own, 1)], in1=mixed[:, s, :], op0=ALU.mult,
                                                         op1=ALU.add).then_inc(tap_done if j < CONV - 1 else conv_done, 1)


def decays(nc, c, ps, w_in, b_f, dt_bias, a_log, h_hi, h_lo, f_rows, dt_tok, a_tok):
    with ExitStack() as ctx:
        def sb(name, shape, dt=F32):
            return ctx.enter_context(nc.sbuf_tensor(name, shape, dt))

        def sem(name):
            return ctx.enter_context(nc.semaphore(name))

        w_raw = sb("small_raw", [P, KT, P])
        w_hi = sb("small_hi", [P, KT, P], F32R)
        w_lo = sb("small_lo", [P, KT, P], F32R)
        sign = sb("small_sign", [SMALL, 1])
        bias = sb("small_bias", [SMALL, 1])
        bias_signed = sb("small_bias_signed", [SMALL, 1])
        a_rate = sb("a_rate", [P, SSD_HEADS])
        a_exp = sb("a_exp", [P, SSD_HEADS])
        arg = sb("softplus_arg", [SMALL, SEQ])
        arg_abs = sb("softplus_abs", [SMALL, SEQ])
        expd = sb("softplus_exp", [SMALL, SEQ])
        logd = sb("softplus_log", [SMALL, SEQ])
        soft = sb("softplus", [SMALL, SEQ])
        one_row = sb("one_row", [HEADS, SEQ])
        neg_f = sb("neg_f", [HEADS, SEQ])
        cleared = sem("small_cleared")
        loaded = sem("small_loaded")
        a_loaded = sem("a_loaded")
        hi_done = sem("small_hi_done")
        lo_done = sem("small_lo_done")
        projected = sem("small_projected")
        vec = sem("decays_vec")
        abs_done = sem("softplus_abs_done")
        expd_done = sem("softplus_exp_done")
        logd_done = sem("softplus_log_done")
        a_exp_done = sem("a_exp_done")
        transposed = sem("dt_transposed")
        stored = sem("f_rows_stored")
        w_cols = w_in.rearrange("(k p) c -> p k c", p=P)
        dt_rows = slice(DT_ROW, DT_ROW + SSD_HEADS)
        block = ctx.enter_context(nc.Block())

        @block.gpsimd
        def _(pool):
            pool.memset(w_raw[:, :, :], 0.0)
            pool.memset(sign[:, :], 1.0)
            pool.memset(bias[:, :], 0.0)
            pool.memset(one_row[:, :], 1.0).then_inc(cleared, 1)
            pool.wait_ge(cleared, 1)
            pool.memset(sign[0:HEADS, :], -1.0).then_inc(cleared, 1)
            pool.wait_ge(hi_done, 1)
            pool.tensor_tensor(w_lo[:, :, :], w_raw[:, :, :], w_hi[:, :, :].bitcast(F32), ALU.subtract).then_inc(lo_done, 1)

        @block.sync
        def _(sp):
            sp.dma_start(a_rate[:, :], a_log.to_broadcast([P, SSD_HEADS])).then_inc(a_loaded, DMA)
            sp.wait_ge(cleared, 2)
            with nc.allow_non_contiguous_dma(reason="a few narrow columns"):
                sp.dma_start(w_raw[:, :, 0:HEADS], w_cols[:, :, COL_F:COL_F + HEADS]).then_inc(loaded, DMA)
                sp.dma_start(w_raw[:, :, dt_rows], w_cols[:, :, COL_DT:COL_DT + SSD_HEADS]).then_inc(loaded, DMA)
                sp.dma_start(bias[0:HEADS, :], b_f.rearrange("a h -> h a")).then_inc(loaded, DMA)
                sp.dma_start(bias[dt_rows, :], dt_bias.rearrange("a h -> h a")).then_inc(loaded, DMA)
            sp.wait_ge(vec, 4)
            sp.dma_start(f_rows, neg_f[:, :]).then_inc(stored, DMA)
            sp.wait_ge(stored, DMA)

        @block.scalar
        def _(act):
            act.wait_ge(loaded, 4 * DMA)
            act.activation(w_hi[:, :, :], w_raw[:, :, :], ACT.Copy).then_inc(hi_done, 1)
            act.wait_ge(a_loaded, DMA)
            act.activation(a_exp[:, :], a_rate[:, :], ACT.Exp).then_inc(a_exp_done, 1)
            act.wait_ge(vec, 2)
            act.activation(arg_abs[:, :], arg[:, :], ACT.Abs).then_inc(abs_done, 1)
            act.wait_ge(abs_done, 1)
            act.activation(expd[:, :], arg_abs[:, :], ACT.Exp, scale=-1.0).then_inc(expd_done, 1)
            act.wait_ge(expd_done, 1)
            act.activation(logd[:, :], expd[:, :], ACT.Ln, bias=1.0).then_inc(logd_done, 1)

        @block.tensor
        def _(pe):
            pe.wait_ge(lo_done, 1)
            for k in range(KT):
                last = three_passes(pe, [ps[:, 0, :], ps[:, 1, :]], w_hi[:, k, :], w_lo[:, k, :],
                                    [h_hi[:, k, 0:HALF], h_hi[:, k, HALF:SEQ]],
                                    [h_lo[:, k, 0:HALF], h_lo[:, k, HALF:SEQ]], k == 0, k == KT - 1)
            last.then_inc(projected, 1)
            pe.wait_ge(vec, 3)
            for t in range(TT):
                last = pe.transpose(ps[:, 2, t * SMALL:(t + 1) * SMALL], soft[:, t * P:(t + 1) * P],
                                    c.ident[0:SMALL, 0:SMALL])
            last.then_inc(transposed, 1)

        @block.vector
        def _(dve):
            dve.wait_ge(loaded, 4 * DMA)
            dve.tensor_tensor(bias_signed[:, :], bias[:, :], sign[:, :], ALU.mult).then_inc(vec, 1)
            dve.wait_ge(vec, 1)
            dve.wait_ge(projected, 1)
            dve.tensor_scalar(arg[:, :], banks(ps, 0, 2)[0:SMALL, :], sign[:, :], bias_signed[:, :],
                              ALU.mult, ALU.add).then_inc(vec, 1)
            dve.wait_ge(vec, 2)
            dve.wait_ge(logd_done, 1)
            dve.scalar_tensor_tensor(out=soft[:, :], in0=arg[:, :], scalar=0.0, in1=logd[:, :],
                                     op0=ALU.max, op1=ALU.add).then_inc(vec, 1)
            dve.wait_ge(vec, 3)
            dve.wait_ge(cleared, 2)
            dve.tensor_tensor_scan(neg_f[:, :], one_row[:, :], soft[0:HEADS, :], 0.0,
                                   ALU.mult, ALU.add).then_inc(vec, 1)
            dve.wait_ge(transposed, 1)
            dve.tensor_copy(dt_tok[:, :, :], ps[:, 2, :].rearrange("p (t r) -> p t r", t=TT)[:, :, dt_rows]).then_inc(vec, 1)
            dve.wait_ge(vec, 5)
            dve.wait_ge(a_exp_done, 1)
            for t in range(TT):
                dve.scalar_tensor_tensor(out=a_tok[:, t, :], in0=dt_tok[:, t, :], scalar=-1.0, in1=a_exp[:, :],
                                         op0=ALU.mult, op1=ALU.mult)


def attention(nc, c, ps, qkv, f_rows, y_hi, y_lo):
    PAIRS = HEADS // 2
    TILES = 2 * TT
    DT = HD + 1
    with ExitStack() as ctx:
        def sb(name, shape, dt=F32):
            return ctx.enter_context(nc.sbuf_tensor(name, shape, dt))

        def sem(name):
            return ctx.enter_context(nc.semaphore(name))

        q_cur = sb("q_cur", [DT, 2, SEQ])
        k_cur = sb("k_cur", [DT, 2, SEQ])
        v_cur = sb("v_cur", [P, SEQ])
        v_tok = sb("v_tok", [P, TT, P])
        probs = sb("probs", [P, RING, SEQ])
        probs_t = sb("probs_t", [P, RING, SEQ])
        neg_max = sb("neg_max", [P, TILES])
        row_sum = sb("row_sum", [P, TILES])
        inv_sum = sb("inv_sum", [P, TILES])
        y_pair = sb("y_pair", [P, TT, P])
        ones_set = sem("ones_set")
        f_loaded = [sem(f"f_loaded{s}") for s in range(2)]
        q_copied = sem("q_copied")
        k_copied = sem("k_copied")
        v_copied = sem("v_copied")
        v_turned = sem("v_turned")
        v_ready = sem("v_ready")
        scored = sem("scored")
        maxed = sem("maxed")
        expd = sem("expd")
        turned = sem("turned")
        evac_low = sem("evac_low")
        evac_high = sem("evac_high")
        weighed = sem("weighed")
        inverted = sem("inverted")
        normed = sem("normed")
        pair_turned = sem("pair_turned")
        hi_done = sem("attn_hi_done")
        lo_done = sem("attn_lo_done")
        order = [(0, t) for t in range(TT)] + [(1, TT - 1 - t) for t in range(TT)]
        block = ctx.enter_context(nc.Block())

        @block.sync
        def _(sp):
            with sp.Fori(0, PAIRS) as i:
                sp.wait_ge(pair_turned, i + 1)
                for s in range(2):
                    sp.dma_start(k_cur[HD:DT, s, :], f_rows[ds(2 * i + s, 1), :]).then_inc(f_loaded[s], DMA)

        @block.gpsimd
        def _(pool):
            pool.memset(q_cur[HD:DT, :, :], 1.0).then_inc(ones_set, 1)
            pool.wait_ge(ones_set, 1)
            with pool.Fori(0, PAIRS) as i:
                pool.wait_ge(pair_turned, i + 1)
                pool.tensor_copy(v_cur[:, :], qkv[:, ds(2 * PAIRS + i, 1), :].rearrange("p a t -> p (a t)")).then_inc(v_copied, 1)

        @block.vector
        def _(dve):
            dve.sem_inc(normed, RING)
            dve.sem_inc(evac_low, 1)
            dve.sem_inc(lo_done, 1)

            def row_max(i, n):
                s, t = order[n]
                dve.wait_ge(scored, TILES * i + n + 1)
                dve.tensor_reduce(neg_max[:, n:n + 1], banks(ps, 2 * (n % RING), 2)[:, 0:(t + 1) * P], AX.X, ALU.max,
                                  negate=True).then_inc(maxed, 1)

            def evacuate(i, n):
                s, t = order[n]
                width = min(t + 1, 4) * P
                dve.wait_ge(turned, RING + TILES * i + n + 1)
                dve.wait_ge(weighed, TILES * i + n + 1)
                dve.tensor_copy(probs_t[:, n % RING, 0:width], ps[:, 4, 0:width]).then_inc(evac_low, 1)
                dve.wait_ge(expd, RING + TILES * i + n + 1)
                dve.reciprocal(inv_sum[:, n:n + 1], row_sum[:, n:n + 1]).then_inc(inverted, 1)

            def normalise(i, n):
                s, t = order[n]
                dve.wait_ge(weighed, RING + TILES * i + n + 1)
                dve.wait_ge(inverted, TILES * i + n + 1)
                dve.tensor_scalar(y_pair[:, t, s * HD:(s + 1) * HD], ps[:, 6 + n % RING, 0:HD], inv_sum[:, n:n + 1],
                                  None, ALU.mult).then_inc(normed, 1)

            with dve.Fori(0, PAIRS) as i:
                dve.wait_ge(pair_turned, i + 1)
                for s in range(2):
                    dve.tensor_scalar(q_cur[0:HD, s, :], qkv[s * HD:(s + 1) * HD, ds(i, 1), :].rearrange("p a t -> p (a t)"),
                                      HD ** -0.5, None, ALU.mult).then_inc(q_copied, 1)
                dve.wait_ge(v_turned, i + 1)
                dve.tensor_copy(v_tok[:, :, :].rearrange("p t d -> p (t d)"), banks(ps, 4, 2)).then_inc(v_ready, 1)
                row_max(i, 0)
                for n in range(TILES):
                    if n + 1 < TILES:
                        row_max(i, n + 1)
                    evacuate(i, n)
                    if n > 0:
                        normalise(i, n - 1)
                normalise(i, TILES - 1)
                dve.wait_ge(hi_done, i + 1)
                dve.tensor_tensor(y_lo[:, ds(i, 1), :].rearrange("p a t -> p (a t)"), banks(ps, 4, 2),
                                  y_hi[:, ds(i, 1), :].rearrange("p a t -> p (a t)").bitcast(F32),
                                  ALU.subtract).then_inc(lo_done, 1)

        @block.scalar
        def _(act):
            act.sem_inc(expd, RING)
            act.sem_inc(evac_high, 1)

            def exponent(i, n):
                s, t = order[n]
                act.wait_ge(maxed, TILES * i + n + 1)
                act.wait_ge(turned, TILES * i + n + 1)
                width = (t + 1) * P
                act.activation(probs[:, n % RING, 0:width], banks(ps, 2 * (n % RING), 2)[:, 0:width], ACT.Exp,
                               bias=neg_max[:, n:n + 1], accum_out=row_sum[:, n:n + 1]).then_inc(expd, 1)

            def evacuate(i, n):
                s, t = order[n]
                act.wait_ge(turned, RING + TILES * i + n + 1)
                act.wait_ge(weighed, TILES * i + n + 1)
                act.activation(probs_t[:, n % RING, HALF:(t + 1) * P], ps[:, 5, 0:(t + 1) * P - HALF], ACT.Copy).then_inc(evac_high, 1)

            with act.Fori(0, PAIRS) as i:
                act.wait_ge(pair_turned, i + 1)
                for s in range(2):
                    act.activation(k_cur[0:HD, s, :], qkv[s * HD:(s + 1) * HD, ds(PAIRS + i, 1), :].rearrange("p a t -> p (a t)"),
                                   ACT.Copy).then_inc(k_copied, 1)
                exponent(i, 0)
                for n in range(TILES):
                    if n + 1 < TILES:
                        exponent(i, n + 1)
                    if order[n][1] >= 4:
                        evacuate(i, n)
                act.wait_ge(pair_turned, 1 + i + 1)
                act.activation(y_hi[:, ds(i, 1), :].rearrange("p a t -> p (a t)"), banks(ps, 4, 2), ACT.Copy).then_inc(hi_done, 1)

        @block.tensor
        def _(pe):
            pe.sem_inc(turned, RING)
            pe.sem_inc(weighed, RING)
            pe.sem_inc(pair_turned, 1)
            pe.wait_ge(ones_set, 1)

            def score(i, n):
                s, t = order[n]
                if n == 0 or n == TT:
                    pe.wait_ge(q_copied, 2 * i + s + 1)
                    pe.wait_ge(k_copied, 2 * i + s + 1)
                    pe.wait_ge(f_loaded[s], DMA * i + DMA)
                pe.wait_ge(expd, TILES * i + n + 1)
                for b in range(t // 4 + 1):
                    keys = min((t + 1) * P - b * HALF, HALF)
                    out = ps[:, 2 * (n % RING) + b, 0:keys]
                    last = pe.matmul(out, q_cur[:, s, t * P:(t + 1) * P], k_cur[:, s, b * HALF:b * HALF + keys],
                                     start=True, stop=True)
                    if b == t // 4:
                        last = pe.matmul(out[:, keys - P:keys], c.ident_bf[:, :], c.causal_bf[:, :], start=False, stop=True,
                                         skip_group_check=True)
                last.then_inc(scored, 1)

            def turn(i, n, high):
                s, t = order[n]
                pe.wait_ge(expd, RING + TILES * i + n + 1)
                pe.wait_ge(evac_low, 1 + TILES * i + n)
                pe.wait_ge(evac_high, 1 + 8 * i + high)
                for j in range(t + 1):
                    last = pe.transpose(ps[:, 4 + j // 4, (j % 4) * P:(j % 4 + 1) * P], probs[:, n % RING, j * P:(j + 1) * P],
                                        c.ident[:, :])
                last.then_inc(turned, 1)

            def weigh(i, n, high):
                s, t = order[n]
                pe.wait_ge(evac_low, 1 + TILES * i + n + 1)
                pe.wait_ge(evac_high, 1 + 8 * i + high)
                pe.wait_ge(normed, TILES * i + n + 1)
                for j in range(t + 1):
                    last = pe.matmul(ps[:, 6 + n % RING, 0:HD], probs_t[:, n % RING, j * P:(j + 1) * P],
                                     v_tok[:, j, s * HD:(s + 1) * HD], start=j == 0, stop=j == t)
                last.then_inc(weighed, 1)

            highs = [sum(t >= 4 for _, t in order[:n]) for n in range(TILES + 1)]
            with pe.Fori(0, PAIRS) as i:
                pe.wait_ge(v_copied, i + 1)
                pe.wait_ge(lo_done, i + 1)
                for t in range(TT):
                    last = pe.transpose(ps[:, 4 + t // 4, (t % 4) * P:(t % 4 + 1) * P], v_cur[:, t * P:(t + 1) * P], c.ident[:, :])
                last.then_inc(v_turned, 1)
                score(i, 0)
                pe.wait_ge(v_ready, i + 1)
                for n in range(TILES):
                    if n + 1 < TILES:
                        score(i, n + 1)
                    turn(i, n, highs[n])
                    if n > 0:
                        weigh(i, n - 1, highs[n])
                weigh(i, TILES - 1, highs[TILES])
                pe.wait_ge(normed, RING + TILES * i + TILES)
                for t in range(TT):
                    last = pe.transpose(ps[:, 4 + t // 4, (t % 4) * P:(t % 4 + 1) * P], y_pair[:, t, :], c.ident[:, :])
                last.then_inc(pair_turned, 1)


def spread(ap, shape, axis):
    return ap.unsqueeze(axis).to_broadcast(shape)


def state_space(nc, c, ps, xbc, dt_tok, a_tok, d_skip, silu_z, gated, square_sum, load_next):
    CHUNKS = SEQ // P
    H, HP = SSD_HEADS, SSD_HD
    QUARTER = H // 4
    with ExitStack() as ctx:
        def sb(name, shape, dt=F32):
            return ctx.enter_context(nc.sbuf_tensor(name, shape, dt))

        def sem(name):
            return ctx.enter_context(nc.semaphore(name))

        d_col = sb("d_col", [P, XB])
        a_cs = sb("a_cs", [P, CHUNKS, H])
        a_total = sb("a_total", [P, CHUNKS, H])
        a_left = sb("a_left", [P, CHUNKS, H])
        grow_in = sb("grow_in", [P, CHUNKS, H])
        chunk_decay = sb("chunk_decay", [P, CHUNKS, H])
        to_end = sb("to_end", [P, CHUNKS, H])
        dt_to_end = sb("dt_to_end", [P, CHUNKS, H])
        chan = sb("chan", [P, RING, CB, P])
        a_spread = sb("a_spread", [P, RING, H, P])
        cb_masked = sb("cb_masked", [P, RING, GROUPS, P])
        b_tok = sb("b_tok", [P, RING, GROUPS, P])
        decay = sb("decay", [P, RING, H, P])
        x_dt = sb("x_dt", [P, RING, H, HP])
        x_end = sb("x_end", [P, RING, H, HP])
        y_tok = sb("y_tok", [P, H, HP])
        state = sb("state", [P, H, HP])
        skip = sb("skip", [P, XB, P])
        y_sum = sb("y_sum", [P, XB, P])
        z_chunk = sb("z_chunk", [P, RING, XB, P])
        gated_sq = sb("gated_sq", [P, XB, P])

        d_loaded = sem("d_loaded")
        z_loaded = [sem(f"z_loaded{s}") for s in range(RING)]
        sums_ready = sem("sums_ready")
        pre = sem("ssd_prelude_vec")
        pre_exp = sem("ssd_prelude_exp")
        state_zero = sem("state_zero")
        copied = sem("chunk_copied")
        a_ready = sem("a_spread_ready")
        small_ready = sem("cb_and_b_ready")
        cb_done = sem("cb_masked_done")
        b_done = sem("b_tok_done")
        x_turned = sem("x_turned")
        x_scaled = sem("x_scaled")
        seg_done = sem("seg_done")
        decay_done = sem("decay_done")
        m_done = sem("m_done")
        y_parts = sem("y_parts")
        off_scaled = sem("off_scaled")
        y_added = sem("y_added")
        gain_ready = sem("state_gain_ready")
        state_scaled = sem("state_scaled")
        state_done = sem("state_done")
        y_turned = sem("y_turned")
        skip_done = sem("skip_done")
        y_done = sem("y_done")
        gated_done = sem("gated_done")
        held = sem("gated_held")
        act_held = sem("squared_held")
        gated_squared = sem("gated_squared")
        square_summed = sem("square_summed")
        z_cols = silu_z.rearrange("b p t -> p b t")
        block = ctx.enter_context(nc.Block())
        y_in = banks(ps, 4, 2)
        y_off = banks(ps, 6, 2)

        def steps(eng, step):
            with eng.Fori(0, CHUNKS // 2 - 1) as i:
                step(2 * i, 0, True)
                step(2 * i + 1, 1, True)
            step(CHUNKS - 2, 0, True)
            step(CHUNKS - 1, 1, False)

        @block.sync
        def _(sp):
            heads = d_skip.rearrange("a (b two) -> two a b", two=2)
            with nc.allow_non_contiguous_dma(reason="16 numbers"):
                for half in range(2):
                    sp.dma_start(d_col[half * HP:(half + 1) * HP, :], heads[half].to_broadcast([HP, XB])).then_inc(d_loaded, DMA)

            def step(n, s, more):
                sp.wait_ge(gated_done, n + 1)
                sp.dma_start(z_chunk[:, s, :, :], z_cols[:, :, ds(n * P, P)]).then_inc(z_loaded[s], DMA)

            steps(sp, step)
            load_next(sp)

        @block.gpsimd
        def _(pool):
            pool.sem_inc(gated_done, RING)
            pool.sem_inc(skip_done, 1)
            pool.memset(state[:, :, :], 0.0).then_inc(state_zero, 1)

            def front(n, s):
                pool.wait_ge(seg_done, 4 * n + 4)
                pool.tensor_tensor(a_spread[:, s, :, :],
                                   spread(a_tok[:, ds(n, 1), :].rearrange("p a h -> p (a h)"), [P, H, P], 2),
                                   spread(c.tri[:, :], [P, H, P], 1), ALU.mult).then_inc(a_ready, 1)

            def step(n, s, more):
                if more:
                    front(n + 1, 1 - s)
                pool.wait_ge(y_done, 1 + n)
                pool.wait_ge(copied, n + 1)
                pool.tensor_tensor(skip[:, :, :], chan[:, s, 0:XB, :], spread(d_col[:, :], [P, XB, P], 2),
                                   ALU.mult).then_inc(skip_done, 1)
                pool.wait_ge(y_done, 1 + n + 1)
                pool.wait_ge(z_loaded[s], DMA * (n // 2 if isinstance(n, int) else (n - s) // 2) + DMA)
                pool.sem_inc(held, 1)
                pool.tensor_tensor(gated[:, :, ds(n * P, P)], y_sum[:, :, :], z_chunk[:, s, :, :],
                                   ALU.mult).then_inc(gated_done, 1)

            pool.wait_ge(d_loaded, 2 * DMA)
            front(0, 0)
            steps(pool, step)

        @block.scalar
        def _(act):
            act.sem_inc(decay_done, 4)
            act.wait_ge(pre, 2)
            act.activation(grow_in[:, :, :], a_cs[:, :, :], ACT.Exp).then_inc(pre_exp, 1)
            act.activation(chunk_decay[:, :, :], a_total[:, :, :], ACT.Exp).then_inc(pre_exp, 1)
            act.wait_ge(pre, 3)
            act.activation(to_end[:, :, :], a_left[:, :, :], ACT.Exp).then_inc(pre_exp, 1)

            def copy_chunk(n, s):
                act.wait_ge(y_parts, n + 1)
                act.wait_ge(skip_done, n)
                act.activation(chan[:, s, :, :], xbc[:, :, ds(n * P, P)], ACT.Copy).then_inc(copied, 1)

            def front(n, s):
                act.wait_ge(small_ready, n + 1)
                act.wait_ge(cb_done, n + 1)
                act.activation(b_tok[:, s, :, :].rearrange("p g d -> p (g d)"), ps[:, 0, GROUPS * P:], ACT.Copy).then_inc(b_done, 1)
                for q in range(4):
                    act.wait_ge(seg_done, 4 * RING + 4 * n + q + 1)
                    if q == 0:
                        act.wait_ge(y_parts, n + 1)
                    act.activation(decay[:, s, q * QUARTER:(q + 1) * QUARTER, :].rearrange("p h l -> p (h l)"),
                                   ps[:, (q + 1) % 2, :], ACT.Exp).then_inc(decay_done, 1)

            def step(n, s, more):
                if more:
                    copy_chunk(n + 1, 1 - s)
                    front(n + 1, 1 - s)
                act.wait_ge(gated_done, RING + n + 1)
                act.wait_ge(square_summed, 1 + n)
                act.sem_inc(act_held, 1)
                act.activation(gated_sq[:, :, :], gated[:, :, ds(n * P, P)], ACT.Square).then_inc(gated_squared, 1)

            copy_chunk(0, 0)
            front(0, 0)
            steps(act, step)

        @block.vector
        def _(dve):
            for s in (y_done, x_scaled, state_done, square_summed):
                dve.sem_inc(s, 1)
            dve.wait_ge(sums_ready, 1)
            dve.tensor_copy(a_cs[:, :, :].rearrange("p t h -> p (t h)"), ps[:, 0, 0:P]).then_inc(pre, 1)
            dve.tensor_copy(a_total[:, :, :].rearrange("p t h -> p (t h)"), ps[:, 0, P:2 * P]).then_inc(pre, 1)
            dve.wait_ge(pre, 2)
            dve.tensor_tensor(a_left[:, :, :], a_total[:, :, :], a_cs[:, :, :], ALU.subtract).then_inc(pre, 1)
            dve.wait_ge(pre_exp, 3)
            dve.tensor_tensor(dt_to_end[:, :, :], dt_tok[:, :, :], to_end[:, :, :], ALU.mult).then_inc(pre, 1)
            dve.wait_ge(pre, 4)
            dve.wait_ge(state_zero, 1)

            def per_head(t, n):
                return spread(t[:, ds(n, 1), :].rearrange("p a h -> p (a h)"), [P, H, HP], 2)

            def x_psum():
                return banks(ps, 2, 2).rearrange("p (h d) -> p h d", h=H)

            def front_x(n, s):
                dve.wait_ge(small_ready, n + 1)
                dve.tensor_tensor(cb_masked[:, s, :, :], ps[:, 0, 0:GROUPS * P].rearrange("p (g l) -> p g l", g=GROUPS),
                                  spread(c.tri[:, :], [P, GROUPS, P], 1), ALU.mult).then_inc(cb_done, 1)
                dve.wait_ge(x_turned, n + 1)
                dve.tensor_tensor(x_dt[:, s, :, :], x_psum(), per_head(dt_tok, n), ALU.mult)
                dve.tensor_tensor(x_end[:, s, :, :], x_psum(), per_head(dt_to_end, n), ALU.mult).then_inc(x_scaled, 1)

            def front_m(n, s):
                dve.wait_ge(cb_done, n + 1)
                for q in range(4):
                    dve.wait_ge(decay_done, 4 + 4 * n + q + 1)
                    heads = slice(q * QUARTER, (q + 1) * QUARTER)
                    dve.tensor_tensor(decay[:, s, heads, :], decay[:, s, heads, :],
                                      spread(cb_masked[:, s, q * GROUPS // 4, :], [P, QUARTER, P], 1), ALU.mult).then_inc(m_done, 1)

            def step(n, s, more):
                dve.wait_ge(y_parts, RING + n + 1)
                dve.tensor_tensor(y_tok[:, :, :], y_off.rearrange("p (h d) -> p h d", h=H), per_head(grow_in, n),
                                  ALU.mult).then_inc(off_scaled, 1)
                dve.wait_ge(off_scaled, n + 1)
                dve.tensor_tensor(y_tok[:, :, :].rearrange("p h d -> p (h d)"), y_in,
                                  y_tok[:, :, :].rearrange("p h d -> p (h d)"), ALU.add).then_inc(y_added, 1)
                if more:
                    front_x(n + 1, 1 - s)
                dve.tensor_tensor(state[:, :, :], state[:, :, :], per_head(chunk_decay, n), ALU.mult).then_inc(state_scaled, 1)
                dve.wait_ge(state_scaled, n + 1)
                dve.wait_ge(gain_ready, n + 1)
                dve.tensor_tensor(state[:, :, :].rearrange("p h d -> p (h d)"), y_off,
                                  state[:, :, :].rearrange("p h d -> p (h d)"), ALU.add).then_inc(state_done, 1)
                if more:
                    front_m(n + 1, 1 - s)
                dve.wait_ge(y_turned, n + 1)
                dve.wait_ge(skip_done, 1 + n + 1)
                dve.wait_ge(gated_done, RING + n)
                dve.tensor_tensor(y_sum[:, :, :].rearrange("p b l -> p (b l)"), y_in,
                                  skip[:, :, :].rearrange("p b l -> p (b l)"), ALU.add).then_inc(y_done, 1)
                dve.wait_ge(gated_squared, n + 1)
                dve.tensor_reduce(square_sum[:, ds(n * P, P)], gated_sq[:, :, :].rearrange("p b l -> p l b"), AX.X,
                                  ALU.add).then_inc(square_summed, 1)

            front_x(0, 0)
            front_m(0, 0)
            steps(dve, step)

        @block.tensor
        def _(pe):
            pe.sem_inc(y_parts, RING)
            pe.sem_inc(seg_done, 4 * RING)
            flat = a_tok[:, :, :].rearrange("p t h -> p (t h)")
            pe.matmul(ps[:, 0, 0:P], c.tri[:, :], flat, start=True, stop=True)
            pe.matmul(ps[:, 0, P:2 * P], c.ones[:, :], flat, start=True, stop=True).then_inc(sums_ready, 1)

            def front_small(n, s):
                pe.wait_ge(copied, n + 1)
                pe.wait_ge(decay_done, 4 + 4 * n)
                for g in range(GROUPS):
                    pe.matmul(ps[:, 0, g * P:(g + 1) * P], chan[:, s, XB + g, :], chan[:, s, XB + GROUPS + g, :],
                              start=True, stop=True)
                for g in range(GROUPS):
                    last = pe.transpose(ps[:, 0, (GROUPS + g) * P:(GROUPS + g + 1) * P], chan[:, s, XB + g, :], c.ident[:, :])
                last.then_inc(small_ready, 1)
                pe.wait_ge(x_scaled, 1 + n)
                for b in range(XB):
                    last = pe.transpose(ps[:, 2 + b // 4, (b % 4) * P:(b % 4 + 1) * P], chan[:, s, b, :], c.ident[:, :])
                last.then_inc(x_turned, 1)

            def front_seg(n, s):
                pe.wait_ge(a_ready, n + 1)
                for q in range(4):
                    if q == 1:
                        pe.wait_ge(cb_done, n + 1)
                        pe.wait_ge(b_done, n + 1)
                    if q >= 2:
                        pe.wait_ge(decay_done, 4 + 4 * n + q - 1)
                    pe.matmul(ps[:, (q + 1) % 2, :], c.tri_after[:, :],
                              a_spread[:, s, q * QUARTER:(q + 1) * QUARTER, :].rearrange("p h l -> p (h l)"),
                              start=True, stop=True).then_inc(seg_done, 1)

            def step(n, s, more):
                pe.wait_ge(m_done, 4 * n + 4)
                pe.wait_ge(y_done, 1 + n)
                for h in range(H):
                    pe.matmul(y_in[:, h * HP:(h + 1) * HP], decay[:, s, h, :], x_dt[:, s, h, :], start=True, stop=True)
                pe.wait_ge(state_done, 1 + n)
                for g in range(GROUPS):
                    heads = slice(g * H // GROUPS, (g + 1) * H // GROUPS)
                    last = pe.matmul(ps[:, 6 + g, :], chan[:, s, XB + GROUPS + g, :],
                                     state[:, heads, :].rearrange("p h d -> p (h d)"), start=True, stop=True)
                last.then_inc(y_parts, 1)
                if more:
                    front_small(n + 1, 1 - s)
                pe.wait_ge(off_scaled, n + 1)
                for g in range(GROUPS):
                    heads = slice(g * H // GROUPS, (g + 1) * H // GROUPS)
                    last = pe.matmul(ps[:, 6 + g, :], b_tok[:, s, g, :],
                                     x_end[:, s, heads, :].rearrange("p h d -> p (h d)"), start=True, stop=True)
                last.then_inc(gain_ready, 1)
                if more:
                    front_seg(n + 1, 1 - s)
                pe.wait_ge(y_added, n + 1)
                for b in range(XB):
                    last = pe.transpose(ps[:, 4 + b // 4, (b % 4) * P:(b % 4 + 1) * P],
                                        y_tok[:, 2 * b:2 * b + 2, :].rearrange("p h d -> p (h d)"), c.ident[:, :])
                last.then_inc(y_turned, 1)

            pe.wait_ge(pre, 2)
            front_small(0, 0)
            front_seg(0, 0)
            steps(pe, step)


class BranchWeights:
    KA = D_ATTN // P
    KW = KA + XB

    def __init__(self, nc, ctx, w_attn, w_ssd):
        self.raw = ctx.enter_context(nc.sbuf_tensor("branch_raw", [P, RING, self.KW, P], F32))
        self.loaded = [ctx.enter_context(nc.semaphore(f"branch_loaded{s}")) for s in range(RING)]
        self.w_attn = w_attn.rearrange("(k p) c -> p k c", p=P)
        self.w_ssd = w_ssd.rearrange("(k p) c -> p k c", p=P)

    def load(self, sp, n, s):
        sp.dma_start(self.raw[:, s, 0:self.KA, :], self.w_attn[:, :, ds(n * P, P)]).then_inc(self.loaded[s], DMA)
        sp.dma_start(self.raw[:, s, self.KA:, :], self.w_ssd[:, :, ds(n * P, P)]).then_inc(self.loaded[s], DMA)

    def load_first(self, sp):
        for s in range(RING):
            self.load(sp, s, s)


def merge(nc, c, ps, weights, gates, gated, square_sum, gain, ya_hi, ya_lo, merged):
    KA, KW = weights.KA, weights.KW
    NB = D // P
    with ExitStack() as ctx:
        def sb(name, shape, dt=F32):
            return ctx.enter_context(nc.sbuf_tensor(name, shape, dt))

        def sem(name):
            return ctx.enter_context(nc.semaphore(name))

        ys_hi = sb("ys_hi", [P, XB, SEQ], F32R)
        ys_lo = sb("ys_lo", [P, XB, SEQ], F32R)
        gain_col = sb("ssd_gain_col", [P, XB])
        w_hi = sb("branch_hi", [P, RING, KW, P], F32R)
        w_lo = sb("branch_lo", [P, RING, KW, P], F32R)
        gate = sb("gate", [P, RING, 2, SEQ])
        rstd = square_sum
        gain_loaded = sem("ssd_gain_loaded")
        summed = sem("ssd_summed")
        mean_done = sem("ssd_mean_done")
        root_done = sem("ssd_root_done")
        rstd_done = sem("ssd_rstd_done")
        ys_hi_done = sem("ys_hi_done")
        ys_lo_done = sem("ys_lo_done")
        g_loaded = [sem(f"gate_loaded{s}") for s in range(RING)]
        hi_done = sem("branch_hi_done")
        lo_done = sem("branch_lo_done")
        projected = sem("branch_projected")
        scaled = sem("gate_scaled")
        weighed = sem("branch_weighed")
        added = sem("branch_added")
        block = ctx.enter_context(nc.Block())

        @block.sync
        def _(sp):
            with nc.allow_non_contiguous_dma(reason="a gain per channel"):
                sp.dma_start(gain_col[:, :], gain.rearrange("a (b p) -> p (a b)", p=P)).then_inc(gain_loaded, DMA)

            def load_gates(n, s):
                sp.wait_ge(added, n + 1)
                sp.dma_start(gate[:, s, 0, :], gates[ds(n, 1)].rearrange("a p t -> p (a t)")).then_inc(g_loaded[s], DMA)
                sp.dma_start(gate[:, s, 1, :], gates[ds(NB + n, 1)].rearrange("a p t -> p (a t)")).then_inc(g_loaded[s], DMA)

            for s in range(RING):
                load_gates(s, s)
            with sp.Fori(0, NB // RING - 1) as i:
                for s in range(RING):
                    n = RING * i + RING + s
                    sp.wait_ge(lo_done, n + 1)
                    weights.load(sp, n, s)
                    load_gates(n, s)

        @block.scalar
        def _(act):
            def high(n, s, i):
                act.wait_ge(weights.loaded[s], 2 * DMA * i + 2 * DMA)
                act.wait_ge(projected, n + 1)
                act.activation(w_hi[:, s, :, :], weights.raw[:, s, :, :], ACT.Copy).then_inc(hi_done, 1)

            high(0, 0, 0)
            act.wait_ge(gain_loaded, DMA)
            for b in range(XB):
                act.activation(ys_hi[:, b, :], gated[:, b, :], ACT.Copy, scale=gain_col[:, b:b + 1]).then_inc(ys_hi_done, 1)
            act.wait_ge(mean_done, 1)
            act.activation(rstd[:, :], rstd[:, :], ACT.Sqrt).then_inc(root_done, 1)
            high(1, 1, 0)
            with act.Fori(0, NB // RING - 1) as i:
                for s in range(RING):
                    high(RING * i + RING + s, s, i + 1)

        @block.gpsimd
        def _(pool):
            pool.sem_inc(lo_done, RING)

            def rest(n, s):
                pool.wait_ge(hi_done, n + 1)
                pool.tensor_tensor(w_lo[:, s, :, :], weights.raw[:, s, :, :], w_hi[:, s, :, :].bitcast(F32),
                                   ALU.subtract).then_inc(lo_done, 1)

            def scale_gate(n, s, i):
                pool.wait_ge(g_loaded[s], 2 * DMA * i + 2 * DMA)
                pool.tensor_tensor(gate[:, s, 1, :], gate[:, s, 1, :], rstd[:, :], ALU.mult).then_inc(scaled, 1)

            rest(0, 0)
            pool.wait_ge(rstd_done, 1)
            rest(1, 1)
            scale_gate(0, 0, 0)
            scale_gate(1, 1, 0)
            with pool.Fori(0, NB // RING - 1) as i:
                for s in range(RING):
                    n = RING * i + RING + s
                    rest(n, s)
                    scale_gate(n, s, i + 1)

        @block.tensor
        def _(pe):
            pe.sem_inc(projected, RING)
            for h in range(2):
                last = pe.matmul(ps[:, 4 + h, :], c.ones[:, :], square_sum[:, h * HALF:(h + 1) * HALF], start=True, stop=True)
            last.then_inc(summed, 1)

            def product(n, s, first):
                pe.wait_ge(lo_done, RING + n + 1)
                pe.wait_ge(added, n + 1)
                for k in range(KW):
                    hi, lo, kk, b = (ya_hi, ya_lo, k, 4 * s) if k < KA else (ys_hi, ys_lo, k - KA, 4 * s + 2)
                    if first and k >= KA:
                        pe.wait_ge(ys_lo_done, kk + 1)
                    last = three_passes(pe, [ps[:, b, :], ps[:, b + 1, :]], w_hi[:, s, k, :], w_lo[:, s, k, :],
                                        [hi[:, kk, 0:HALF], hi[:, kk, HALF:SEQ]], [lo[:, kk, 0:HALF], lo[:, kk, HALF:SEQ]],
                                        kk == 0, k in (KA - 1, KW - 1))
                last.then_inc(projected, 1)

            product(0, 0, True)
            pe.wait_ge(mean_done, 1)
            product(1, 1, False)
            with pe.Fori(0, NB // RING - 1) as i:
                for s in range(RING):
                    product(RING * i + RING + s, s, False)

        @block.vector
        def _(dve):
            dve.sem_inc(added, RING)
            dve.wait_ge(summed, 1)
            dve.tensor_scalar(rstd[:, :], banks(ps, 4, 2), 1.0 / D_SSD, EPS, ALU.mult, ALU.add).then_inc(mean_done, 1)
            for b in range(XB):
                dve.wait_ge(ys_hi_done, b + 1)
                dve.scalar_tensor_tensor(out=ys_lo[:, b, :], in0=gated[:, b, :], scalar=gain_col[:, b:b + 1],
                                         in1=ys_hi[:, b, :].bitcast(F32), op0=ALU.mult, op1=ALU.subtract).then_inc(ys_lo_done, 1)
            dve.wait_ge(root_done, 1)
            dve.reciprocal(rstd[:, :], rstd[:, :]).then_inc(rstd_done, 1)
            with dve.Fori(0, NB // RING) as i:
                for s in range(RING):
                    n = RING * i + s
                    out = merged[:, ds(n, 1), :].rearrange("p a t -> p (a t)")
                    dve.wait_ge(projected, RING + n + 1)
                    dve.wait_ge(scaled, n + 1)
                    for g in range(2):
                        dve.tensor_tensor(gate[:, s, g, :], banks(ps, 4 * s + 2 * g, 2), gate[:, s, g, :], ALU.mult).then_inc(weighed, 1)
                    dve.wait_ge(weighed, 2 * n + 2)
                    dve.tensor_tensor(out, gate[:, s, 0, :], gate[:, s, 1, :], ALU.add).then_inc(added, 1)


def project_out(nc, ps, w_out, x, merged, x2):
    W_RING = 4
    with ExitStack() as ctx:
        def sb(name, shape, dt=F32):
            return ctx.enter_context(nc.sbuf_tensor(name, shape, dt))

        def sem(name):
            return ctx.enter_context(nc.semaphore(name))

        w_raw = sb("out_raw", [P, W_RING, D])
        w_hi = sb("out_hi", [P, KT, D], F32R)
        w_lo = sb("out_lo", [P, KT, D], F32R)
        m_hi = sb("merged_hi", [P, RING, KT, P], F32R)
        m_lo = sb("merged_lo", [P, RING, KT, P], F32R)
        x_tile = sb("x_tile", [P, RING, D])
        w_loaded = [sem(f"out_loaded{s}") for s in range(W_RING)]
        x_loaded = [sem(f"res_loaded{s}") for s in range(RING)]
        w_hi_done = sem("out_hi_done")
        w_lo_done = sem("out_lo_done")
        m_hi_done = sem("merged_hi_done")
        m_lo_done = sem("merged_lo_done")
        projected = sem("out_projected")
        added = sem("out_added")
        x_tiles = x[0].rearrange("(t p) d -> t p d", p=P)
        w_rows = w_out.rearrange("(k p) c -> k p c", p=P)
        block = ctx.enter_context(nc.Block())

        @block.sync
        def _(sp):
            for k in range(KT):
                sp.wait_ge(w_lo_done, k + 1)
                sp.dma_start(w_raw[:, k % W_RING, :], w_rows[k]).then_inc(w_loaded[k % W_RING], DMA)
            with sp.Fori(0, TT // RING) as i:
                for s in range(RING):
                    sp.wait_ge(added, RING * i + s + 1)
                    sp.dma_start(x_tile[:, s, :], x_tiles[ds(RING * i + s, 1)].rearrange("a p d -> p (a d)")).then_inc(x_loaded[s], DMA)

        @block.scalar
        def _(act):
            def high(t, s):
                act.wait_ge(projected, t + 1)
                act.activation(m_hi[:, s, :, :], merged[:, :, ds(t * P, P)], ACT.Copy).then_inc(m_hi_done, 1)

            high(0, 0)
            for k in range(KT):
                act.wait_ge(w_loaded[k % W_RING], DMA * (k // W_RING) + DMA)
                act.activation(w_hi[:, k, :], w_raw[:, k % W_RING, :], ACT.Copy).then_inc(w_hi_done, 1)
            high(1, 1)
            with act.Fori(0, TT // RING - 1) as i:
                for s in range(RING):
                    high(RING * i + RING + s, s)

        @block.tensor
        def _(pe):
            pe.sem_inc(projected, RING)

            def product(t, s, first):
                pe.wait_ge(m_lo_done, t + 1)
                pe.wait_ge(added, t + 1)
                for k in range(KT):
                    if first:
                        pe.wait_ge(w_lo_done, W_RING + k + 1)
                    last = three_passes(pe, [ps[:, 2 * s, :], ps[:, 2 * s + 1, :]], m_hi[:, s, k, :], m_lo[:, s, k, :],
                                        [w_hi[:, k, 0:HALF], w_hi[:, k, HALF:D]], [w_lo[:, k, 0:HALF], w_lo[:, k, HALF:D]],
                                        k == 0, k == KT - 1)
                last.then_inc(projected, 1)

            product(0, 0, True)
            product(1, 1, False)
            with pe.Fori(0, TT // RING - 1) as i:
                for s in range(RING):
                    product(RING * i + RING + s, s, False)

        @block.vector
        def _(dve):
            dve.sem_inc(w_lo_done, W_RING)
            dve.sem_inc(added, RING)

            def rest(t, s):
                dve.wait_ge(m_hi_done, t + 1)
                dve.tensor_tensor(m_lo[:, s, :, :], merged[:, :, ds(t * P, P)], m_hi[:, s, :, :].bitcast(F32),
                                  ALU.subtract).then_inc(m_lo_done, 1)

            rest(0, 0)
            for k in range(KT):
                dve.wait_ge(w_hi_done, k + 1)
                dve.tensor_tensor(w_lo[:, k, :], w_raw[:, k % W_RING, :], w_hi[:, k, :].bitcast(F32), ALU.subtract).then_inc(w_lo_done, 1)
            def add(t, s, i):
                dve.wait_ge(projected, RING + t + 1)
                dve.wait_ge(x_loaded[s], DMA * i + DMA)
                dve.tensor_tensor(x2[:, ds(t, 1), :].rearrange("p a d -> p (a d)"), banks(ps, 2 * s, 2), x_tile[:, s, :],
                                  ALU.add).then_inc(added, 1)

            rest(1, 1)
            with dve.Fori(0, TT // RING - 1) as i:
                for s in range(RING):
                    add(RING * i + s, s, i)
                    rest(RING * i + RING + s, s)
            for s in range(RING):
                add(TT - RING + s, s, TT // RING - 1)


def router_logits(nc, c, ps, x2, gain, w_group, b_group, w_expert, b_expert, h2_rows, logits, weights):
    NL = N_GROUPS + NE
    with ExitStack() as ctx:
        def sb(name, shape, dt=F32):
            return ctx.enter_context(nc.sbuf_tensor(name, shape, dt))

        def sem(name):
            return ctx.enter_context(nc.semaphore(name))

        w_router = sb("w_router", [P, KT, NL])
        b_router = sb("b_router", [P, NL])
        gain_row = sb("gain2_row", [P, D])
        squares = sb("squares2", [P, D])
        sum_sq = sb("sum_sq2", [P, TT])
        mean_sq = sb("mean_sq2", [P, TT])
        root = sb("root2", [P, TT])
        rstd = sb("rstd2", [P, TT])
        h2 = sb("h2", [P, RING, D])
        h2_t = sb("h2_t", [P, RING, KT, P])
        loaded = sem("router_loaded")
        squared = sem("squared2")
        mean_done = sem("mean_done2")
        root_done = sem("root_done2")
        rstd_done = sem("rstd_done2")
        h2_done = sem("h2_done")
        stored = [sem(f"h2_stored{s}") for s in range(RING)]
        turned = sem("h2_turned")
        t_done = sem("h2_t_done")
        routed = sem("routed")
        logit_done = sem("logit_done")
        h2_tiles = h2_rows.rearrange("(t p) d -> t p d", p=P)
        block = ctx.enter_context(nc.Block())

        @block.sync
        def _(sp):
            with nc.allow_non_contiguous_dma(reason="narrow router weights"):
                sp.dma_start(w_router[:, :, 0:N_GROUPS], w_group.rearrange("(k p) g -> p k g", p=P)).then_inc(loaded, DMA)
                sp.dma_start(w_router[:, :, N_GROUPS:NL], w_expert.rearrange("(k p) g -> p k g", p=P)).then_inc(loaded, DMA)
                sp.dma_start(b_router[:, 0:N_GROUPS], b_group.to_broadcast([P, N_GROUPS])).then_inc(loaded, DMA)
                sp.dma_start(b_router[:, N_GROUPS:NL], b_expert.to_broadcast([P, NE])).then_inc(loaded, DMA)
            sp.dma_start(gain_row[:, :], gain.to_broadcast([P, D])).then_inc(loaded, DMA)
            load_first_expert(sp, weights)
            for s in range(RING):
                sp.sem_inc(stored[s], DMA)
            with sp.Fori(0, TT // RING) as i:
                for s in range(RING):
                    sp.wait_ge(h2_done, RING * i + s + 1)
                    sp.dma_start(h2_tiles[ds(RING * i + s, 1)].rearrange("a p d -> p (a d)"), h2[:, s, :]).then_inc(stored[s], DMA)
            for s in range(RING):
                sp.wait_ge(stored[s], DMA * (TT // RING) + DMA)

        @block.scalar
        def _(act):
            act.sem_inc(squared, 1)
            with act.Fori(0, TT) as t:
                act.wait_ge(squared, 1 + t)
                act.activation(squares[:, :], x2[:, ds(t, 1), :].rearrange("p a d -> p (a d)"), ACT.Square,
                               accum_out=sum_sq[:, ds(t, 1)]).then_inc(squared, 1)
            act.wait_ge(mean_done, 1)
            act.activation(root[:, :], mean_sq[:, :], ACT.Sqrt).then_inc(root_done, 1)
            with act.Fori(0, TT // RING) as i:
                for s in range(RING):
                    t = RING * i + s
                    act.wait_ge(turned, RING + t + 1)
                    act.wait_ge(routed, t + 1)
                    act.activation(h2_t[:, s, :, :].rearrange("p k t -> p (k t)"), banks(ps, 2 * s, 2), ACT.Copy).then_inc(t_done, 1)

        @block.vector
        def _(dve):
            dve.sem_inc(logit_done, RING)
            dve.wait_ge(squared, 1 + TT)
            dve.tensor_scalar(mean_sq[:, :], sum_sq[:, :], 1.0 / D, EPS, ALU.mult, ALU.add).then_inc(mean_done, 1)
            dve.wait_ge(root_done, 1)
            dve.reciprocal(rstd[:, :], root[:, :]).then_inc(rstd_done, 1)
            dve.wait_ge(rstd_done, 1)
            dve.wait_ge(loaded, 5 * DMA)
            with dve.Fori(0, TT // RING) as i:
                for s in range(RING):
                    t = RING * i + s
                    dve.wait_ge(turned, t + 1)
                    dve.wait_ge(stored[s], DMA * i + DMA)
                    dve.scalar_tensor_tensor(out=h2[:, s, :], in0=x2[:, ds(t, 1), :].rearrange("p a d -> p (a d)"),
                                             scalar=rstd[:, ds(t, 1)], in1=gain_row[:, :], op0=ALU.mult,
                                             op1=ALU.mult).then_inc(h2_done, 1)
                for s in range(RING):
                    t = RING * i + s
                    dve.wait_ge(routed, RING + t + 1)
                    dve.tensor_tensor(logits[:, ds(t, 1), :].rearrange("p a l -> p (a l)"), ps[:, 4 + s, 0:NL], b_router[:, :],
                                      ALU.add).then_inc(logit_done, 1)

        @block.tensor
        def _(pe):
            pe.sem_inc(turned, RING)
            pe.sem_inc(routed, RING)
            pe.wait_ge(loaded, 5 * DMA)
            with pe.Fori(0, TT // RING) as i:
                for s in range(RING):
                    t = RING * i + s
                    pe.wait_ge(h2_done, t + 1)
                    for k in range(KT):
                        last = pe.transpose(banks(ps, 2 * s, 2)[:, k * P:(k + 1) * P], h2[:, s, k * P:(k + 1) * P], c.ident[:, :])
                    last.then_inc(turned, 1)
                for s in range(RING):
                    t = RING * i + s
                    pe.wait_ge(t_done, t + 1)
                    pe.wait_ge(logit_done, t + 1)
                    for k in range(KT):
                        last = pe.matmul(ps[:, 4 + s, 0:NL], h2_t[:, s, k, :], w_router[:, k, :], start=k == 0, stop=k == KT - 1)
                    last.then_inc(routed, 1)


def route(nc, c, ps, logits, gates, slot_table, gather_src, scatter_dst, over_expert):
    with ExitStack() as ctx:
        def sb(name, shape, dt=F32):
            return ctx.enter_context(nc.sbuf_tensor(name, shape, dt))

        def sem(name):
            return ctx.enter_context(nc.semaphore(name))

        unused = sb("unused", [P, BLOCKS], I32)
        source = sb("source", [P, TOPK, TT], I32)
        expert_no = sb("expert_no", [P, NE])
        expert_base = sb("expert_base", [P, NE])
        block_no = sb("block_no", [P, MAX_OVER])
        limits = sb("limits", [P, TT - 1])
        group_logits = sb("group_logits", [P, TT, 8])
        group_top = sb("group_top", [P, TT, 8])
        group_at = sb("group_at", [P, TT, 8], U32)
        group_index = sb("group_index", [P, TT])
        group_less = sb("group_less", [P, TT, N_GROUPS])
        group_exp = sb("group_exp", [P, TT, N_GROUPS])
        group_sum = sb("group_sum", [P, TT])
        penalty = sb("penalty", [P, TT, N_GROUPS])
        expert_logits = sb("expert_logits", [P, TT, NE])
        expert_top = sb("expert_top", [P, TT, 8])
        expert_at = sb("expert_at", [P, TT, 8], U32)
        choice = sb("choice", [P, TOPK, TT])
        expert_less = sb("expert_less", [P, TT, NE])
        expert_exp = sb("expert_exp", [P, TT, NE])
        expert_sum = sb("expert_sum", [P, TT])
        second_less = sb("second_less", [P, TT])
        second_exp = sb("second_exp", [P, TT])
        denominator = sb("denominator", [P, TT])
        picked = sb("picked", [P, TOPK, TT, NE])
        either = sb("either", [P, TT, NE])
        running = sb("running", [P, TT + 1, NE])
        position = sb("position", [P, TT, NE])
        count = sb("count", [P, NE])
        above = sb("above", [P, NE, TT - 1])
        over = sb("over", [P, NE])
        over_upto = sb("over_upto", [P, NE])
        ones_row = sb("ones_row", [P, NE])
        over_base = sb("over_base", [P, NE])
        base_gap = sb("base_gap", [P, NE])
        low = sb("low", [P, TT, NE])
        slot_of = sb("slot_of", [P, TT, NE])
        slot_pick = sb("slot_pick", [P, TOPK, TT, NE])
        slot_f = sb("slot_f", [P, TOPK, TT])
        slot_i = sb("slot_i", [P, TOPK, TT], I32)
        passed = sb("passed", [P, MAX_OVER, NE])
        over_f = sb("over_f", [P, MAX_OVER + 1])
        table = sb("table", [P, BLOCKS], I32)
        made = sem("route_constants")
        cleared = sem("table_cleared")
        vec = sem("route_vec")
        expd = sem("route_exp")
        placed = sem("route_placed")
        slots_done = sem("slots_done")
        scattered = sem("table_scattered")
        table_loaded = sem("table_loaded")
        block = ctx.enter_context(nc.Block())
        steps = [0]

        def bc(ap, shape, axis):
            return spread(ap, shape, axis)

        @block.gpsimd
        def _(pool):
            pool.memset(group_logits[:, :, :], MASKED)
            pool.memset(ones_row[:, :], 1.0)
            pool.memset(running[:, 0, :], 0.0)
            pool.iota(unused[:, :], pattern=[[1, BLOCKS]], base=TOPK * SEQ, channel_multiplier=BLOCKS)
            pool.iota(source[:, :, :], pattern=[[SEQ, TOPK], [P, TT]], base=0, channel_multiplier=1)
            f = {"allow_small_or_imprecise_dtypes": True}
            pool.iota(expert_no[:, :], pattern=[[1, NE]], base=0, channel_multiplier=0, **f)
            pool.iota(expert_base[:, :], pattern=[[P, NE]], base=0, channel_multiplier=0, **f)
            pool.iota(block_no[:, :], pattern=[[1, MAX_OVER]], base=0, channel_multiplier=0, **f)
            pool.iota(limits[:, :], pattern=[[P, TT - 1]], base=P, channel_multiplier=0, **f).then_inc(made, 1)
            pool.wait_ge(made, 1)
            pool.dma_start(slot_table.rearrange("(p b) a -> p (b a)", p=P), unused[:, :]).then_inc(cleared, DMA)
            pool.wait_ge(cleared, DMA)
            pool.wait_ge(slots_done, 1)
            for k in range(TOPK):
                for t in range(TT):
                    pool.indirect_dma_start(out=slot_table, out_offset=bass.IndirectOffsetOnAxis(ap=slot_i[:, k, t:t + 1], axis=0),
                                            in_=source[:, k, t:t + 1], in_offset=None).then_inc(scattered, DMA)
            pool.wait_ge(scattered, TOPK * TT * DMA)
            pool.dma_start(table[:, :], slot_table.rearrange("(b p) a -> p (b a)", p=P),
                           allow_slow_non_contiguous=True).then_inc(table_loaded, DMA)

        @block.scalar
        def _(act):
            act.wait_ge(expd, 1)
            act.activation(group_exp[:, :, :], group_less[:, :, :], ACT.Exp).then_inc(expd, 1)
            act.wait_ge(expd, 3)
            act.activation(expert_exp[:, :, :], expert_less[:, :, :], ACT.Exp)
            act.activation(second_exp[:, :], second_less[:, :], ACT.Exp).then_inc(expd, 1)

        @block.tensor
        def _(pe):
            pe.wait_ge(placed, 1)
            flat = ps[:, 0, 0:TT * NE]
            pe.matmul(flat, c.tri_before[:, :], either[:, :, :].rearrange("p t e -> p (t e)"), start=True, stop=False)
            pe.matmul(flat, c.ones[:, :], running[:, 0:TT, :].rearrange("p t e -> p (t e)"), start=False, stop=True)
            pe.matmul(ps[:, 1, 0:NE], c.ones[:, :], running[:, TT, :], start=True, stop=True).then_inc(placed, 1)

        @block.vector
        def _(dve):
            def then(ins):
                steps[0] += 1
                ins.then_inc(vec, 1)
                dve.wait_ge(vec, steps[0])

            dve.wait_ge(made, 1)
            then(dve.tensor_copy(group_logits[:, :, 0:N_GROUPS], logits[:, :, 0:N_GROUPS]))
            for t in range(TT):
                ins = dve.max(group_top[:, t, :], group_logits[:, t, :])
            then(ins)
            for t in range(TT):
                ins = dve.max_index(group_at[:, t, :], group_top[:, t, :], group_logits[:, t, :])
            then(ins)
            dve.tensor_tensor(group_less[:, :, :], logits[:, :, 0:N_GROUPS],
                              group_top[:, :, 0:1].to_broadcast([P, TT, N_GROUPS]), ALU.subtract).then_inc(expd, 1)
            then(dve.tensor_copy(group_index[:, :], group_at[:, :, 0]))
            then(dve.tensor_tensor(penalty[:, :, :], bc(expert_no[:, 0:N_GROUPS], [P, TT, N_GROUPS], 1),
                                   bc(group_index[:, :], [P, TT, N_GROUPS], 2), ALU.is_equal))
            then(dve.tensor_scalar(penalty[:, :, :], penalty[:, :, :], -MASKED, MASKED, ALU.mult, ALU.add))
            then(dve.tensor_tensor(expert_logits[:, :, :].rearrange("p t (g e) -> p t g e", g=N_GROUPS),
                                   logits[:, :, N_GROUPS:].rearrange("p t (g e) -> p t g e", g=N_GROUPS),
                                   bc(penalty[:, :, :], [P, TT, N_GROUPS, PER_GROUP], 3), ALU.add))
            for t in range(TT):
                ins = dve.max(expert_top[:, t, :], expert_logits[:, t, :])
            then(ins)
            for t in range(TT):
                ins = dve.max_index(expert_at[:, t, :], expert_top[:, t, :], expert_logits[:, t, :])
            then(ins)
            dve.wait_ge(expd, 2)
            dve.tensor_tensor(expert_less[:, :, :], expert_logits[:, :, :], expert_top[:, :, 0:1].to_broadcast([P, TT, NE]),
                              ALU.subtract)
            dve.tensor_tensor(second_less[:, :], expert_top[:, :, 1], expert_top[:, :, 0], ALU.subtract).then_inc(expd, 1)
            dve.tensor_reduce(group_sum[:, :], group_exp[:, :, :], AX.X, ALU.add)
            for k in range(TOPK):
                ins = dve.tensor_copy(choice[:, k, :], expert_at[:, :, k])
            then(ins)
            for k in range(TOPK):
                ins = dve.tensor_tensor(picked[:, k, :, :], bc(expert_no[:, :], [P, TT, NE], 1),
                                        bc(choice[:, k, :], [P, TT, NE], 2), ALU.is_equal)
            then(ins)
            then(dve.tensor_tensor(either[:, :, :], picked[:, 0, :, :], picked[:, 1, :, :], ALU.add))
            for t in range(TT):
                then(dve.tensor_tensor(running[:, t + 1, :], running[:, t, :], either[:, t, :], ALU.add))
            dve.sem_inc(placed, 1)
            dve.wait_ge(expd, 4)
            then(dve.tensor_reduce(expert_sum[:, :], expert_exp[:, :, :], AX.X, ALU.add))
            then(dve.tensor_tensor(denominator[:, :], group_sum[:, :], expert_sum[:, :], ALU.mult))
            then(dve.reciprocal(gates[:, 0, :], denominator[:, :]))
            dve.tensor_tensor(gates[:, 1, :], gates[:, 0, :], second_exp[:, :], ALU.mult)
            dve.wait_ge(placed, 2)
            dve.tensor_copy(position[:, :, :].rearrange("p t e -> p (t e)"), ps[:, 0, 0:TT * NE])
            then(dve.tensor_copy(count[:, :], ps[:, 1, 0:NE]))
            then(dve.tensor_tensor(above[:, :, :], bc(count[:, :], [P, NE, TT - 1], 2), bc(limits[:, :], [P, NE, TT - 1], 1), ALU.is_gt))
            then(dve.tensor_reduce(over[:, :], above[:, :, :], AX.X, ALU.add))
            then(dve.tensor_tensor_scan(over_upto[:, :], ones_row[:, :], over[:, :], 0.0, ALU.mult, ALU.add))
            then(dve.tensor_tensor(over_base[:, :], over_upto[:, :], over[:, :], ALU.subtract))
            then(dve.tensor_scalar(over_base[:, :], over_base[:, :], float(NE - 1), float(P), ALU.add, ALU.mult))
            dve.tensor_tensor(base_gap[:, :], expert_base[:, :], over_base[:, :], ALU.subtract)
            then(dve.tensor_scalar(low[:, :, :], position[:, :, :], float(P), None, ALU.is_lt))
            then(dve.tensor_tensor(slot_of[:, :, :], low[:, :, :], bc(base_gap[:, :], [P, TT, NE], 1), ALU.mult))
            then(dve.tensor_tensor(slot_of[:, :, :], slot_of[:, :, :], bc(over_base[:, :], [P, TT, NE], 1), ALU.add))
            then(dve.tensor_tensor(slot_of[:, :, :], slot_of[:, :, :], position[:, :, :], ALU.add))
            for k in range(TOPK):
                ins = dve.tensor_tensor(slot_pick[:, k, :, :], picked[:, k, :, :], slot_of[:, :, :], ALU.mult)
            then(ins)
            then(dve.tensor_reduce(slot_f[:, :, :], slot_pick[:, :, :, :], AX.X, ALU.add))
            dve.tensor_copy(slot_i[:, :, :], slot_f[:, :, :]).then_inc(slots_done, 1)
            then(dve.tensor_tensor(passed[:, :, :], bc(over_upto[:, :], [P, MAX_OVER, NE], 1),
                                   bc(block_no[:, :], [P, MAX_OVER, NE], 2), ALU.is_le))
            then(dve.tensor_reduce(over_f[:, 0:MAX_OVER], passed[:, :, :], AX.X, ALU.add))
            then(dve.tensor_scalar(over_f[:, 0:MAX_OVER], over_f[:, 0:MAX_OVER], float(NE - 1), None, ALU.min))
            then(dve.tensor_copy(over_f[:, MAX_OVER:], over_upto[:, NE - 1:NE]))
            dve.tensor_copy(over_expert[:, :], over_f[:, :])
            dve.wait_ge(table_loaded, DMA)
            dve.tensor_copy(scatter_dst[:, :], table[:, :])
            dve.tensor_scalar(gather_src[:, :], table[:, :], SEQ - 1, None, ALU.bitwise_and)


UP_WAVES = 4
DOWN_WAVES = 2
WAVES = UP_WAVES + DOWN_WAVES


class ExpertWeights:

    def __init__(self, nc, ctx, w1, w3, w2):
        shape = [P, WAVES, 2, D]
        at = region(nc, ctx, "weights_at", WAVES * 2 * D * 4)
        self.raw = nc.alloc_sbuf_tensor_at("weights_raw", shape, F32, offset=at)
        self.lo = nc.alloc_sbuf_tensor_at("weights_lo", shape, F32R, offset=at)
        self.hi = ctx.enter_context(nc.sbuf_tensor("weights_hi", shape, F32R))
        self.loaded = [ctx.enter_context(nc.semaphore(f"wave_loaded{w}")) for w in range(WAVES)]
        self.w1 = w1.rearrange("e (w k p) f -> e w p k f", k=2, p=P)
        self.w3 = w3.rearrange("e (w k p) f -> e w p k f", k=2, p=P)
        self.w2 = w2.rearrange("e (w k p) f -> e w p k f", k=2, p=P)

    def load_up(self, sp, n, wave):
        for half, w in enumerate((self.w1, self.w3)):
            sp.dma_start(self.raw[:, wave, :, half * FF:(half + 1) * FF],
                         w[ds(n, 1), wave].rearrange("e p k f -> p (e k) f")).then_inc(self.loaded[wave], DMA)

    def load_down(self, sp, n, wave):
        sp.dma_start(self.raw[:, wave, :, :],
                     self.w2[ds(n, 1), wave - UP_WAVES].rearrange("e p k f -> p (e k) f")).then_inc(self.loaded[wave], DMA)

    def count(self, wave):
        return 2 * DMA if wave < UP_WAVES else DMA


def load_first_expert(sp, weights):
    for w in range(UP_WAVES):
        weights.load_up(sp, 0, w)
    for w in range(UP_WAVES, WAVES):
        weights.load_down(sp, 0, w)


def experts(nc, c, ps, weights, h2_rows, y_rows, gather_src, scatter_dst):
    UP = range(UP_WAVES)
    DOWN = range(UP_WAVES, WAVES)
    BY_POOL = (1, 4)
    with ExitStack() as ctx:
        def sb(name, shape, dt=F32):
            return ctx.enter_context(nc.sbuf_tensor(name, shape, dt))

        def sem(name):
            return ctx.enter_context(nc.semaphore(name))

        index = sb("index", [P, RING, 2], I32)
        x_rows = sb("x_rows", [P, RING, D])
        x_hi = sb("x_hi", [P, RING, KT, P], F32R)
        x_lo = sb("x_lo", [P, RING, KT, P], F32R)
        act_up = sb("act_up", [P, FF])
        g_tok = sb("g_tok", [P, FF])
        g_hi = sb("g_hi", [P, FT, P], F32R)
        g_lo = sb("g_lo", [P, FT, P], F32R)
        y_out = sb("y_out", [P, RING, D])
        w_hi_done = [sem(f"wave_hi{w}") for w in range(WAVES)]
        w_lo_done = [sem(f"wave_lo{w}") for w in range(WAVES)]
        used = [sem(f"wave_used{w}") for w in range(WAVES)]
        held = sem("experts_held")
        indexed = sem("indexed")
        aimed = sem("aimed")
        gathered = [sem(f"gathered{s}") for s in range(RING)]
        scattered = [sem(f"scattered{s}") for s in range(RING)]
        x_turned = sem("moe_x_turned")
        x_hi_done = sem("moe_x_hi")
        x_lo_done = sem("moe_x_lo")
        up_done = used[UP[-1]]
        silu_done = sem("moe_silu_done")
        g_done = sem("g_done")
        g_turned = sem("g_turned")
        g_hi_done = sem("moe_g_hi")
        g_lo_done = sem("moe_g_lo")
        down_done = used[DOWN[-1]]
        y_ready = sem("y_ready")
        y_free = sem("y_free")
        block = ctx.enter_context(nc.Block())

        def rounds(eng, body):
            body(0, 0, True, False)
            with eng.Fori(0, NE // RING - 1) as i:
                body(RING * i + 1, 1, True, True)
                body(RING * i + 2, 0, True, True)
            body(NE - 1, 1, True, True)
            body(NE, 0, False, True)

        def follows(n):
            return not isinstance(n, int) or n + 1 < NE

        @block.sync
        def _(sp):
            def load_up(n):
                for w in UP:
                    sp.wait_ge(used[w], n)
                    weights.load_up(sp, n, w)

            def load_down(n):
                for w in DOWN:
                    sp.wait_ge(used[w], n)
                    weights.load_down(sp, n, w)

            load_up(1)
            with sp.Fori(0, NE - 2) as i:
                load_up(i + 2)
                load_down(i + 1)
            load_down(NE - 1)

        @block.gpsimd
        def _(pool):
            def gather(n, s):
                pool.wait_ge(x_turned, n + 1)
                pool.tensor_copy(index[:, s, 0:1], gather_src[:, ds(n, 1)]).then_inc(indexed, 1)
                pool.wait_ge(indexed, n + 1)
                pool.sem_inc(held, 1)
                pool.indirect_dma_start(out=x_rows[:, s, :], out_offset=None, in_=h2_rows,
                                        in_offset=bass.IndirectOffsetOnAxis(ap=index[:, s, 0:1], axis=0)).then_inc(gathered[s], DMA)

            def scatter(n, s, i):
                if i is not None:
                    pool.wait_ge(scattered[s], DMA * i)
                    pool.sem_inc(y_free, 1)
                pool.tensor_copy(index[:, s, 1:2], scatter_dst[:, ds(n, 1)]).then_inc(aimed, 1)
                pool.wait_ge(aimed, n + 1)
                pool.wait_ge(y_ready, 1 + n + 1)
                pool.sem_inc(held, 1)
                pool.indirect_dma_start(out=y_rows, out_offset=bass.IndirectOffsetOnAxis(ap=index[:, s, 1:2], axis=0),
                                        in_=y_out[:, s, :], in_offset=None).then_inc(scattered[s], DMA)

            def rest(n, w):
                pool.wait_ge(w_hi_done[w], n + 1)
                pool.tensor_tensor(weights.lo[:, w, :, :], weights.raw[:, w, :, :], weights.hi[:, w, :, :].bitcast(F32),
                                   ALU.subtract).then_inc(w_lo_done[w], 1)

            def body(n, s, i, ahead, nxt):
                if ahead:
                    gather(n + RING, s)
                rest(n - 1, DOWN[0])
                if nxt:
                    rest(n + 1, UP[1])
                scatter(n - 1, 1 - s, i)

            pool.sem_inc(y_free, RING)
            for s in range(RING):
                gather(s, s)
            rest(0, UP[1])
            gather(RING, 0)
            rest(1, UP[1])
            body(1, 1, None, True, True)
            body(2, 0, None, True, True)
            with pool.Fori(0, NE // RING - 3) as i:
                body(RING * i + 3, 1, i + 1, True, True)
                body(RING * i + 4, 0, i + 1, True, True)
            body(NE - 3, 1, NE // RING - 2, True, True)
            body(NE - 2, 0, NE // RING - 2, False, True)
            body(NE - 1, 1, NE // RING - 1, False, False)
            body(NE, 0, NE // RING - 1, False, False)
            for s in range(RING):
                pool.wait_ge(scattered[s], DMA * (NE // RING))

        @block.scalar
        def _(act):
            def high(n, w):
                act.wait_ge(weights.loaded[w], weights.count(w) * n + weights.count(w))
                act.activation(weights.hi[:, w, :, :], weights.raw[:, w, :, :], ACT.Copy).then_inc(w_hi_done[w], 1)

            def x_out(n, s):
                act.wait_ge(x_turned, RING + n + 1)
                act.activation(x_hi[:, s, :, :].rearrange("p k t -> p (k t)"), banks(ps, 0, 2), ACT.Copy).then_inc(x_hi_done, 1)

            def body(n, s, up, down):
                if follows(n) and up:
                    x_out(n + 1, 1 - s)
                if down:
                    high(n - 1, DOWN[0])
                    act.wait_ge(g_turned, n)
                    act.activation(g_hi[:, :, :].rearrange("p k t -> p (k t)"), ps[:, 4, :], ACT.Copy).then_inc(g_hi_done, 1)
                    high(n - 1, DOWN[1])
                if follows(n) and up:
                    for w in (0, 1):
                        high(n + 1, w)
                if up:
                    act.wait_ge(up_done, n + 1)
                    act.wait_ge(g_done, 1 + n)
                    act.activation(act_up[:, :], ps[:, 2, :], ACT.Silu).then_inc(silu_done, 1)
                if follows(n) and up:
                    for w in (2, 3):
                        high(n + 1, w)

            for w in UP:
                high(0, w)
            x_out(0, 0)
            rounds(act, body)

        @block.vector
        def _(dve):
            for ready in (g_done, g_lo_done, x_lo_done, y_ready):
                dve.sem_inc(ready, 1)

            def rest(n, w):
                dve.wait_ge(w_hi_done[w], n + 1)
                dve.tensor_tensor(weights.lo[:, w, :, :], weights.raw[:, w, :, :], weights.hi[:, w, :, :].bitcast(F32),
                                  ALU.subtract).then_inc(w_lo_done[w], 1)

            def x_rest(n, s):
                dve.wait_ge(x_hi_done, n + 1)
                dve.tensor_tensor(x_lo[:, s, :, :].rearrange("p k t -> p (k t)"), banks(ps, 0, 2),
                                  x_hi[:, s, :, :].rearrange("p k t -> p (k t)").bitcast(F32), ALU.subtract).then_inc(x_lo_done, 1)

            def body(n, s, up, down):
                nxt = follows(n) and up
                if nxt:
                    x_rest(n + 1, 1 - s)
                if down:
                    dve.wait_ge(g_hi_done, n)
                    dve.tensor_tensor(g_lo[:, :, :].rearrange("p k t -> p (k t)"), ps[:, 4, :],
                                      g_hi[:, :, :].rearrange("p k t -> p (k t)").bitcast(F32), ALU.subtract).then_inc(g_lo_done, 1)
                    rest(n - 1, DOWN[1])
                if nxt:
                    rest(n + 1, 0)
                if up:
                    dve.wait_ge(silu_done, n + 1)
                    dve.tensor_tensor(g_tok[:, :], ps[:, 3, :], act_up[:, :], ALU.mult).then_inc(g_done, 1)
                if nxt:
                    rest(n + 1, 2)
                if down:
                    dve.wait_ge(down_done, n)
                    dve.wait_ge(y_free, n)
                    dve.tensor_copy(y_out[:, 1 - s, :], banks(ps, 5, 2)).then_inc(y_ready, 1)
                if nxt:
                    rest(n + 1, 3)

            for w in UP:
                if w not in BY_POOL:
                    rest(0, w)
            x_rest(0, 0)
            rounds(dve, body)

        @block.tensor
        def _(pe):
            pe.sem_inc(x_turned, RING)

            def turn_x(n, s, i):
                pe.wait_ge(gathered[s], DMA * i + DMA)
                pe.wait_ge(x_lo_done, 1 + n)
                for k in range(KT):
                    last = pe.transpose(ps[:, k // 4, (k % 4) * P:(k % 4 + 1) * P], x_rows[:, s, k * P:(k + 1) * P], c.ident[:, :])
                last.then_inc(x_turned, 1)

            def turn_g(n):
                pe.wait_ge(g_done, 1 + n + 1)
                pe.wait_ge(g_lo_done, 1 + n)
                for k in range(FT):
                    last = pe.transpose(ps[:, 4, k * P:(k + 1) * P], g_tok[:, k * P:(k + 1) * P], c.ident[:, :])
                last.then_inc(g_turned, 1)

            def products(out, w, kk, a_hi, a_lo, first, last):
                for a, b, opens, closes in ((a_hi, weights.hi, first, False), (a_hi, weights.lo, False, False),
                                            (a_lo, weights.hi, False, last)):
                    for h in range(2):
                        ins = pe.matmul(out[h], a, b[:, w, kk, h * HALF:(h + 1) * HALF], start=opens, stop=closes)
                return ins

            def up(n, s):
                pe.wait_ge(x_lo_done, 1 + n + 1)
                pe.wait_ge(g_done, 1 + n)
                for w in UP:
                    pe.wait_ge(w_lo_done[w], n + 1)
                    for kk in range(2):
                        k = 2 * w + kk
                        last = products([ps[:, 2, :], ps[:, 3, :]], w, kk, x_hi[:, s, k, :], x_lo[:, s, k, :], k == 0, k == KT - 1)
                    last.then_inc(used[w], 1)

            def down(n):
                pe.wait_ge(g_lo_done, 1 + n + 1)
                pe.wait_ge(y_ready, 1 + n)
                for w in DOWN:
                    pe.wait_ge(w_lo_done[w], n + 1)
                    for kk in range(2):
                        k = 2 * (w - UP_WAVES) + kk
                        last = products([ps[:, 5, :], ps[:, 6, :]], w, kk, g_hi[:, k, :], g_lo[:, k, :], k == 0, k == FT - 1)
                    last.then_inc(used[w], 1)

            turn_x(0, 0, 0)
            turn_x(1, 1, 0)
            up(0, 0)
            with pe.Fori(0, NE // RING - 1) as i:
                for s in (1, 0):
                    n = RING * i + 2 - s
                    turn_x(n + 1, 1 - s, i + 1)
                    turn_g(n - 1)
                    up(n, s)
                    down(n - 1)
            turn_g(NE - 2)
            up(NE - 1, 1)
            down(NE - 2)
            turn_g(NE - 1)
            down(NE - 1)


def overflow(nc, c, ps, w1, w3, w2, h2_rows, y_rows, gather_src, scatter_dst, over_expert):
    with ExitStack() as ctx:
        def sb(name, shape, dt=F32):
            return ctx.enter_context(nc.sbuf_tensor(name, shape, dt))

        def sem(name):
            return ctx.enter_context(nc.semaphore(name))

        w1_sb = sb("over_w1", [P, KT, FF])
        w3_sb = sb("over_w3", [P, KT, FF])
        w2_sb = sb("over_w2", [P, FT, D])
        index = sb("over_index", [P, 2], I32)
        x_rows = sb("over_x", [P, D])
        x_t = sb("over_x_t", [P, KT, P])
        act_up = sb("over_act_up", [P, FF])
        g_tok = sb("over_g", [P, FF])
        g_t = sb("over_g_t", [P, FT, P])
        y_out = sb("over_y", [P, D])
        loaded = sem("over_loaded")
        held = sem("over_held")
        indexed = sem("over_indexed")
        gathered = sem("over_gathered")
        x_turned = sem("over_x_turned")
        x_ready = sem("over_x_ready")
        up_done = sem("over_up_done")
        silu_done = sem("over_silu_done")
        g_done = sem("over_g_done")
        g_turned = sem("over_g_turned")
        g_ready = sem("over_g_ready")
        down_done = sem("over_down_done")
        y_ready = sem("over_y_ready")
        scattered = sem("over_scattered")
        w1_rows = w1.rearrange("e (k p) f -> e p k f", p=P)
        w3_rows = w3.rearrange("e (k p) f -> e p k f", p=P)
        w2_rows = w2.rearrange("e (k p) f -> e p k f", p=P)
        block = ctx.enter_context(nc.Block())

        def each(eng, body):
            blocks = eng.value_load(over_expert[0:1, MAX_OVER:MAX_OVER + 1], min_val=0, max_val=MAX_OVER)
            with eng.If(blocks > 0):
                with eng.Fori(0, MAX_OVER) as b:
                    with eng.If(b < blocks):
                        body(b)

        @block.sync
        def _(sp):
            def body(b):
                e = sp.value_load(over_expert[0:1, ds(b, 1)], min_val=0, max_val=NE - 1)
                sp.wait_ge(down_done, 1 + b)
                for dst, src in ((w1_sb, w1_rows), (w3_sb, w3_rows), (w2_sb, w2_rows)):
                    sp.dma_start(dst[:, :, :], src[ds(e, 1)].rearrange("e p k f -> p (e k) f")).then_inc(loaded, DMA)

            each(sp, body)

        @block.gpsimd
        def _(pool):
            def body(b):
                pool.tensor_copy(index[:, 0:1], gather_src[:, ds(NE + b, 1)])
                pool.tensor_copy(index[:, 1:2], scatter_dst[:, ds(NE + b, 1)]).then_inc(indexed, 1)
                pool.wait_ge(indexed, b + 1)
                pool.sem_inc(held, 1)
                pool.indirect_dma_start(out=x_rows[:, :], out_offset=None, in_=h2_rows,
                                        in_offset=bass.IndirectOffsetOnAxis(ap=index[:, 0:1], axis=0)).then_inc(gathered, DMA)
                pool.wait_ge(y_ready, 1 + b + 1)
                pool.sem_inc(held, 1)
                pool.indirect_dma_start(out=y_rows, out_offset=bass.IndirectOffsetOnAxis(ap=index[:, 1:2], axis=0),
                                        in_=y_out[:, :], in_offset=None).then_inc(scattered, DMA)
                pool.wait_ge(scattered, DMA * b + DMA)

            each(pool, body)

        @block.scalar
        def _(act):
            def body(b):
                act.wait_ge(x_turned, b + 1)
                act.activation(x_t[:, :, :].rearrange("p k t -> p (k t)"), banks(ps, 0, 2), ACT.Copy).then_inc(x_ready, 1)
                act.wait_ge(up_done, b + 1)
                act.activation(act_up[:, :], ps[:, 2, :], ACT.Silu).then_inc(silu_done, 1)

            each(act, body)

        @block.vector
        def _(dve):
            dve.sem_inc(y_ready, 1)

            def body(b):
                dve.wait_ge(silu_done, b + 1)
                dve.tensor_tensor(g_tok[:, :], ps[:, 3, :], act_up[:, :], ALU.mult).then_inc(g_done, 1)
                dve.wait_ge(g_turned, b + 1)
                dve.tensor_copy(g_t[:, :, :].rearrange("p k t -> p (k t)"), ps[:, 4, :]).then_inc(g_ready, 1)
                dve.wait_ge(down_done, 1 + b + 1)
                dve.tensor_copy(y_out[:, :], banks(ps, 5, 2)).then_inc(y_ready, 1)

            each(dve, body)

        @block.tensor
        def _(pe):
            pe.sem_inc(down_done, 1)

            def body(b):
                pe.wait_ge(gathered, DMA * b + DMA)
                for k in range(KT):
                    last = pe.transpose(ps[:, k // 4, (k % 4) * P:(k % 4 + 1) * P], x_rows[:, k * P:(k + 1) * P], c.ident[:, :])
                last.then_inc(x_turned, 1)
                pe.wait_ge(x_ready, b + 1)
                pe.wait_ge(loaded, 3 * DMA * b + 3 * DMA)
                for n, w in ((2, w1_sb), (3, w3_sb)):
                    for k in range(KT):
                        last = pe.matmul(ps[:, n, :], x_t[:, k, :], w[:, k, :], start=k == 0, stop=k == KT - 1)
                last.then_inc(up_done, 1)
                pe.wait_ge(g_done, b + 1)
                for k in range(FT):
                    last = pe.transpose(ps[:, 4, k * P:(k + 1) * P], g_tok[:, k * P:(k + 1) * P], c.ident[:, :])
                last.then_inc(g_turned, 1)
                pe.wait_ge(g_ready, b + 1)
                pe.wait_ge(y_ready, 1 + b)
                for k in range(FT):
                    for h in range(2):
                        last = pe.matmul(ps[:, 5 + h, :], g_t[:, k, :], w2_sb[:, k, h * HALF:(h + 1) * HALF],
                                         start=k == 0, stop=k == FT - 1)
                last.then_inc(down_done, 1)

            each(pe, body)


def finish(nc, x2, gates, y_rows, gain, out):
    with ExitStack() as ctx:
        def sb(name, shape, dt=F32):
            return ctx.enter_context(nc.sbuf_tensor(name, shape, dt))

        def sem(name):
            return ctx.enter_context(nc.semaphore(name))

        gain_row = sb("final_row", [P, D])
        y_tile = sb("y_tile", [P, RING, TOPK, D])
        total = sb("total", [P, RING, D])
        squares = sb("final_squares", [P, D])
        sum_sq = sb("final_sum", [P, TT])
        mean_sq = sb("final_mean", [P, TT])
        root = sb("final_root", [P, TT])
        rstd = sb("final_rstd", [P, TT])
        result = sb("result", [P, RING, D])
        gain_loaded = sem("final_gain_loaded")
        y_loaded = [sem(f"y_loaded{s}") for s in range(RING)]
        first_added = sem("first_added")
        summed = sem("final_summed")
        squared = sem("final_squared")
        mean_done = sem("final_mean_done")
        root_done = sem("final_root_done")
        rstd_done = sem("final_rstd_done")
        scaled = sem("final_scaled")
        stored = [sem(f"out_stored{s}") for s in range(RING)]
        y_tiles = y_rows[0:TOPK * SEQ].rearrange("(k t p) d -> t p k d", k=TOPK, p=P)
        out_tiles = out[0].rearrange("(t p) d -> t p d", p=P)
        block = ctx.enter_context(nc.Block())

        @block.sync
        def _(sp):
            sp.dma_start(gain_row[:, :], gain.rearrange("(a d) -> a d", a=1).to_broadcast([P, D])).then_inc(gain_loaded, DMA)
            with sp.Fori(0, TT // RING) as i:
                for s in range(RING):
                    sp.wait_ge(summed, RING * i + s + 1)
                    sp.dma_start(y_tile[:, s, :, :], y_tiles[ds(RING * i + s, 1)].rearrange("a p k d -> p (a k) d")).then_inc(y_loaded[s], DMA)

        @block.scalar
        def _(act):
            act.sem_inc(squared, RING)
            for s in range(RING):
                act.sem_inc(stored[s], DMA)
            with act.Fori(0, TT // RING) as i:
                for s in range(RING):
                    t = RING * i + s
                    act.wait_ge(summed, RING + t + 1)
                    act.wait_ge(squared, RING + t)
                    act.activation(squares[:, :], total[:, s, :], ACT.Square, accum_out=sum_sq[:, ds(t, 1)]).then_inc(squared, 1)
                    act.wait_ge(mean_done, t + 1)
                    act.activation(root[:, ds(t, 1)], mean_sq[:, ds(t, 1)], ACT.Sqrt).then_inc(root_done, 1)
                    act.wait_ge(scaled, t + 1)
                    act.dma_start(out_tiles[ds(t, 1)].rearrange("a p d -> p (a d)"), result[:, s, :]).then_inc(stored[s], DMA)
            for s in range(RING):
                act.wait_ge(stored[s], DMA * (TT // RING) + DMA)

        @block.vector
        def _(dve):
            dve.sem_inc(summed, RING)
            dve.wait_ge(gain_loaded, DMA)
            with dve.Fori(0, TT // RING) as i:
                for s in range(RING):
                    t = RING * i + s
                    dve.wait_ge(y_loaded[s], DMA * i + DMA)
                    dve.scalar_tensor_tensor(out=total[:, s, :], in0=y_tile[:, s, 0, :], scalar=gates[:, 0, ds(t, 1)],
                                             in1=x2[:, ds(t, 1), :].rearrange("p a d -> p (a d)"), op0=ALU.mult,
                                             op1=ALU.add).then_inc(first_added, 1)
                    dve.wait_ge(first_added, t + 1)
                    dve.scalar_tensor_tensor(out=total[:, s, :], in0=y_tile[:, s, 1, :], scalar=gates[:, 1, ds(t, 1)],
                                             in1=total[:, s, :], op0=ALU.mult, op1=ALU.add).then_inc(summed, 1)
                for s in range(RING):
                    t = RING * i + s
                    dve.wait_ge(squared, RING + t + 1)
                    dve.tensor_scalar(mean_sq[:, ds(t, 1)], sum_sq[:, ds(t, 1)], 1.0 / D, EPS, ALU.mult, ALU.add).then_inc(mean_done, 1)
                    dve.wait_ge(root_done, t + 1)
                    dve.reciprocal(rstd[:, ds(t, 1)], root[:, ds(t, 1)]).then_inc(rstd_done, 1)
                    dve.wait_ge(rstd_done, t + 1)
                    dve.wait_ge(stored[s], DMA * i + DMA)
                    dve.scalar_tensor_tensor(out=result[:, s, :], in0=total[:, s, :], scalar=rstd[:, ds(t, 1)], in1=gain_row[:, :],
                                             op0=ALU.mult, op1=ALU.mult).then_inc(scaled, 1)


def clear_semaphores(nc):
    used = sorted(nc.released_uncleared_semaphores)
    nc.gpsimd.sem_clear(range(used[0], used[-1] + 1))
    nc.all_engine_barrier()


def load_taps(nc, conv_w, conv_b, taps, bias):
    with ExitStack() as ctx:
        loaded = ctx.enter_context(nc.semaphore("taps_loaded"))
        block = ctx.enter_context(nc.Block())

        @block.sync
        def _(sp):
            with nc.allow_non_contiguous_dma(reason="five numbers a channel"):
                for j in range(CONV):
                    sp.dma_start(taps[:, j, :], conv_w[0][j].rearrange("(b p) -> p b", p=P)).then_inc(loaded, DMA)
                sp.dma_start(bias[:, :], conv_b[0].rearrange("(b p) -> p b", p=P)).then_inc(loaded, DMA)
            sp.wait_ge(loaded, (CONV + 1) * DMA)


def trunk(nc, x, norm_mix_g, w_in, b_f, conv_w, conv_b, dt_bias, a_log, d_skip, ssd_norm_g, w_br_attn, w_br_ssd,
          w_out, norm_ffn_g, w_group_router, b_group_router, w_expert_router, b_expert_router, w1, w3, w2, final_g, out):
    with ExitStack() as ctx:
        def sb(name, shape, dt=F32):
            return ctx.enter_context(nc.sbuf_tensor(name, shape, dt))

        def dram(name, shape, dt=F32):
            return nc.dram_tensor(name, shape, dt, kind="Internal").ap()

        ps = ctx.enter_context(nc.psum_tensor("ps", [P, 8, HALF], F32))
        c = Constants(ident=sb("ident", [P, P]), ident_bf=sb("ident_bf", [P, P], BF16), ones=sb("ones", [P, P]),
                            tri=sb("tri", [P, P]), tri_after=sb("tri_after", [P, P]), tri_before=sb("tri_before", [P, P]),
                            causal_bf=sb("causal_bf", [P, P], BF16))
        dt_tok = sb("dt_tok", [P, TT, SSD_HEADS])
        a_tok = sb("a_tok", [P, TT, SSD_HEADS])
        gates = sb("gates", [P, TOPK, TT])
        logits = sb("logits", [P, TT, N_GROUPS + NE])
        gather_src = sb("gather_src", [P, BLOCKS], I32)
        scatter_dst = sb("scatter_dst", [P, BLOCKS], I32)
        over_expert = sb("over_expert", [P, MAX_OVER + 1], I32)
        f_rows = dram("f_rows", (HEADS, SEQ))
        silu_z = dram("silu_z", (XB, P, SEQ))
        gate_rows = dram("gate_rows", (2 * KT, P, SEQ))
        h2_rows = dram("h2_rows", (SEQ, D))
        y_rows = dram("y_rows", (TOPK * SEQ + BLOCKS * P, D))
        slot_table = dram("slot_table", (BLOCKS * P, 1), I32)
        make_constants(nc, c)

        held_at = region(nc, ctx, "held", TT * D * 4)
        size = (D_ATTN // P) * SEQ * 4
        ya_hi = nc.alloc_sbuf_tensor_at("ya_hi", [P, D_ATTN // P, SEQ], F32R, offset=held_at)
        ya_lo = nc.alloc_sbuf_tensor_at("ya_lo", [P, D_ATTN // P, SEQ], F32R, offset=held_at + size)
        x2 = nc.alloc_sbuf_tensor_at("x2", [P, TT, D], F32, offset=held_at)
        with ExitStack() as mixer:
            xbc = mixer.enter_context(nc.sbuf_tensor("xbc", [P, CB, SEQ], F32))
            gated = xbc[:, 0:XB, :]
            merged = xbc[:, 0:KT, :]
            with ExitStack() as proj:
                h_hi = proj.enter_context(nc.sbuf_tensor("h_hi", [P, KT, SEQ], F32R))
                h_lo = proj.enter_context(nc.sbuf_tensor("h_lo", [P, KT, SEQ], F32R))
                taps = proj.enter_context(nc.sbuf_tensor("taps", [P, CONV, CB], F32))
                bias = proj.enter_context(nc.sbuf_tensor("conv_bias", [P, CB], F32))
                normalise_input(nc, c, ps, x, norm_mix_g, h_hi, h_lo)
                load_taps(nc, conv_w, conv_b, taps, bias)
                decays(nc, c, ps, w_in[0], b_f, dt_bias, a_log, h_hi, h_lo, f_rows, dt_tok, a_tok)
                project(nc, ps, w_in[0], [(COL_Q, CB, "keep", xbc)], h_hi, h_lo, taps, bias)
                attention(nc, c, ps, xbc, f_rows, ya_hi, ya_lo)
                project(nc, ps, w_in[0], [(COL_Z, XB, "silu", silu_z), (COL_GA, 2 * KT, "sigmoid", gate_rows),
                                          (COL_XBC, CB, "conv", xbc)], h_hi, h_lo, taps, bias)
            with ExitStack() as branch:
                square_sum = branch.enter_context(nc.sbuf_tensor("square_sum", [P, SEQ], F32))
                weights = BranchWeights(nc, branch, w_br_attn[0], w_br_ssd[0])
                state_space(nc, c, ps, xbc, dt_tok, a_tok, d_skip, silu_z, gated, square_sum, weights.load_first)
                merge(nc, c, ps, weights, gate_rows, gated, square_sum, ssd_norm_g, ya_hi, ya_lo, merged)
            project_out(nc, ps, w_out[0], x, merged, x2)
        clear_semaphores(nc)
        with ExitStack() as moe:
            weights = ExpertWeights(nc, moe, w1[0], w3[0], w2[0])
            router_logits(nc, c, ps, x2, norm_ffn_g, w_group_router[0], b_group_router, w_expert_router[0],
                          b_expert_router, h2_rows, logits, weights)
            route(nc, c, ps, logits, gates, slot_table, gather_src, scatter_dst, over_expert)
            experts(nc, c, ps, weights, h2_rows, y_rows, gather_src, scatter_dst)
        overflow(nc, c, ps, w1[0], w3[0], w2[0], h2_rows, y_rows, gather_src, scatter_dst, over_expert)
        finish(nc, x2, gates, y_rows, final_g, out)


_INS = ["x", "norm_mix_g", "w_in", "b_f", "conv_w", "conv_b", "dt_bias", "a_log", "d_skip", "ssd_norm_g", "w_br_attn",
        "w_br_ssd", "w_out", "norm_ffn_g", "w_group_router", "b_group_router", "w_expert_router", "b_expert_router",
        "w1", "w3", "w2", "final_g"]


def kernel(**inputs):
    import numpy as np
    import concourse.bacc as bacc
    from concourse.bass_utils import run_bass_kernel_spmd

    nc = bacc.Bacc("TRN2", target_bir_lowering=False, num_devices=1)
    arrays, args = {}, []
    for name in _INS:
        a = np.ascontiguousarray(inputs[name])
        arrays[f"in_{name}"] = a
        args.append(nc.dram_tensor(f"in_{name}", a.shape, mybir.dt.from_np(a.dtype), kind="ExternalInput").ap())
    args.append(nc.dram_tensor("result_dram", (1, SEQ, D), F32, kind="ExternalOutput").ap())
    trunk(nc, *args)
    nc.compile()
    r = run_bass_kernel_spmd(nc, [arrays], core_ids=[0])
    return r.results[0]["result_dram"]
```

```python
from collections import namedtuple
from contextlib import ExitStack

import concourse.bass as bass
from concourse import mybir

F32 = mybir.dt.float32
F32R = mybir.dt.float32r
BF16 = mybir.dt.bfloat16
I32 = mybir.dt.int32
U32 = mybir.dt.uint32
ACT = mybir.ActivationFunctionType
ALU = mybir.AluOpType
AX = mybir.AxisListType
ds = bass.ds

P = 128
SEQ = 1024
D = 1024
KT = D // P
TT = SEQ // P
HALF = 512
RING = 2
DMA = 16
EPS = 1e-6

HEADS = 8
HD = 64
D_ATTN = HEADS * HD
SSD_HEADS = 16
SSD_HD = 64
D_SSD = SSD_HEADS * SSD_HD
GROUPS = 2
STATE = 128
CONV = 4
CONV_CH = D_SSD + 2 * GROUPS * STATE
CB = CONV_CH // P
XB = D_SSD // P

COL_Q = 0
COL_F = 3 * D_ATTN
COL_Z = COL_F + HEADS
COL_XBC = COL_Z + D_SSD
COL_DT = COL_XBC + CONV_CH
COL_GA = COL_DT + SSD_HEADS
COL_GS = COL_GA + D
DT_ROW = 32
SMALL = 64

N_GROUPS = 4
PER_GROUP = 8
NE = N_GROUPS * PER_GROUP
FF = 512
FT = FF // P
TOPK = 2
SLOTS = P
MAX_OVER = SEQ * TOPK // P
BLOCKS = NE + MAX_OVER
MASKED = -1.0e30


Constants = namedtuple("Constants", "ident ident_bf ones tri tri_after tri_before causal_bf")


def region(nc, ctx, name, size):
    at = (nc.sbuf_base + 31) // 32 * 32
    ctx.enter_context(nc.sbuf_tensor(name, [P, size // 4 + 8], F32))
    return at


def spread(ap, shape, axis):
    return ap.unsqueeze(axis).to_broadcast(shape)


class Places:

    def __init__(self, nc, at):
        self.nc, self.at = nc, at

    def sb(self, name, shape, dt=F32):
        size = 4
        for extent in shape[1:]:
            size *= extent
        tensor = self.nc.alloc_sbuf_tensor_at(name, shape, dt, offset=self.at)
        self.at += (size + 31) // 32 * 32
        return tensor


def banks(ps, first, n):
    return ps[:, first:first + n, :].rearrange("p b c -> p (b c)")


def make_constants(nc, c):
    with ExitStack() as ctx:
        made = ctx.enter_context(nc.semaphore("const_filled"))
        selected = ctx.enter_context(nc.semaphore("const_selected"))
        block = ctx.enter_context(nc.Block())

        @block.gpsimd
        def _(pool):
            pool.memset(c.ident[:, :], 0.0)
            pool.memset(c.ident_bf[:, :], 0.0)
            pool.memset(c.ones[:, :], 1.0)
            pool.memset(c.tri[:, :], 1.0)
            pool.memset(c.tri_after[:, :], 1.0)
            pool.memset(c.tri_before[:, :], 1.0)
            pool.memset(c.causal_bf[:, :], 0.0).then_inc(made, 1)
            pool.wait_ge(made, 1)
            for m in (c.ident, c.ident_bf):
                pool.affine_select(out=m[:, :], in_=m[:, :], compare_op=ALU.not_equal, fill=1.0,
                                   base=0, pattern=[[-1, P]], channel_multiplier=1)
            pool.affine_select(out=c.tri[:, :], in_=c.tri[:, :], compare_op=ALU.is_ge, fill=0.0,
                               base=0, pattern=[[1, P]], channel_multiplier=-1)
            pool.affine_select(out=c.tri_after[:, :], in_=c.tri_after[:, :], compare_op=ALU.is_ge,
                               fill=0.0, base=-1, pattern=[[-1, P]], channel_multiplier=1)
            pool.affine_select(out=c.tri_before[:, :], in_=c.tri_before[:, :], compare_op=ALU.is_ge,
                               fill=0.0, base=-1, pattern=[[1, P]], channel_multiplier=-1)
            pool.affine_select(out=c.causal_bf[:, :], in_=c.causal_bf[:, :], compare_op=ALU.is_ge,
                               fill=MASKED, base=0, pattern=[[-1, P]],
                               channel_multiplier=1).then_inc(selected, 1)
            pool.wait_ge(selected, 1)


def normalise_input(nc, c, ps, x, gain, h_hi, h_lo, at):
    LOADS = 4
    with ExitStack() as ctx:
        sb = Places(nc, at).sb

        def sem(name):
            return ctx.enter_context(nc.semaphore(name))

        x_all = sb("x_all", [P, TT, D])
        gain_row = sb("gain_row", [P, D])
        squares = sb("squares", [P, D])
        sum_sq = sb("sum_sq", [P, TT])
        mean_sq = sb("mean_sq", [P, TT])
        root = sb("root", [P, TT])
        rstd = sb("rstd", [P, TT])
        xn = sb("xn", [P, RING, D])
        x_loaded = [sem(f"x_loaded{n}") for n in range(LOADS)]
        gain_loaded = sem("gain_loaded")
        squared = sem("squared")
        mean_done = sem("mean_done")
        root_done = sem("root_done")
        rstd_done = sem("rstd_done")
        odd_scaled = sem("odd_scaled")
        xn_done = [sem(f"xn_done{s}") for s in range(RING)]
        transposed = sem("transposed")
        hi_done = sem("hi_done")
        lo_done = sem("lo_done")
        per = TT // LOADS
        x_tiles = x[0].rearrange("(t p) d -> p t d", p=P)
        block = ctx.enter_context(nc.Block())

        def turned(t):
            return banks(ps, 2 * (t % 4), 2).rearrange("p (k t) -> p k t", k=KT), slice(t * P, (t + 1) * P)

        def scale(eng, t):
            eng.wait_ge(gain_loaded, DMA)
            eng.wait_ge(rstd_done, t // per + 1)
            if t >= RING:
                eng.wait_ge(transposed, t - RING + 1)
            eng.scalar_tensor_tensor(out=xn[:, t % RING, :], in0=x_all[:, t, :], scalar=rstd[:, t:t + 1], in1=gain_row[:, :],
                                     op0=ALU.mult, op1=ALU.mult).then_inc(xn_done[t % RING], 1)

        @block.sync
        def _(sp):
            for n in range(LOADS):
                rows = slice(n * per, (n + 1) * per)
                sp.dma_start(x_all[:, rows, :], x_tiles[:, rows, :]).then_inc(x_loaded[n], DMA)
                if n == 0:
                    sp.dma_start(gain_row[:, :], gain.to_broadcast([P, D])).then_inc(gain_loaded, DMA)

        @block.scalar
        def _(act):
            def high(t):
                src, dst = turned(t)
                act.wait_ge(transposed, t + 1)
                act.activation(h_hi[:, :, dst], src, ACT.Copy).then_inc(hi_done, 1)

            for n in range(LOADS):
                act.wait_ge(x_loaded[n], DMA)
                for t in range(n * per, (n + 1) * per):
                    if t > 0:
                        act.wait_ge(squared, t)
                    act.activation(squares[:, :], x_all[:, t, :], ACT.Square, accum_out=sum_sq[:, t:t + 1]).then_inc(squared, 1)
                act.wait_ge(mean_done, n + 1)
                cols = slice(n * per, (n + 1) * per)
                act.activation(root[:, cols], mean_sq[:, cols], ACT.Sqrt).then_inc(root_done, 1)
                act.wait_ge(rstd_done, n + 1)
                t = 2 * n + 1
                if t > RING:
                    act.wait_ge(transposed, t - RING + 1)
                act.activation(xn[:, t % RING, :], x_all[:, t, :], ACT.Copy, scale=rstd[:, t:t + 1]).then_inc(odd_scaled, 1)
                if n > 0:
                    high(n - 1)
            for t in range(LOADS - 1, TT):
                high(t)

        @block.gpsimd
        def _(pool):
            pool.wait_ge(gain_loaded, DMA)
            for t in range(1, TT, 2):
                pool.wait_ge(odd_scaled, t // 2 + 1)
                pool.tensor_tensor(xn[:, t % RING, :], xn[:, t % RING, :], gain_row[:, :], ALU.mult).then_inc(xn_done[t % RING], 1)

        @block.vector
        def _(dve):
            def stats(n):
                cols = slice(n * per, (n + 1) * per)
                dve.wait_ge(squared, (n + 1) * per)
                dve.tensor_scalar(mean_sq[:, cols], sum_sq[:, cols], 1.0 / D, EPS, ALU.mult, ALU.add).then_inc(mean_done, 1)
                dve.wait_ge(root_done, n + 1)
                dve.reciprocal(rstd[:, cols], root[:, cols]).then_inc(rstd_done, 1)

            def rest(t):
                src, dst = turned(t)
                dve.wait_ge(hi_done, t + 1)
                dve.tensor_tensor(h_lo[:, :, dst], src, h_hi[:, :, dst].bitcast(F32), ALU.subtract).then_inc(lo_done, 1)

            for n in range(LOADS):
                stats(n)
                scale(dve, 2 * n)
                if n > 0:
                    rest(n - 1)
            for t in range(LOADS - 1, TT):
                rest(t)

        @block.tensor
        def _(pe):
            for t in range(TT):
                pe.wait_ge(xn_done[t % RING], t // RING + 1)
                if t >= 4:
                    pe.wait_ge(lo_done, t - 3)
                for k in range(KT):
                    last = pe.transpose(banks(ps, 2 * (t % 4), 2)[:, k * P:(k + 1) * P], xn[:, t % RING, k * P:(k + 1) * P],
                                        c.ident[:, :])
                last.then_inc(transposed, 1)


def three_passes(pe, out, w_hi, w_lo, h_hi, h_lo, first, last):
    for a, b, opens, closes in ((w_hi, h_hi, first, False), (w_hi, h_lo, False, False), (w_lo, h_hi, False, last)):
        for n in range(len(out)):
            ins = pe.matmul(out[n], a, b[n], start=opens, stop=closes)
    return ins


class Decays:

    def __init__(self, nc, ctx, at, w_in, b_f, dt_bias, a_log, f_rows, dt_tok, a_tok):
        sb = Places(nc, at).sb

        def sem(name):
            return ctx.enter_context(nc.semaphore(name))

        self.nc = nc
        self.b_f, self.dt_bias, self.a_log = b_f, dt_bias, a_log
        self.f_rows, self.dt_tok, self.a_tok = f_rows, dt_tok, a_tok
        self.w_cols = w_in.rearrange("(k p) c -> p k c", p=P)
        self.dt_rows = slice(DT_ROW, DT_ROW + SSD_HEADS)
        self.w_raw = sb("small_raw", [P, KT, P])
        self.w_hi = sb("small_hi", [P, KT, P], F32R)
        self.w_lo = sb("small_lo", [P, KT, P], F32R)
        self.sign = sb("small_sign", [SMALL, 1])
        self.bias = sb("small_bias", [SMALL, 1])
        self.bias_signed = sb("small_bias_signed", [SMALL, 1])
        self.a_rate = sb("a_rate", [P, SSD_HEADS])
        self.a_exp = sb("a_exp", [P, SSD_HEADS])
        self.arg = sb("softplus_arg", [SMALL, SEQ])
        self.log = sb("softplus_log", [SMALL, SEQ])
        self.soft = sb("softplus", [SMALL, SEQ])
        self.one_row = sb("one_row", [HEADS, SEQ])
        self.neg_f = sb("neg_f", [HEADS, SEQ])
        self.cleared = sem("small_cleared")
        self.loaded = sem("small_loaded")
        self.a_loaded = sem("a_loaded")
        self.hi_done = sem("small_hi_done")
        self.lo_done = sem("small_lo_done")
        self.projected = sem("small_projected")
        self.vec = sem("decays_vec")
        self.abs_done = sem("softplus_abs_done")
        self.expd_done = sem("softplus_exp_done")
        self.log_done = sem("softplus_log_done")
        self.a_exp_done = sem("a_exp_done")
        self.transposed = sem("dt_transposed")
        self.stored = sem("f_rows_stored")

    def gpsimd(self, pool):
        pool.memset(self.w_raw[:, :, :], 0.0)
        pool.memset(self.sign[:, :], 1.0)
        pool.memset(self.bias[:, :], 0.0)
        pool.memset(self.one_row[:, :], 1.0).then_inc(self.cleared, 1)
        pool.wait_ge(self.cleared, 1)
        pool.memset(self.sign[0:HEADS, :], -1.0).then_inc(self.cleared, 1)
        pool.wait_ge(self.hi_done, 1)
        pool.tensor_tensor(self.w_lo[:, :, :], self.w_raw[:, :, :], self.w_hi[:, :, :].bitcast(F32),
                           ALU.subtract).then_inc(self.lo_done, 1)

    def load(self, sp):
        sp.dma_start(self.a_rate[:, :], self.a_log.to_broadcast([P, SSD_HEADS])).then_inc(self.a_loaded, DMA)
        sp.wait_ge(self.cleared, 2)
        with self.nc.allow_non_contiguous_dma(reason="a few narrow columns"):
            sp.dma_start(self.w_raw[:, :, 0:HEADS], self.w_cols[:, :, COL_F:COL_F + HEADS]).then_inc(self.loaded, DMA)
            sp.dma_start(self.w_raw[:, :, self.dt_rows], self.w_cols[:, :, COL_DT:COL_DT + SSD_HEADS]).then_inc(self.loaded, DMA)
            sp.dma_start(self.bias[0:HEADS, :], self.b_f.rearrange("a h -> h a")).then_inc(self.loaded, DMA)
            sp.dma_start(self.bias[self.dt_rows, :], self.dt_bias.rearrange("a h -> h a")).then_inc(self.loaded, DMA)

    def store(self, sp):
        sp.wait_ge(self.vec, 4)
        sp.dma_start(self.f_rows, self.neg_f[:, :]).then_inc(self.stored, DMA)
        sp.wait_ge(self.stored, DMA)

    def high(self, act):
        act.wait_ge(self.loaded, 4 * DMA)
        act.activation(self.w_hi[:, :, :], self.w_raw[:, :, :], ACT.Copy).then_inc(self.hi_done, 1)

    def softplus(self, act):
        act.wait_ge(self.a_loaded, DMA)
        act.activation(self.a_exp[:, :], self.a_rate[:, :], ACT.Exp).then_inc(self.a_exp_done, 1)
        act.wait_ge(self.vec, 2)
        act.activation(self.log[:, :], self.arg[:, :], ACT.Abs).then_inc(self.abs_done, 1)
        act.wait_ge(self.abs_done, 1)
        act.activation(self.log[:, :], self.log[:, :], ACT.Exp, scale=-1.0).then_inc(self.expd_done, 1)
        act.wait_ge(self.expd_done, 1)
        act.activation(self.log[:, :], self.log[:, :], ACT.Ln, bias=1.0).then_inc(self.log_done, 1)

    def product(self, pe, ps, h_hi, h_lo):
        pe.wait_ge(self.lo_done, 1)
        for k in range(KT):
            last = three_passes(pe, [ps[:, 4, :], ps[:, 5, :]], self.w_hi[:, k, :], self.w_lo[:, k, :],
                                [h_hi[:, k, 0:HALF], h_hi[:, k, HALF:SEQ]],
                                [h_lo[:, k, 0:HALF], h_lo[:, k, HALF:SEQ]], k == 0, k == KT - 1)
        last.then_inc(self.projected, 1)

    def turn(self, pe, ps, ident):
        pe.wait_ge(self.vec, 3)
        for t in range(TT):
            last = pe.transpose(ps[:, 6, t * SMALL:(t + 1) * SMALL], self.soft[:, t * P:(t + 1) * P], ident[0:SMALL, 0:SMALL])
        last.then_inc(self.transposed, 1)

    def sums(self, dve, ps):
        vec = self.vec
        dve.wait_ge(self.loaded, 4 * DMA)
        dve.tensor_tensor(self.bias_signed[:, :], self.bias[:, :], self.sign[:, :], ALU.mult).then_inc(vec, 1)
        dve.wait_ge(vec, 1)
        dve.wait_ge(self.projected, 1)
        dve.tensor_scalar(self.arg[:, :], banks(ps, 4, 2)[0:SMALL, :], self.sign[:, :], self.bias_signed[:, :],
                          ALU.mult, ALU.add).then_inc(vec, 1)
        dve.wait_ge(vec, 2)
        dve.wait_ge(self.log_done, 1)
        dve.scalar_tensor_tensor(out=self.soft[:, :], in0=self.arg[:, :], scalar=0.0, in1=self.log[:, :],
                                 op0=ALU.max, op1=ALU.add).then_inc(vec, 1)
        dve.wait_ge(vec, 3)
        dve.tensor_tensor_scan(self.neg_f[:, :], self.one_row[:, :], self.soft[0:HEADS, :], 0.0,
                               ALU.mult, ALU.add).then_inc(vec, 1)

    def tokens(self, dve, ps):
        dve.wait_ge(self.transposed, 1)
        dve.tensor_copy(self.dt_tok[:, :, :], ps[:, 6, :].rearrange("p (t r) -> p t r", t=TT)[:, :, self.dt_rows]).then_inc(self.vec, 1)
        dve.wait_ge(self.vec, 5)
        dve.wait_ge(self.a_exp_done, 1)
        for t in range(TT):
            dve.scalar_tensor_tensor(out=self.a_tok[:, t, :], in0=self.dt_tok[:, t, :], scalar=-1.0, in1=self.a_exp[:, :],
                                     op0=ALU.mult, op1=ALU.mult)


def project(nc, c, ps, w_in, parts, h_hi, h_lo, at, conv, small):
    total = sum(blocks for _, blocks, _, _ in parts)
    firsts = [sum(blocks for _, blocks, _, _ in parts[:k]) for k in range(len(parts))]
    n_kept = sum(blocks for _, blocks, kind, _ in parts if kind == "keep")
    n_staged = sum(blocks for _, blocks, kind, _ in parts if kind in ("silu", "sigmoid"))
    with ExitStack() as ctx:
        def sb(name, shape, dt=F32):
            return ctx.enter_context(nc.sbuf_tensor(name, shape, dt))

        def sem(name):
            return ctx.enter_context(nc.semaphore(name))

        held = Places(nc, at)
        w_raw = held.sb("w_raw", [P, RING, KT, P])
        w_hi = held.sb("w_hi", [P, RING, KT, P], F32R)
        w_lo = held.sb("w_lo", [P, RING, KT, P], F32R)
        mixed = held.sb("mixed", [P, RING, SEQ])
        w_loaded = [sem(f"w_loaded{s}") for s in range(RING)]
        w_hi_done = sem("w_hi_done")
        w_lo_done = sem("w_lo_done")
        projected = sem("projected")
        read_out = sem("read_out")
        taps = sb("taps", [P, CONV, CB])
        bias = sb("conv_bias", [P, CB])
        padded = sb("padded", [P, RING, CONV - 1 + SEQ])
        stage = padded[:, :, CONV - 1:]
        taps_loaded = sem("taps_loaded")
        pad_done = sem("pad_done")
        tap_done = sem("tap_done")
        conv_done = sem("conv_done")
        silu_done = sem("silu_done")
        stored = [sem(f"stored{s}") for s in range(RING)]
        w_cols = w_in.rearrange("(k p) c -> p k c", p=P)
        decays = small(ctx)
        block = ctx.enter_context(nc.Block())

        def flat(t, n):
            return t[:, ds(n, 1), :].rearrange("p a t -> p (a t)")

        @block.sync
        def _(sp):
            decays.load(sp)
            for (col, blocks, _, _), first in zip(parts, firsts):
                with sp.Fori(0, blocks // RING) as i:
                    for s in range(RING):
                        sp.wait_ge(w_lo_done, first + RING * i + s + 1)
                        sp.dma_start(w_raw[:, s, :, :], w_cols[:, :, ds(col + RING * P * i + s * P, P)]).then_inc(w_loaded[s], DMA)
                if first == 0:
                    decays.store(sp)
                    with nc.allow_non_contiguous_dma(reason="five numbers a channel"):
                        for j in range(CONV):
                            sp.dma_start(taps[:, j, :], conv[0][j].rearrange("(b p) -> p b", p=P)).then_inc(taps_loaded, DMA)
                        sp.dma_start(bias[:, :], conv[1].rearrange("(b p) -> p b", p=P)).then_inc(taps_loaded, DMA)

        @block.gpsimd
        def _(pool):
            pool.sem_inc(w_lo_done, RING)
            pool.memset(padded[:, :, 0:CONV - 1], 0.0).then_inc(pad_done, 1)
            decays.gpsimd(pool)
            with pool.Fori(0, total // RING) as i:
                for s in range(RING):
                    pool.wait_ge(w_hi_done, RING * i + s + 1)
                    pool.tensor_tensor(w_lo[:, s, :, :], w_raw[:, s, :, :], w_hi[:, s, :, :].bitcast(F32),
                                       ALU.subtract).then_inc(w_lo_done, 1)

        @block.tensor
        def _(pe):
            pe.sem_inc(projected, RING)

            def product(n, s):
                pe.wait_ge(w_lo_done, RING + n + 1)
                pe.wait_ge(read_out, n + 1)
                for k in range(KT):
                    last = three_passes(pe, [ps[:, 2 * s, :], ps[:, 2 * s + 1, :]], w_hi[:, s, k, :], w_lo[:, s, k, :],
                                        [h_hi[:, k, 0:HALF], h_hi[:, k, HALF:SEQ]],
                                        [h_lo[:, k, 0:HALF], h_lo[:, k, HALF:SEQ]], k == 0, k == KT - 1)
                last.then_inc(projected, 1)

            decays.product(pe, ps, h_hi, h_lo)
            for s in range(RING):
                product(s, s)
            decays.turn(pe, ps, c.ident)
            with pe.Fori(0, total // RING - 1) as i:
                for s in range(RING):
                    product(RING * i + RING + s, s)

        @block.scalar
        def _(act):
            def high(n, s, round_):
                act.wait_ge(w_loaded[s], DMA * round_ + DMA)
                act.wait_ge(projected, n + 1)
                act.activation(w_hi[:, s, :, :], w_raw[:, s, :, :], ACT.Copy).then_inc(w_hi_done, 1)

            def evacuate(n, s, own, kind, dest):
                act.wait_ge(projected, RING + n + 1)
                if kind == "conv":
                    act.wait_ge(conv_done, own + 1)
                    act.activation(padded[:, s, CONV - 1:], banks(ps, 2 * s, 2), ACT.Copy).then_inc(read_out, 1)
                else:
                    act.wait_ge(stored[s], (n - n_kept - s) * (DMA // RING) + DMA)
                    act.activation(stage[:, s, :], banks(ps, 2 * s, 2),
                                   ACT.Silu if kind == "silu" else ACT.Sigmoid).then_inc(read_out, 1)
                    act.wait_ge(read_out, RING + n + 1)
                    act.dma_start(dest[ds(own, 1)].rearrange("a p t -> p (a t)"), stage[:, s, :]).then_inc(stored[s], DMA)

            def silu(own, s, dest):
                act.wait_ge(conv_done, RING + own + 1)
                act.activation(flat(dest, own), mixed[:, s, :], ACT.Silu).then_inc(silu_done, 1)

            for s in range(RING):
                act.sem_inc(stored[s], DMA)
            act.sem_inc(read_out, RING)
            act.sem_inc(silu_done, RING)
            act.wait_ge(pad_done, 1)
            decays.high(act)
            high(0, 0, 0)
            high(1, 1, 0)
            decays.softplus(act)
            for (_, blocks, kind, dest), first in zip(parts, firsts):
                if first == n_kept:
                    act.wait_ge(read_out, RING + n_kept)

                def pair(i, first_pair, last_pair):
                    for s in range(RING):
                        own = RING * i + s
                        n = first + own
                        if s == 0 and not (first == 0 and first_pair):
                            high(n + 1, 1, first // RING + i)
                        if s == 1 and not last_pair:
                            high(n + 1, 0, first // RING + i + 1)
                        if kind != "keep":
                            evacuate(n, s, own, kind, dest)
                        if kind == "conv" and not (first_pair and s == 0):
                            silu(own - 1, 1 - s, dest)

                if kind == "conv":
                    for s in range(RING):
                        act.wait_ge(stored[s], DMA * (n_staged // RING) + DMA)
                pair(0, True, False)
                with act.Fori(0, blocks // RING - 2) as i:
                    pair(i + 1, False, False)
                pair(blocks // RING - 1, False, first + blocks == total)
                if kind == "conv":
                    silu(blocks - 1, 1, dest)

        @block.vector
        def _(dve):
            dve.sem_inc(conv_done, RING)
            decays.sums(dve, ps)
            for (_, blocks, kind, dest), first in zip(parts, firsts):
                if kind == "keep":
                    with dve.Fori(0, blocks // RING) as i:
                        for s in range(RING):
                            own = RING * i + s
                            dve.wait_ge(projected, RING + first + own + 1)
                            dve.tensor_copy(flat(dest, own), banks(ps, 2 * s, 2)).then_inc(read_out, 1)
                    decays.tokens(dve, ps)
                if kind == "conv":
                    dve.wait_ge(taps_loaded, (CONV + 1) * DMA)
                    with dve.Fori(0, blocks // RING) as i:
                        for s in range(RING):
                            own = RING * i + s
                            dve.wait_ge(read_out, RING + first + own + 1)
                            dve.wait_ge(silu_done, own + 1)
                            dve.tensor_scalar(mixed[:, s, :], padded[:, s, 0:SEQ], taps[:, 0, ds(own, 1)], bias[:, ds(own, 1)],
                                              ALU.mult, ALU.add).then_inc(tap_done, 1)
                            for j in range(1, CONV):
                                dve.wait_ge(tap_done, (CONV - 1) * own + j)
                                dve.scalar_tensor_tensor(out=mixed[:, s, :], in0=padded[:, s, j:j + SEQ],
                                                         scalar=taps[:, j, ds(own, 1)], in1=mixed[:, s, :], op0=ALU.mult,
                                                         op1=ALU.add).then_inc(tap_done if j < CONV - 1 else conv_done, 1)


def attention(nc, c, ps, qkv, f_rows, y_hi, y_lo, v_at):
    PAIRS = HEADS // 2
    TILES = 2 * TT
    GS = TILES // 2
    PER_HEAD = GS // 2
    units = [(g, u) for g in range(GS) for u in range(g % PER_HEAD + 1)]
    UNITS = len(units)
    upto = [sum(g < k for g, _ in units) for k in range(GS + 1)]
    PROBS = 4
    QW = 2 * P
    with ExitStack() as ctx:
        def sb(name, shape, dt=F32):
            return ctx.enter_context(nc.sbuf_tensor(name, shape, dt))

        def sem(name):
            return ctx.enter_context(nc.semaphore(name))

        q_split = sb("q_split", [P, 2, SEQ], F32R)
        k_twice = sb("k_twice", [P, 2, SEQ], F32R)
        q_ones = sb("q_ones", [P, 2, SEQ], F32R)
        k_rest = sb("k_rest", [P, 2, SEQ], F32R)
        v_cur = nc.alloc_sbuf_tensor_at("v_cur", [P, SEQ], F32, offset=v_at)
        f_cur = sb("f_cur", [P, SEQ])
        v_split = sb("v_split", [P, 2, TT, 2 * HD], F32R)
        probs = sb("probs", [P, PROBS, SEQ])
        diag = sb("diag", [P, PROBS, P])
        pt_hi = sb("probs_t_hi", [P, RING, HALF], F32R)
        pt_lo = sb("probs_t_lo", [P, RING, HALF], F32R)
        neg_max = sb("neg_max", [P, TILES])
        row_sum = sb("row_sum", [P, TILES])
        inv_sum = sb("inv_sum", [P, TILES])
        low_part = sb("low_part", [HD, RING, QW])
        rows_set = sem("rows_set")
        f_loaded = [sem(f"f_loaded{s}") for s in range(2)]
        q_hi_done = sem("q_hi_done")
        k_hi_done = sem("k_hi_done")
        f_hi_done = sem("f_hi_done")
        q_lo_done = sem("q_lo_done")
        k_lo_done = sem("k_lo_done")
        f_lo_done = sem("f_lo_done")
        k_twin_done = sem("k_twin_done")
        twins_done = sem("twins_done")
        v_copied = sem("v_copied")
        held = sem("attn_held")
        v_turned = sem("v_turned")
        v_hi_done = sem("v_hi_done")
        v_ready = sem("v_ready")
        scored = sem("scored")
        maxed = sem("maxed")
        expd = sem("expd")
        inverted = sem("inverted")
        diag_done = sem("diag_done")
        turned = sem("turned")
        pt_hi_done = sem("pt_hi_done")
        pt_lo_done = sem("pt_lo_done")
        weighed = sem("weighed")
        low_done = sem("low_part_done")
        added = sem("attn_added")
        hi_done = sem("attn_hi_done")
        lo_done = sem("attn_lo_done")
        block = ctx.enter_context(nc.Block())

        def own(s):
            return slice(s * HD, (s + 1) * HD)

        def other(s):
            return own(1 - s)

        def f_row(s):
            return slice(HD + 32 * s, HD + 32 * s + 1)

        def flat(t, n):
            return t[:, ds(n, 1), :].rearrange("p a t -> p (a t)")

        def after(i, g):
            return [(i, 2 * g + 2 + k) if g + 1 < GS else (i + 1, k) for k in range(2)]

        def pairs(eng, body):
            with eng.Fori(0, PAIRS - 1) as i:
                body(i, False)
            body(PAIRS - 1, True)

        def raw(n, s):
            return qkv[own(s), ds(n, 1), :].rearrange("p a t -> p (a t)")

        def width(m):
            g, u = units[m]
            return HALF if u < g % PER_HEAD else HALF - P

        @block.sync
        def _(sp):
            def load(i, s):
                sp.dma_start(f_cur[f_row(s), :], f_rows[ds(2 * i + s, 1), :]).then_inc(f_loaded[s], DMA)

            for s in range(2):
                load(0, s)
            with sp.Fori(0, PAIRS - 1) as i:
                for s in range(2):
                    sp.wait_ge(f_lo_done, 2 * i + s + 1)
                    load(i + 1, s)

        @block.gpsimd
        def _(pool):
            def twins(i, s):
                pool.wait_ge(k_hi_done, 2 * i + s + 1)
                pool.sem_inc(held, 1)
                pool.tensor_copy(k_twice[other(s), s, :], k_twice[own(s), s, :]).then_inc(k_twin_done, 1)
                pool.wait_ge(k_twin_done, 2 * i + s + 1)
                pool.sem_inc(held, 1)
                pool.tensor_tensor(k_rest[0:HD, s, :], raw(PAIRS + i, s), k_twice[own(s), s, :].bitcast(F32),
                                   ALU.subtract).then_inc(k_lo_done, 1)
                pool.wait_ge(k_lo_done, 2 * i + s + 1)
                pool.wait_ge(f_hi_done, 2 * i + s + 1)
                pool.tensor_tensor(k_rest[f_row(1 - s), s, :], f_cur[f_row(s), :], k_rest[f_row(s), s, :].bitcast(F32),
                                   ALU.subtract).then_inc(f_lo_done, 1)
                pool.wait_ge(f_lo_done, 2 * i + s + 1)
                pool.wait_ge(q_hi_done, 2 * i + s + 1)
                pool.sem_inc(held, 1)
                pool.tensor_copy(q_ones[0:HD, s, :], q_split[own(s), s, :]).then_inc(twins_done, 1)
                pool.wait_ge(twins_done, 2 * i + s + 1)

            def body(i, last):
                if not last:
                    for s in range(2):
                        twins(i + 1, s)
                pool.wait_ge(hi_done, i + 1)
                pool.sem_inc(held, 1)
                pool.tensor_tensor(flat(y_lo, i), flat(qkv, i), flat(y_hi, i).bitcast(F32), ALU.subtract).then_inc(lo_done, 1)
                pool.wait_ge(lo_done, i + 1)

            for s in range(2):
                twins(0, s)
            pairs(pool, body)

        @block.vector
        def _(dve):
            dve.sem_inc(added, RING)
            dve.sem_inc(pt_lo_done, RING)

            def row_max(i, n):
                dve.wait_ge(scored, TILES * i + n + 1)
                dve.tensor_reduce(neg_max[:, n:n + 1], banks(ps, 2 * (n % RING), 2)[:, 0:(n % TT + 1) * P], AX.X, ALU.max,
                                  negate=True).then_inc(maxed, 1)

            def make_diag(i, n):
                dve.wait_ge(expd, RING + TILES * i + n + 1)
                dve.reciprocal(inv_sum[:, n:n + 1], row_sum[:, n:n + 1]).then_inc(inverted, 1)
                dve.wait_ge(inverted, TILES * i + n + 1)
                dve.tensor_scalar(diag[:, n % PROBS, :], c.ident[:, :], inv_sum[:, n:n + 1], None, ALU.mult).then_inc(diag_done, 1)

            def low(i, m):
                dve.wait_ge(pt_hi_done, UNITS * i + m + 1)
                cols = slice(0, width(m))
                dve.tensor_tensor(pt_lo[:, m % RING, cols], ps[:, 4 + m % RING, cols], pt_hi[:, m % RING, cols].bitcast(F32),
                                  ALU.subtract).then_inc(pt_lo_done, 1)

            def add(i, g):
                dve.wait_ge(low_done, GS * i + g + 1)
                q = g % PER_HEAD
                dve.tensor_tensor(flat(qkv, i)[own(g // PER_HEAD), q * QW:(q + 1) * QW], ps[0:HD, 6 + g % RING, 0:QW],
                                  low_part[:, g % RING, :], ALU.add).then_inc(added, 1)

            def rests(i, s):
                dve.wait_ge(q_hi_done, 2 * i + s + 1)
                dve.scalar_tensor_tensor(out=q_split[other(s), s, :], in0=raw(i, s), scalar=HD ** -0.5,
                                         in1=q_split[own(s), s, :].bitcast(F32), op0=ALU.mult, op1=ALU.subtract).then_inc(q_lo_done, 1)

            def copy_v(i):
                dve.tensor_copy(v_cur[:, :], flat(qkv, 2 * PAIRS + i)).then_inc(v_copied, 1)

            def v_rest(i):
                dve.wait_ge(v_hi_done, i + 1)
                for s in range(2):
                    ins = dve.tensor_tensor(v_split[:, s, :, HD:], banks(ps, 4, 2).rearrange("p (t d) -> p t d", t=TT)[:, :, own(s)],
                                            v_split[:, s, :, 0:HD].bitcast(F32), ALU.subtract)
                ins.then_inc(v_ready, 1)

            def body(i, last):
                for g in range(GS):
                    ms = range(upto[g], upto[g + 1])
                    more = g + 1 < GS or not last
                    if more:
                        row_max(*after(i, g)[0])
                    low(i, ms[0])
                    if more:
                        row_max(*after(i, g)[1])
                    if g > 0:
                        add(i, g - 1)
                    if more:
                        make_diag(*after(i, g)[0])
                    for k, m in enumerate(ms[1:]):
                        low(i, m)
                        if k == 1 and more:
                            make_diag(*after(i, g)[1])
                    if len(ms) < 3 and more:
                        make_diag(*after(i, g)[1])
                    if g == GS - 4 and not last:
                        rests(i + 1, 0)
                    if g == GS - 3 and not last:
                        copy_v(i + 1)
                    if g == GS - 1 and not last:
                        rests(i + 1, 1)
                add(i, GS - 1)
                if not last:
                    v_rest(i + 1)

            copy_v(0)
            for s in range(2):
                rests(0, s)
            v_rest(0)
            for n in range(2):
                row_max(0, n)
            for n in range(2):
                make_diag(0, n)
            pairs(dve, body)

        @block.scalar
        def _(act):
            act.sem_inc(expd, RING)
            for s in range(2):
                ones = spread(c.ones[HD:P, :], [P - HD, SEQ // P, P], 1)
                act.activation(q_ones[HD:P, s, :].rearrange("p (a t) -> p a t", t=P), ones, ACT.Copy)
                act.activation(k_rest[HD:P, s, :].rearrange("p (a t) -> p a t", t=P), ones, ACT.Copy, scale=0.0).then_inc(rows_set, 1)
            act.wait_ge(rows_set, 2)

            def exponent(i, n):
                act.wait_ge(maxed, TILES * i + n + 1)
                if n < PROBS:
                    act.wait_ge(turned, UNITS * i + upto[GS - 1 + n // 2])
                else:
                    act.wait_ge(turned, UNITS * i + UNITS + upto[n // 2 - 1])
                cols = (n % TT + 1) * P
                act.activation(probs[:, n % PROBS, 0:cols], banks(ps, 2 * (n % RING), 2)[:, 0:cols], ACT.Exp,
                               bias=neg_max[:, n:n + 1], accum_out=row_sum[:, n:n + 1]).then_inc(expd, 1)

            def high(i, m):
                act.wait_ge(turned, UNITS * i + UNITS + m + 1)
                act.wait_ge(weighed, UNITS * i + m + 1)
                cols = slice(0, width(m))
                act.activation(pt_hi[:, m % RING, cols], ps[:, 4 + m % RING, cols], ACT.Copy).then_inc(pt_hi_done, 1)

            def low_rows(i, g):
                act.wait_ge(weighed, RING + UNITS * i + upto[g + 1])
                act.wait_ge(added, GS * i + g + 1)
                act.activation(low_part[:, g % RING, :], ps[HD:P, 6 + g % RING, 0:QW], ACT.Copy).then_inc(low_done, 1)

            def operands(i, s):
                act.activation(q_split[own(s), s, :], raw(i, s), ACT.Copy, scale=HD ** -0.5).then_inc(q_hi_done, 1)
                act.activation(k_twice[own(s), s, :], raw(PAIRS + i, s), ACT.Copy).then_inc(k_hi_done, 1)
                act.wait_ge(f_loaded[s], DMA * i + DMA)
                act.activation(k_rest[f_row(s), s, :], f_cur[f_row(s), :], ACT.Copy).then_inc(f_hi_done, 1)

            def v_high(i):
                act.wait_ge(v_turned, i + 1)
                for s in range(2):
                    ins = act.activation(v_split[:, s, :, 0:HD], banks(ps, 4, 2).rearrange("p (t d) -> p t d", t=TT)[:, :, own(s)],
                                         ACT.Copy)
                ins.then_inc(v_hi_done, 1)

            def body(i, last):
                for g in range(GS):
                    ms = range(upto[g], upto[g + 1])
                    more = g + 1 < GS or not last
                    if more:
                        exponent(*after(i, g)[0])
                    high(i, ms[0])
                    if g > 0:
                        low_rows(i, g - 1)
                    for k, m in enumerate(ms[1:]):
                        high(i, m)
                        if k == 0 and more:
                            exponent(*after(i, g)[1])
                    if len(ms) == 1 and more:
                        exponent(*after(i, g)[1])
                    if g == GS - 4 and not last:
                        operands(i + 1, 0)
                    if g == GS - 1 and not last:
                        operands(i + 1, 1)
                low_rows(i, GS - 1)
                if not last:
                    v_high(i + 1)
                act.wait_ge(added, RING + GS * i + GS)
                act.activation(flat(y_hi, i), flat(qkv, i), ACT.Copy).then_inc(hi_done, 1)

            for s in range(2):
                operands(0, s)
            v_high(0)
            exponent(0, 0)
            exponent(0, 1)
            pairs(act, body)

        @block.tensor
        def _(pe):
            pe.sem_inc(turned, UNITS)
            pe.sem_inc(weighed, RING)
            pe.wait_ge(rows_set, 2)

            def score(i, n):
                s, t = n // TT, n % TT
                if t == 0:
                    pe.wait_ge(q_lo_done, 2 * i + s + 1)
                    pe.wait_ge(twins_done, 2 * i + s + 1)
                pe.wait_ge(expd, TILES * i + n + 1)
                q = slice(t * P, (t + 1) * P)
                for a, b, opens in ((q_split, k_twice, True), (q_ones, k_rest, False)):
                    for h in range(t // 4 + 1):
                        keys = slice(h * HALF, min((t + 1) * P, (h + 1) * HALF))
                        last = pe.matmul(ps[:, 2 * (n % RING) + h, 0:keys.stop - keys.start], a[:, s, q], b[:, s, keys],
                                         start=opens, stop=not opens)
                at = t % 4 * P
                last = pe.matmul(ps[:, 2 * (n % RING) + t // 4, at:at + P], c.ident_bf[:, :], c.causal_bf[:, :], start=False,
                                 stop=True, skip_group_check=True)
                last.then_inc(scored, 1)

            def turn(i, m):
                g, u = units[m]
                if u == 0:
                    pe.wait_ge(diag_done, TILES * i + 2 * g + 2)
                pe.wait_ge(pt_lo_done, UNITS * i + m + 1)
                blocks = [(j, n) for j in (2 * u, 2 * u + 1) for n in (2 * g, 2 * g + 1) if j <= n % TT]
                for k, (j, n) in enumerate(blocks):
                    last = pe.matmul(ps[:, 4 + m % RING, k * P:(k + 1) * P], probs[:, n % PROBS, j * P:(j + 1) * P],
                                     diag[:, n % PROBS, :], start=True, stop=True)
                last.then_inc(turned, 1)

            def weigh(i, m):
                g, u = units[m]
                s = g // PER_HEAD
                pe.wait_ge(pt_lo_done, RING + UNITS * i + m + 1)
                if u == 0:
                    pe.wait_ge(added, GS * i + g + 1)
                closing = u == g % PER_HEAD
                for k, j in enumerate((2 * u, 2 * u + 1)):
                    past = closing and k == 1
                    out = ps[:, 6 + g % RING, P:QW] if past else ps[:, 6 + g % RING, 0:QW]
                    for part in (pt_hi, pt_lo):
                        last = pe.matmul(out, v_split[:, s, j, :], part[:, m % RING, k * QW:k * QW + (P if past else QW)],
                                         start=j == 0 and part is pt_hi, stop=past or (closing and part is pt_lo),
                                         skip_group_check=past)
                last.then_inc(weighed, 1)

            def turn_v(i):
                pe.wait_ge(v_copied, i + 1)
                for t in range(TT):
                    last = pe.transpose(ps[:, 4 + t // 4, (t % 4) * P:(t % 4 + 1) * P], v_cur[:, t * P:(t + 1) * P], c.ident[:, :])
                last.then_inc(v_turned, 1)

            def body(i, last):
                for g in range(GS):
                    more = g + 1 < GS or not last
                    if more:
                        score(*after(i, g)[0])
                    if g == 0:
                        pe.wait_ge(v_ready, i + 1)
                    for k, m in enumerate(range(upto[g], upto[g + 1])):
                        turn(i, m)
                        if k == 0 and more:
                            score(*after(i, g)[1])
                        if m > 0:
                            weigh(i, m - 1)
                weigh(i, UNITS - 1)
                if not last:
                    turn_v(i + 1)

            turn_v(0)
            score(0, 0)
            score(0, 1)
            pairs(pe, body)


def state_space(nc, c, ps, xbc, dt_tok, a_tok, d_skip, silu_z, gated, square_sum, load_next):
    CHUNKS = SEQ // P
    H, HP = SSD_HEADS, SSD_HD
    QUARTER = H // 4
    with ExitStack() as ctx:
        def sb(name, shape, dt=F32):
            return ctx.enter_context(nc.sbuf_tensor(name, shape, dt))

        def sem(name):
            return ctx.enter_context(nc.semaphore(name))

        d_col = sb("d_col", [P, XB])
        a_cs = sb("a_cs", [P, CHUNKS, H])
        a_total = sb("a_total", [P, CHUNKS, H])
        a_left = sb("a_left", [P, CHUNKS, H])
        grow_in = sb("grow_in", [P, CHUNKS, H])
        chunk_decay = sb("chunk_decay", [P, CHUNKS, H])
        to_end = sb("to_end", [P, CHUNKS, H])
        dt_to_end = sb("dt_to_end", [P, CHUNKS, H])
        chan = sb("chan", [P, RING, CB, P])
        a_spread = sb("a_spread", [P, RING, H, P])
        cb_masked = sb("cb_masked", [P, RING, GROUPS, P])
        b_tok = sb("b_tok", [P, RING, GROUPS, P])
        decay = sb("decay", [P, RING, H, P])
        x_dt = sb("x_dt", [P, RING, H, HP])
        x_end = sb("x_end", [P, RING, H, HP])
        y_tok = sb("y_tok", [P, H, HP])
        state = sb("state", [P, H, HP])
        skip = sb("skip", [P, XB, P])
        y_sum = sb("y_sum", [P, XB, P])
        z_chunk = sb("z_chunk", [P, RING, XB, P])
        gated_sq = sb("gated_sq", [P, XB, P])

        d_loaded = sem("d_loaded")
        z_loaded = [sem(f"z_loaded{s}") for s in range(RING)]
        sums_ready = sem("sums_ready")
        pre = sem("ssd_prelude_vec")
        pre_exp = sem("ssd_prelude_exp")
        state_zero = sem("state_zero")
        copied = sem("chunk_copied")
        a_ready = sem("a_spread_ready")
        small_ready = sem("cb_and_b_ready")
        cb_done = sem("cb_masked_done")
        b_done = sem("b_tok_done")
        x_turned = sem("x_turned")
        x_scaled = sem("x_scaled")
        seg_done = sem("seg_done")
        decay_done = sem("decay_done")
        m_done = sem("m_done")
        y_parts = sem("y_parts")
        off_ready = sem("off_ready")
        off_scaled = sem("off_scaled")
        y_added = sem("y_added")
        gain_ready = sem("state_gain_ready")
        state_scaled = sem("state_scaled")
        state_done = sem("state_done")
        y_turned = sem("y_turned")
        skip_done = sem("skip_done")
        y_done = sem("y_done")
        gated_done = sem("gated_done")
        held = sem("gated_held")
        act_held = sem("squared_held")
        gated_squared = sem("gated_squared")
        square_summed = sem("square_summed")
        z_cols = silu_z.rearrange("b p t -> p b t")
        block = ctx.enter_context(nc.Block())
        y_in = banks(ps, 4, 2)
        y_off = banks(ps, 6, 2)

        def steps(eng, step):
            step(0, 0, 2)
            step(1, 1, 2)
            with eng.Fori(0, CHUNKS // 2 - 2) as i:
                step(2 * i + 2, 0, 2)
                step(2 * i + 3, 1, 2)
            step(CHUNKS - 2, 0, 1)
            step(CHUNKS - 1, 1, 0)

        @block.sync
        def _(sp):
            heads = d_skip.rearrange("a (b two) -> two a b", two=2)
            with nc.allow_non_contiguous_dma(reason="16 numbers"):
                for half in range(2):
                    sp.dma_start(d_col[half * HP:(half + 1) * HP, :], heads[half].to_broadcast([HP, XB])).then_inc(d_loaded, DMA)

            def step(n, s, after):
                sp.wait_ge(gated_done, n + 1)
                sp.dma_start(z_chunk[:, s, :, :], z_cols[:, :, ds(n * P, P)]).then_inc(z_loaded[s], DMA)

            steps(sp, step)
            load_next(sp)

        @block.gpsimd
        def _(pool):
            pool.sem_inc(gated_done, RING)
            pool.sem_inc(skip_done, 1)
            pool.memset(state[:, :, :], 0.0).then_inc(state_zero, 1)

            def front(n, s):
                pool.wait_ge(seg_done, 4 * n + 4)
                pool.tensor_tensor(a_spread[:, s, :, :],
                                   spread(a_tok[:, ds(n, 1), :].rearrange("p a h -> p (a h)"), [P, H, P], 2),
                                   spread(c.tri[:, :], [P, H, P], 1), ALU.mult).then_inc(a_ready, 1)

            def step(n, s, after):
                pool.wait_ge(y_done, 1 + n)
                pool.wait_ge(copied, n + 1)
                pool.tensor_tensor(skip[:, :, :], chan[:, s, 0:XB, :], spread(d_col[:, :], [P, XB, P], 2),
                                   ALU.mult).then_inc(skip_done, 1)
                pool.wait_ge(off_ready, n + 1)
                pool.tensor_tensor(state[:, :, :], state[:, :, :],
                                   spread(chunk_decay[:, ds(n, 1), :].rearrange("p a h -> p (a h)"), [P, H, HP], 2),
                                   ALU.mult).then_inc(state_scaled, 1)
                if after == 2:
                    front(n + 2, s)
                pool.wait_ge(y_done, 1 + n + 1)
                pool.wait_ge(z_loaded[s], DMA * (n // 2 if isinstance(n, int) else (n - s) // 2) + DMA)
                pool.sem_inc(held, 1)
                pool.tensor_tensor(gated[:, :, ds(n * P, P)], y_sum[:, :, :], z_chunk[:, s, :, :],
                                   ALU.mult).then_inc(gated_done, 1)

            pool.wait_ge(d_loaded, 2 * DMA)
            front(0, 0)
            front(1, 1)
            pool.wait_ge(pre_exp, 2)
            steps(pool, step)

        @block.scalar
        def _(act):
            act.sem_inc(decay_done, 4)
            act.wait_ge(pre, 2)
            act.activation(grow_in[:, :, :], a_cs[:, :, :], ACT.Exp).then_inc(pre_exp, 1)
            act.activation(chunk_decay[:, :, :], a_total[:, :, :], ACT.Exp).then_inc(pre_exp, 1)
            act.wait_ge(pre, 3)
            act.activation(to_end[:, :, :], a_left[:, :, :], ACT.Exp).then_inc(pre_exp, 1)

            def copy_chunk(n, s):
                act.wait_ge(y_parts, n + 1)
                act.wait_ge(skip_done, n)
                act.activation(chan[:, s, :, :], xbc[:, :, ds(n * P, P)], ACT.Copy).then_inc(copied, 1)

            def front(n, s):
                act.wait_ge(small_ready, n + 1)
                act.wait_ge(cb_done, n + 1)
                act.activation(b_tok[:, s, :, :].rearrange("p g d -> p (g d)"), ps[:, 0, GROUPS * P:], ACT.Copy).then_inc(b_done, 1)
                for q in range(4):
                    act.wait_ge(seg_done, 4 * RING + 4 * n + q + 1)
                    if q == 0:
                        act.wait_ge(y_parts, n + 1)
                    act.activation(decay[:, s, q * QUARTER:(q + 1) * QUARTER, :].rearrange("p h l -> p (h l)"),
                                   ps[:, (q + 1) % 2, :], ACT.Exp).then_inc(decay_done, 1)

            def square(n):
                act.wait_ge(gated_done, RING + n + 1)
                act.wait_ge(square_summed, 1 + n)
                act.sem_inc(act_held, 1)
                act.activation(gated_sq[:, :, :], gated[:, :, ds(n * P, P)], ACT.Square).then_inc(gated_squared, 1)

            def step(n, s, after):
                if after:
                    front(n + 1, 1 - s)
                if not (isinstance(n, int) and n == 0):
                    square(n - 1)
                if after == 2:
                    copy_chunk(n + 2, s)

            copy_chunk(0, 0)
            copy_chunk(1, 1)
            front(0, 0)
            steps(act, step)
            square(CHUNKS - 1)

        @block.vector
        def _(dve):
            for s in (y_done, x_scaled, state_done, square_summed):
                dve.sem_inc(s, 1)
            dve.wait_ge(sums_ready, 1)
            dve.tensor_copy(a_cs[:, :, :].rearrange("p t h -> p (t h)"), ps[:, 0, 0:P]).then_inc(pre, 1)
            dve.tensor_copy(a_total[:, :, :].rearrange("p t h -> p (t h)"), ps[:, 0, P:2 * P]).then_inc(pre, 1)
            dve.wait_ge(pre, 2)
            dve.tensor_tensor(a_left[:, :, :], a_total[:, :, :], a_cs[:, :, :], ALU.subtract).then_inc(pre, 1)
            dve.wait_ge(pre_exp, 3)
            dve.tensor_tensor(dt_to_end[:, :, :], dt_tok[:, :, :], to_end[:, :, :], ALU.mult).then_inc(pre, 1)
            dve.wait_ge(pre, 4)
            dve.wait_ge(state_zero, 1)

            def per_head(t, n):
                return spread(t[:, ds(n, 1), :].rearrange("p a h -> p (a h)"), [P, H, HP], 2)

            def x_psum():
                return banks(ps, 2, 2).rearrange("p (h d) -> p h d", h=H)

            def front_x(n, s):
                dve.wait_ge(small_ready, n + 1)
                dve.tensor_tensor(cb_masked[:, s, :, :], ps[:, 0, 0:GROUPS * P].rearrange("p (g l) -> p g l", g=GROUPS),
                                  spread(c.tri[:, :], [P, GROUPS, P], 1), ALU.mult).then_inc(cb_done, 1)
                dve.wait_ge(x_turned, n + 1)
                dve.tensor_tensor(x_dt[:, s, :, :], x_psum(), per_head(dt_tok, n), ALU.mult)
                dve.tensor_tensor(x_end[:, s, :, :], x_psum(), per_head(dt_to_end, n), ALU.mult).then_inc(x_scaled, 1)

            def front_m(n, s):
                dve.wait_ge(cb_done, n + 1)
                for q in range(4):
                    dve.wait_ge(decay_done, 4 + 4 * n + q + 1)
                    heads = slice(q * QUARTER, (q + 1) * QUARTER)
                    dve.tensor_tensor(decay[:, s, heads, :], decay[:, s, heads, :],
                                      spread(cb_masked[:, s, q * GROUPS // 4, :], [P, QUARTER, P], 1), ALU.mult).then_inc(m_done, 1)

            def sum_squares(n):
                dve.wait_ge(gated_squared, n + 1)
                dve.tensor_reduce(square_sum[:, ds(n * P, P)], gated_sq[:, :, :].rearrange("p b l -> p l b"), AX.X,
                                  ALU.add).then_inc(square_summed, 1)

            def step(n, s, after):
                if after:
                    front_x(n + 1, 1 - s)
                    front_m(n + 1, 1 - s)
                dve.wait_ge(off_ready, n + 1)
                if not (isinstance(n, int) and n == 0):
                    dve.wait_ge(y_turned, n)
                dve.tensor_tensor(y_tok[:, :, :], y_off.rearrange("p (h d) -> p h d", h=H), per_head(grow_in, n),
                                  ALU.mult).then_inc(off_scaled, 1)
                dve.wait_ge(off_scaled, n + 1)
                dve.wait_ge(y_parts, RING + n + 1)
                dve.tensor_tensor(y_tok[:, :, :].rearrange("p h d -> p (h d)"), y_in,
                                  y_tok[:, :, :].rearrange("p h d -> p (h d)"), ALU.add).then_inc(y_added, 1)
                dve.wait_ge(state_scaled, n + 1)
                dve.wait_ge(gain_ready, n + 1)
                dve.tensor_tensor(state[:, :, :].rearrange("p h d -> p (h d)"), y_off,
                                  state[:, :, :].rearrange("p h d -> p (h d)"), ALU.add).then_inc(state_done, 1)
                if not (isinstance(n, int) and n == 0):
                    sum_squares(n - 1)
                dve.wait_ge(y_turned, n + 1)
                dve.wait_ge(skip_done, 1 + n + 1)
                dve.wait_ge(gated_done, RING + n)
                dve.tensor_tensor(y_sum[:, :, :].rearrange("p b l -> p (b l)"), y_in,
                                  skip[:, :, :].rearrange("p b l -> p (b l)"), ALU.add).then_inc(y_done, 1)

            front_x(0, 0)
            front_m(0, 0)
            steps(dve, step)
            sum_squares(CHUNKS - 1)

        @block.tensor
        def _(pe):
            pe.sem_inc(y_parts, RING)
            pe.sem_inc(seg_done, 4 * RING)
            flat = a_tok[:, :, :].rearrange("p t h -> p (t h)")
            pe.matmul(ps[:, 0, 0:P], c.tri[:, :], flat, start=True, stop=True)
            pe.matmul(ps[:, 0, P:2 * P], c.ones[:, :], flat, start=True, stop=True).then_inc(sums_ready, 1)

            def front_small(n, s):
                pe.wait_ge(copied, n + 1)
                pe.wait_ge(decay_done, 4 + 4 * n)
                for g in range(GROUPS):
                    pe.matmul(ps[:, 0, g * P:(g + 1) * P], chan[:, s, XB + g, :], chan[:, s, XB + GROUPS + g, :],
                              start=True, stop=True)
                for g in range(GROUPS):
                    last = pe.transpose(ps[:, 0, (GROUPS + g) * P:(GROUPS + g + 1) * P], chan[:, s, XB + g, :], c.ident[:, :])
                last.then_inc(small_ready, 1)
                pe.wait_ge(x_scaled, 1 + n)
                for b in range(XB):
                    last = pe.transpose(ps[:, 2 + b // 4, (b % 4) * P:(b % 4 + 1) * P], chan[:, s, b, :], c.ident[:, :])
                last.then_inc(x_turned, 1)

            def front_seg(n, s):
                pe.wait_ge(a_ready, n + 1)
                for q in range(4):
                    if q == 1:
                        pe.wait_ge(cb_done, n + 1)
                        pe.wait_ge(b_done, n + 1)
                    if q >= 2:
                        pe.wait_ge(decay_done, 4 + 4 * n + q - 1)
                    pe.matmul(ps[:, (q + 1) % 2, :], c.tri_after[:, :],
                              a_spread[:, s, q * QUARTER:(q + 1) * QUARTER, :].rearrange("p h l -> p (h l)"),
                              start=True, stop=True).then_inc(seg_done, 1)

            def step(n, s, after):
                if after:
                    front_small(n + 1, 1 - s)
                pe.wait_ge(state_done, 1 + n)
                for g in range(GROUPS):
                    heads = slice(g * H // GROUPS, (g + 1) * H // GROUPS)
                    last = pe.matmul(ps[:, 6 + g, :], chan[:, s, XB + GROUPS + g, :],
                                     state[:, heads, :].rearrange("p h d -> p (h d)"), start=True, stop=True)
                last.then_inc(off_ready, 1)
                if after:
                    front_seg(n + 1, 1 - s)
                pe.wait_ge(m_done, 4 * n + 4)
                pe.wait_ge(y_done, 1 + n)
                for h in range(H):
                    last = pe.matmul(y_in[:, h * HP:(h + 1) * HP], decay[:, s, h, :], x_dt[:, s, h, :], start=True, stop=True)
                last.then_inc(y_parts, 1)
                pe.wait_ge(off_scaled, n + 1)
                for g in range(GROUPS):
                    heads = slice(g * H // GROUPS, (g + 1) * H // GROUPS)
                    last = pe.matmul(ps[:, 6 + g, :], b_tok[:, s, g, :],
                                     x_end[:, s, heads, :].rearrange("p h d -> p (h d)"), start=True, stop=True)
                last.then_inc(gain_ready, 1)
                pe.wait_ge(y_added, n + 1)
                for b in range(XB):
                    last = pe.transpose(ps[:, 4 + b // 4, (b % 4) * P:(b % 4 + 1) * P],
                                        y_tok[:, 2 * b:2 * b + 2, :].rearrange("p h d -> p (h d)"), c.ident[:, :])
                last.then_inc(y_turned, 1)

            pe.wait_ge(pre, 2)
            front_small(0, 0)
            front_seg(0, 0)
            steps(pe, step)


class BranchWeights:
    KA = D_ATTN // P
    KW = KA + XB

    def __init__(self, nc, ctx, w_attn, w_ssd):
        self.raw = ctx.enter_context(nc.sbuf_tensor("branch_raw", [P, RING, self.KW, P], F32))
        self.loaded = [ctx.enter_context(nc.semaphore(f"branch_loaded{s}")) for s in range(RING)]
        self.w_attn = w_attn.rearrange("(k p) c -> p k c", p=P)
        self.w_ssd = w_ssd.rearrange("(k p) c -> p k c", p=P)

    def load(self, sp, n, s):
        sp.dma_start(self.raw[:, s, 0:self.KA, :], self.w_attn[:, :, ds(n * P, P)]).then_inc(self.loaded[s], DMA)
        sp.dma_start(self.raw[:, s, self.KA:, :], self.w_ssd[:, :, ds(n * P, P)]).then_inc(self.loaded[s], DMA)

    def load_first(self, sp):
        for s in range(RING):
            self.load(sp, s, s)


def merge(nc, c, ps, weights, gates, gated, square_sum, gain, ya_hi, ya_lo, merged):
    KA, KW = weights.KA, weights.KW
    NB = D // P
    with ExitStack() as ctx:
        def sb(name, shape, dt=F32):
            return ctx.enter_context(nc.sbuf_tensor(name, shape, dt))

        def sem(name):
            return ctx.enter_context(nc.semaphore(name))

        ys_hi = sb("ys_hi", [P, XB, SEQ], F32R)
        ys_lo = sb("ys_lo", [P, XB, SEQ], F32R)
        gain_col = sb("ssd_gain_col", [P, XB])
        w_hi = sb("branch_hi", [P, RING, KW, P], F32R)
        w_lo = sb("branch_lo", [P, RING, KW, P], F32R)
        gate = sb("gate", [P, RING, 2, SEQ])
        rstd = square_sum
        gain_loaded = sem("ssd_gain_loaded")
        summed = sem("ssd_summed")
        mean_done = sem("ssd_mean_done")
        root_done = sem("ssd_root_done")
        rstd_done = sem("ssd_rstd_done")
        ys_hi_done = sem("ys_hi_done")
        ys_lo_done = sem("ys_lo_done")
        g_loaded = [sem(f"gate_loaded{s}") for s in range(RING)]
        hi_done = sem("branch_hi_done")
        lo_done = sem("branch_lo_done")
        projected = sem("branch_projected")
        scaled = sem("gate_scaled")
        weighed = sem("branch_weighed")
        added = sem("branch_added")
        block = ctx.enter_context(nc.Block())

        @block.sync
        def _(sp):
            with nc.allow_non_contiguous_dma(reason="a gain per channel"):
                sp.dma_start(gain_col[:, :], gain.rearrange("a (b p) -> p (a b)", p=P)).then_inc(gain_loaded, DMA)

            def load_gates(n, s):
                sp.wait_ge(added, n + 1)
                sp.dma_start(gate[:, s, 0, :], gates[ds(n, 1)].rearrange("a p t -> p (a t)")).then_inc(g_loaded[s], DMA)
                sp.dma_start(gate[:, s, 1, :], gates[ds(NB + n, 1)].rearrange("a p t -> p (a t)")).then_inc(g_loaded[s], DMA)

            for s in range(RING):
                load_gates(s, s)
            with sp.Fori(0, NB // RING - 1) as i:
                for s in range(RING):
                    n = RING * i + RING + s
                    sp.wait_ge(lo_done, n + 1)
                    weights.load(sp, n, s)
                    load_gates(n, s)

        @block.scalar
        def _(act):
            def high(n, s, i):
                act.wait_ge(weights.loaded[s], 2 * DMA * i + 2 * DMA)
                act.wait_ge(projected, n + 1)
                act.activation(w_hi[:, s, :, :], weights.raw[:, s, :, :], ACT.Copy).then_inc(hi_done, 1)

            high(0, 0, 0)
            act.wait_ge(gain_loaded, DMA)
            for b in range(XB):
                act.activation(ys_hi[:, b, :], gated[:, b, :], ACT.Copy, scale=gain_col[:, b:b + 1]).then_inc(ys_hi_done, 1)
            act.wait_ge(mean_done, 1)
            act.activation(rstd[:, :], rstd[:, :], ACT.Sqrt).then_inc(root_done, 1)
            high(1, 1, 0)
            with act.Fori(0, NB // RING - 1) as i:
                for s in range(RING):
                    high(RING * i + RING + s, s, i + 1)

        @block.gpsimd
        def _(pool):
            pool.sem_inc(lo_done, RING)

            def rest(n, s):
                pool.wait_ge(hi_done, n + 1)
                pool.tensor_tensor(w_lo[:, s, :, :], weights.raw[:, s, :, :], w_hi[:, s, :, :].bitcast(F32),
                                   ALU.subtract).then_inc(lo_done, 1)

            def scale_gate(n, s, i):
                pool.wait_ge(g_loaded[s], 2 * DMA * i + 2 * DMA)
                pool.tensor_tensor(gate[:, s, 1, :], gate[:, s, 1, :], rstd[:, :], ALU.mult).then_inc(scaled, 1)

            rest(0, 0)
            pool.wait_ge(rstd_done, 1)
            rest(1, 1)
            scale_gate(0, 0, 0)
            scale_gate(1, 1, 0)
            with pool.Fori(0, NB // RING - 1) as i:
                for s in range(RING):
                    n = RING * i + RING + s
                    rest(n, s)
                    scale_gate(n, s, i + 1)

        @block.tensor
        def _(pe):
            pe.sem_inc(projected, RING)
            for h in range(2):
                last = pe.matmul(ps[:, 4 + h, :], c.ones[:, :], square_sum[:, h * HALF:(h + 1) * HALF], start=True, stop=True)
            last.then_inc(summed, 1)

            def product(n, s, first):
                pe.wait_ge(lo_done, RING + n + 1)
                pe.wait_ge(added, n + 1)
                for k in range(KW):
                    hi, lo, kk, b = (ya_hi, ya_lo, k, 4 * s) if k < KA else (ys_hi, ys_lo, k - KA, 4 * s + 2)
                    if first and k >= KA:
                        pe.wait_ge(ys_lo_done, kk + 1)
                    last = three_passes(pe, [ps[:, b, :], ps[:, b + 1, :]], w_hi[:, s, k, :], w_lo[:, s, k, :],
                                        [hi[:, kk, 0:HALF], hi[:, kk, HALF:SEQ]], [lo[:, kk, 0:HALF], lo[:, kk, HALF:SEQ]],
                                        kk == 0, k in (KA - 1, KW - 1))
                last.then_inc(projected, 1)

            product(0, 0, True)
            pe.wait_ge(mean_done, 1)
            product(1, 1, False)
            with pe.Fori(0, NB // RING - 1) as i:
                for s in range(RING):
                    product(RING * i + RING + s, s, False)

        @block.vector
        def _(dve):
            dve.sem_inc(added, RING)
            dve.wait_ge(summed, 1)
            dve.tensor_scalar(rstd[:, :], banks(ps, 4, 2), 1.0 / D_SSD, EPS, ALU.mult, ALU.add).then_inc(mean_done, 1)
            for b in range(XB):
                dve.wait_ge(ys_hi_done, b + 1)
                dve.scalar_tensor_tensor(out=ys_lo[:, b, :], in0=gated[:, b, :], scalar=gain_col[:, b:b + 1],
                                         in1=ys_hi[:, b, :].bitcast(F32), op0=ALU.mult, op1=ALU.subtract).then_inc(ys_lo_done, 1)
            dve.wait_ge(root_done, 1)
            dve.reciprocal(rstd[:, :], rstd[:, :]).then_inc(rstd_done, 1)
            with dve.Fori(0, NB // RING) as i:
                for s in range(RING):
                    n = RING * i + s
                    out = merged[:, ds(n, 1), :].rearrange("p a t -> p (a t)")
                    dve.wait_ge(projected, RING + n + 1)
                    dve.wait_ge(scaled, n + 1)
                    for g in range(2):
                        dve.tensor_tensor(gate[:, s, g, :], banks(ps, 4 * s + 2 * g, 2), gate[:, s, g, :], ALU.mult).then_inc(weighed, 1)
                    dve.wait_ge(weighed, 2 * n + 2)
                    dve.tensor_tensor(out, gate[:, s, 0, :], gate[:, s, 1, :], ALU.add).then_inc(added, 1)


def project_out(nc, c, ps, w_out, x, merged, x2, gain, w_group, b_group, w_expert, b_expert, h2_rows, logits):
    W_RING = 3
    NL = N_GROUPS + NE
    with ExitStack() as ctx:
        def sb(name, shape, dt=F32):
            return ctx.enter_context(nc.sbuf_tensor(name, shape, dt))

        def sem(name):
            return ctx.enter_context(nc.semaphore(name))

        w_raw = sb("out_raw", [P, W_RING, D])
        w_hi = sb("out_hi", [P, KT, D], F32R)
        w_lo = sb("out_lo", [P, KT, D], F32R)
        m_hi = sb("merged_hi", [P, RING, KT, P], F32R)
        m_lo = sb("merged_lo", [P, RING, KT, P], F32R)
        x_tile = sb("x_tile", [P, RING, D])
        w_router = sb("w_router", [P, KT, NL])
        b_router = sb("b_router", [P, NL])
        gain_row = sb("gain2_row", [P, D])
        sum_sq = sb("sum_sq2", [P, TT])
        mean_sq = sb("mean_sq2", [P, TT])
        root = sb("root2", [P, TT])
        rstd = sb("rstd2", [P, TT])
        h2 = sb("h2", [P, RING, D])
        h2_t = sb("h2_t", [P, KT, P])
        w_loaded = [sem(f"out_loaded{s}") for s in range(W_RING)]
        x_loaded = [sem(f"res_loaded{s}") for s in range(RING)]
        w_hi_done = sem("out_hi_done")
        w_lo_done = sem("out_lo_done")
        m_hi_done = sem("merged_hi_done")
        m_lo_done = sem("merged_lo_done")
        projected = sem("out_projected")
        added = sem("out_added")
        router_loaded = sem("router_loaded")
        squared = sem("squared2")
        mean_done = sem("mean_done2")
        root_done = sem("root_done2")
        rstd_done = sem("rstd_done2")
        h2_done = sem("h2_done")
        stored = [sem(f"h2_stored{s}") for s in range(RING)]
        turned = sem("h2_turned")
        t_done = sem("h2_t_done")
        routed = sem("routed")
        logit_done = sem("logit_done")
        x_tiles = x[0].rearrange("(t p) d -> t p d", p=P)
        w_rows = w_out.rearrange("(k p) c -> k p c", p=P)
        h2_tiles = h2_rows.rearrange("(t p) d -> t p d", p=P)
        block = ctx.enter_context(nc.Block())

        def tiles(eng, body):
            body(0, 0, 0)
            body(1, 1, 0)
            with eng.Fori(0, TT // RING - 2) as i:
                for s in range(RING):
                    body(RING * i + RING + s, s, i + 1)
            for s in range(RING):
                body(TT - RING + s, s, TT // RING - 1)

        def at_least(t, n):
            return not isinstance(t, int) or t >= n

        def follows(t):
            return not isinstance(t, int) or t + 1 < TT

        def row(tensor, t):
            return tensor[:, ds(t, 1), :].rearrange("p a d -> p (a d)")

        @block.sync
        def _(sp):
            for k in range(KT):
                sp.wait_ge(w_lo_done, k + 1)
                sp.dma_start(w_raw[:, k % W_RING, :], w_rows[k]).then_inc(w_loaded[k % W_RING], DMA)
            with nc.allow_non_contiguous_dma(reason="narrow router weights"):
                sp.dma_start(w_router[:, :, 0:N_GROUPS], w_group.rearrange("(k p) g -> p k g", p=P)).then_inc(router_loaded, DMA)
                sp.dma_start(w_router[:, :, N_GROUPS:NL], w_expert.rearrange("(k p) g -> p k g", p=P)).then_inc(router_loaded, DMA)
                sp.dma_start(b_router[:, 0:N_GROUPS], b_group.to_broadcast([P, N_GROUPS])).then_inc(router_loaded, DMA)
                sp.dma_start(b_router[:, N_GROUPS:NL], b_expert.to_broadcast([P, NE])).then_inc(router_loaded, DMA)
            sp.dma_start(gain_row[:, :], gain.to_broadcast([P, D])).then_inc(router_loaded, DMA)
            for s in range(RING):
                sp.sem_inc(stored[s], DMA)

            def load_x(t, s):
                sp.wait_ge(added, t + 1)
                sp.dma_start(x_tile[:, s, :], x_tiles[ds(t, 1)].rearrange("a p d -> p (a d)")).then_inc(x_loaded[s], DMA)

            def store_h2(t, s):
                sp.wait_ge(h2_done, t + 1)
                sp.dma_start(h2_tiles[ds(t, 1)].rearrange("a p d -> p (a d)"), h2[:, s, :]).then_inc(stored[s], DMA)

            for s in range(RING):
                load_x(s, s)
            with sp.Fori(0, TT // RING - 1) as i:
                for s in range(RING):
                    load_x(RING * i + RING + s, s)
                    store_h2(RING * i + s, s)
            for s in range(RING):
                store_h2(TT - RING + s, s)
            for s in range(RING):
                sp.wait_ge(stored[s], DMA * (TT // RING) + DMA)

        @block.scalar
        def _(act):
            def high(t, s):
                act.wait_ge(projected, t + 1)
                act.activation(m_hi[:, s, :, :], merged[:, :, ds(t * P, P)], ACT.Copy).then_inc(m_hi_done, 1)

            def turn_out(t):
                act.wait_ge(turned, RING + t + 1)
                act.wait_ge(routed, 1 + t)
                act.activation(h2_t[:, :, :].rearrange("p k t -> p (k t)"), banks(ps, 4, 2), ACT.Copy).then_inc(t_done, 1)

            def body(t, s, i):
                if follows(t):
                    high(t + 1, 1 - s)
                act.wait_ge(turned, t + 1)
                act.wait_ge(stored[s], DMA * i + DMA)
                act.wait_ge(added, RING + t + 1)
                act.activation(h2[:, s, :], row(x2, t), ACT.Square, accum_out=sum_sq[:, ds(t, 1)]).then_inc(squared, 1)
                act.wait_ge(mean_done, t + 1)
                act.activation(root[:, ds(t, 1)], mean_sq[:, ds(t, 1)], ACT.Sqrt).then_inc(root_done, 1)
                if at_least(t, 1):
                    turn_out(t - 1)

            high(0, 0)
            for k in range(KT):
                act.wait_ge(w_loaded[k % W_RING], DMA * (k // W_RING) + DMA)
                act.activation(w_hi[:, k, :], w_raw[:, k % W_RING, :], ACT.Copy).then_inc(w_hi_done, 1)
            tiles(act, body)
            turn_out(TT - 1)

        @block.tensor
        def _(pe):
            pe.sem_inc(projected, RING)
            pe.sem_inc(turned, RING)
            pe.sem_inc(routed, 1)

            def product(t, s, first):
                pe.wait_ge(m_lo_done, t + 1)
                pe.wait_ge(added, t + 1)
                for k in range(KT):
                    if first:
                        pe.wait_ge(w_lo_done, W_RING + k + 1)
                    last = three_passes(pe, [ps[:, 2 * s, :], ps[:, 2 * s + 1, :]], m_hi[:, s, k, :], m_lo[:, s, k, :],
                                        [w_hi[:, k, 0:HALF], w_hi[:, k, HALF:D]], [w_lo[:, k, 0:HALF], w_lo[:, k, HALF:D]],
                                        k == 0, k == KT - 1)
                last.then_inc(projected, 1)

            def turn(t, s):
                pe.wait_ge(h2_done, t + 1)
                for k in range(KT):
                    last = pe.transpose(banks(ps, 4, 2)[:, k * P:(k + 1) * P], h2[:, s, k * P:(k + 1) * P], c.ident[:, :])
                last.then_inc(turned, 1)

            def score(t, s):
                pe.wait_ge(t_done, t + 1)
                pe.wait_ge(logit_done, t + 1)
                for k in range(KT):
                    last = pe.matmul(ps[:, 6 + s, 0:NL], h2_t[:, k, :], w_router[:, k, :], start=k == 0, stop=k == KT - 1)
                last.then_inc(routed, 1)

            def body(t, s, i):
                product(t, s, isinstance(t, int) and t == 0)
                if at_least(t, 2):
                    score(t - 2, s)
                if at_least(t, 1):
                    turn(t - 1, 1 - s)

            tiles(pe, body)
            score(TT - 2, 0)
            turn(TT - 1, 1)
            score(TT - 1, 1)

        @block.vector
        def _(dve):
            dve.sem_inc(w_lo_done, W_RING)
            dve.sem_inc(added, RING)
            dve.sem_inc(logit_done, RING)

            def rest(t, s):
                dve.wait_ge(m_hi_done, t + 1)
                dve.tensor_tensor(m_lo[:, s, :, :], merged[:, :, ds(t * P, P)], m_hi[:, s, :, :].bitcast(F32),
                                  ALU.subtract).then_inc(m_lo_done, 1)

            def logit(t, s):
                dve.wait_ge(routed, 1 + t + 1)
                dve.tensor_tensor(row(logits, t), ps[:, 6 + s, 0:NL], b_router[:, :], ALU.add).then_inc(logit_done, 1)

            def body(t, s, i):
                if follows(t):
                    rest(t + 1, 1 - s)
                dve.wait_ge(projected, RING + t + 1)
                dve.wait_ge(x_loaded[s], DMA * i + DMA)
                dve.tensor_tensor(row(x2, t), banks(ps, 2 * s, 2), x_tile[:, s, :], ALU.add).then_inc(added, 1)
                dve.wait_ge(squared, t + 1)
                dve.tensor_scalar(mean_sq[:, ds(t, 1)], sum_sq[:, ds(t, 1)], 1.0 / D, EPS, ALU.mult, ALU.add).then_inc(mean_done, 1)
                dve.wait_ge(root_done, t + 1)
                dve.reciprocal(rstd[:, ds(t, 1)], root[:, ds(t, 1)]).then_inc(rstd_done, 1)
                dve.wait_ge(rstd_done, t + 1)
                dve.scalar_tensor_tensor(out=h2[:, s, :], in0=row(x2, t), scalar=rstd[:, ds(t, 1)], in1=gain_row[:, :],
                                         op0=ALU.mult, op1=ALU.mult).then_inc(h2_done, 1)
                if at_least(t, 2):
                    logit(t - 2, s)

            rest(0, 0)
            for k in range(KT):
                dve.wait_ge(w_hi_done, k + 1)
                dve.tensor_tensor(w_lo[:, k, :], w_raw[:, k % W_RING, :], w_hi[:, k, :].bitcast(F32), ALU.subtract).then_inc(w_lo_done, 1)
            dve.wait_ge(router_loaded, 5 * DMA)
            tiles(dve, body)
            logit(TT - 2, 0)
            logit(TT - 1, 1)


def route(nc, c, ps, logits, gates, slot_table, gather_src, scatter_dst, over_expert, weights):
    with ExitStack() as ctx:
        def sb(name, shape, dt=F32):
            return ctx.enter_context(nc.sbuf_tensor(name, shape, dt))

        def sem(name):
            return ctx.enter_context(nc.semaphore(name))

        unused = sb("unused", [P, BLOCKS], I32)
        source = sb("source", [P, TOPK, TT], I32)
        expert_no = sb("expert_no", [P, NE])
        expert_base = sb("expert_base", [P, NE])
        block_no = sb("block_no", [P, MAX_OVER])
        limits = sb("limits", [P, TT - 1])
        group_logits = sb("group_logits", [P, TT, 8])
        group_top = sb("group_top", [P, TT, 8])
        group_at = sb("group_at", [P, TT, 8], U32)
        group_index = sb("group_index", [P, TT])
        group_less = sb("group_less", [P, TT, N_GROUPS])
        group_exp = sb("group_exp", [P, TT, N_GROUPS])
        group_sum = sb("group_sum", [P, TT])
        penalty = sb("penalty", [P, TT, N_GROUPS])
        expert_logits = sb("expert_logits", [P, TT, NE])
        expert_top = sb("expert_top", [P, TT, 8])
        expert_at = sb("expert_at", [P, TT, 8], U32)
        choice = sb("choice", [P, TOPK, TT])
        expert_less = sb("expert_less", [P, TT, NE])
        expert_exp = sb("expert_exp", [P, TT, NE])
        expert_sum = sb("expert_sum", [P, TT])
        second_less = sb("second_less", [P, TT])
        second_exp = sb("second_exp", [P, TT])
        denominator = sb("denominator", [P, TT])
        picked = sb("picked", [P, TOPK, TT, NE])
        either = sb("either", [P, TT, NE])
        running = sb("running", [P, TT + 1, NE])
        position = sb("position", [P, TT, NE])
        count = sb("count", [P, NE])
        above = sb("above", [P, NE, TT - 1])
        over = sb("over", [P, NE])
        over_upto = sb("over_upto", [P, NE])
        ones_row = sb("ones_row", [P, NE])
        over_base = sb("over_base", [P, NE])
        base_gap = sb("base_gap", [P, NE])
        low = sb("low", [P, TT, NE])
        slot_of = sb("slot_of", [P, TT, NE])
        slot_pick = sb("slot_pick", [P, TOPK, TT, NE])
        slot_f = sb("slot_f", [P, TOPK, TT])
        slot_i = sb("slot_i", [P, TOPK, TT], I32)
        passed = sb("passed", [P, MAX_OVER, NE])
        over_f = sb("over_f", [P, MAX_OVER + 1])
        table = sb("table", [P, BLOCKS], I32)
        made = sem("route_constants")
        cleared = sem("table_cleared")
        vec = sem("route_vec")
        expd = sem("route_exp")
        placed = sem("route_placed")
        slots_done = sem("slots_done")
        scattered = sem("table_scattered")
        table_loaded = sem("table_loaded")
        block = ctx.enter_context(nc.Block())
        steps = [0]

        def bc(ap, shape, axis):
            return spread(ap, shape, axis)

        @block.sync
        def _(sp):
            load_first_expert(sp, weights)

        @block.gpsimd
        def _(pool):
            pool.memset(group_logits[:, :, :], MASKED)
            pool.memset(ones_row[:, :], 1.0)
            pool.memset(running[:, 0, :], 0.0)
            pool.iota(unused[:, :], pattern=[[1, BLOCKS]], base=TOPK * SEQ, channel_multiplier=BLOCKS)
            pool.iota(source[:, :, :], pattern=[[SEQ, TOPK], [P, TT]], base=0, channel_multiplier=1)
            f = {"allow_small_or_imprecise_dtypes": True}
            pool.iota(expert_no[:, :], pattern=[[1, NE]], base=0, channel_multiplier=0, **f)
            pool.iota(expert_base[:, :], pattern=[[P, NE]], base=0, channel_multiplier=0, **f)
            pool.iota(block_no[:, :], pattern=[[1, MAX_OVER]], base=0, channel_multiplier=0, **f)
            pool.iota(limits[:, :], pattern=[[P, TT - 1]], base=P, channel_multiplier=0, **f).then_inc(made, 1)
            pool.wait_ge(made, 1)
            pool.dma_start(slot_table.rearrange("(p b) a -> p (b a)", p=P), unused[:, :]).then_inc(cleared, DMA)
            pool.wait_ge(cleared, DMA)
            pool.wait_ge(slots_done, 1)
            for k in range(TOPK):
                for t in range(TT):
                    pool.indirect_dma_start(out=slot_table, out_offset=bass.IndirectOffsetOnAxis(ap=slot_i[:, k, t:t + 1], axis=0),
                                            in_=source[:, k, t:t + 1], in_offset=None).then_inc(scattered, DMA)
            pool.wait_ge(scattered, TOPK * TT * DMA)
            pool.dma_start(table[:, :], slot_table.rearrange("(b p) a -> p (b a)", p=P),
                           allow_slow_non_contiguous=True).then_inc(table_loaded, DMA)

        @block.scalar
        def _(act):
            act.wait_ge(expd, 1)
            act.activation(group_exp[:, :, :], group_less[:, :, :], ACT.Exp).then_inc(expd, 1)
            act.wait_ge(expd, 3)
            act.activation(expert_exp[:, :, :], expert_less[:, :, :], ACT.Exp)
            act.activation(second_exp[:, :], second_less[:, :], ACT.Exp).then_inc(expd, 1)

        @block.tensor
        def _(pe):
            pe.wait_ge(placed, 1)
            flat = ps[:, 0, 0:TT * NE]
            pe.matmul(flat, c.tri_before[:, :], either[:, :, :].rearrange("p t e -> p (t e)"), start=True, stop=False)
            pe.matmul(flat, c.ones[:, :], running[:, 0:TT, :].rearrange("p t e -> p (t e)"), start=False, stop=True)
            pe.matmul(ps[:, 1, 0:NE], c.ones[:, :], running[:, TT, :], start=True, stop=True).then_inc(placed, 1)

        @block.vector
        def _(dve):
            def then(ins):
                steps[0] += 1
                ins.then_inc(vec, 1)
                dve.wait_ge(vec, steps[0])

            dve.wait_ge(made, 1)
            then(dve.tensor_copy(group_logits[:, :, 0:N_GROUPS], logits[:, :, 0:N_GROUPS]))
            for t in range(TT):
                ins = dve.max(group_top[:, t, :], group_logits[:, t, :])
            then(ins)
            for t in range(TT):
                ins = dve.max_index(group_at[:, t, :], group_top[:, t, :], group_logits[:, t, :])
            then(ins)
            dve.tensor_tensor(group_less[:, :, :], logits[:, :, 0:N_GROUPS],
                              group_top[:, :, 0:1].to_broadcast([P, TT, N_GROUPS]), ALU.subtract).then_inc(expd, 1)
            then(dve.tensor_copy(group_index[:, :], group_at[:, :, 0]))
            then(dve.tensor_tensor(penalty[:, :, :], bc(expert_no[:, 0:N_GROUPS], [P, TT, N_GROUPS], 1),
                                   bc(group_index[:, :], [P, TT, N_GROUPS], 2), ALU.is_equal))
            then(dve.tensor_scalar(penalty[:, :, :], penalty[:, :, :], -MASKED, MASKED, ALU.mult, ALU.add))
            then(dve.tensor_tensor(expert_logits[:, :, :].rearrange("p t (g e) -> p t g e", g=N_GROUPS),
                                   logits[:, :, N_GROUPS:].rearrange("p t (g e) -> p t g e", g=N_GROUPS),
                                   bc(penalty[:, :, :], [P, TT, N_GROUPS, PER_GROUP], 3), ALU.add))
            for t in range(TT):
                ins = dve.max(expert_top[:, t, :], expert_logits[:, t, :])
            then(ins)
            for t in range(TT):
                ins = dve.max_index(expert_at[:, t, :], expert_top[:, t, :], expert_logits[:, t, :])
            then(ins)
            dve.wait_ge(expd, 2)
            dve.tensor_tensor(expert_less[:, :, :], expert_logits[:, :, :], expert_top[:, :, 0:1].to_broadcast([P, TT, NE]),
                              ALU.subtract)
            dve.tensor_tensor(second_less[:, :], expert_top[:, :, 1], expert_top[:, :, 0], ALU.subtract).then_inc(expd, 1)
            dve.tensor_reduce(group_sum[:, :], group_exp[:, :, :], AX.X, ALU.add)
            for k in range(TOPK):
                ins = dve.tensor_copy(choice[:, k, :], expert_at[:, :, k])
            then(ins)
            for k in range(TOPK):
                ins = dve.tensor_tensor(picked[:, k, :, :], bc(expert_no[:, :], [P, TT, NE], 1),
                                        bc(choice[:, k, :], [P, TT, NE], 2), ALU.is_equal)
            then(ins)
            then(dve.tensor_tensor(either[:, :, :], picked[:, 0, :, :], picked[:, 1, :, :], ALU.add))
            for t in range(TT):
                then(dve.tensor_tensor(running[:, t + 1, :], running[:, t, :], either[:, t, :], ALU.add))
            dve.sem_inc(placed, 1)
            dve.wait_ge(expd, 4)
            then(dve.tensor_reduce(expert_sum[:, :], expert_exp[:, :, :], AX.X, ALU.add))
            then(dve.tensor_tensor(denominator[:, :], group_sum[:, :], expert_sum[:, :], ALU.mult))
            then(dve.reciprocal(gates[:, 0, :], denominator[:, :]))
            dve.tensor_tensor(gates[:, 1, :], gates[:, 0, :], second_exp[:, :], ALU.mult)
            dve.wait_ge(placed, 2)
            dve.tensor_copy(position[:, :, :].rearrange("p t e -> p (t e)"), ps[:, 0, 0:TT * NE])
            then(dve.tensor_copy(count[:, :], ps[:, 1, 0:NE]))
            then(dve.tensor_tensor(above[:, :, :], bc(count[:, :], [P, NE, TT - 1], 2), bc(limits[:, :], [P, NE, TT - 1], 1), ALU.is_gt))
            then(dve.tensor_reduce(over[:, :], above[:, :, :], AX.X, ALU.add))
            then(dve.tensor_tensor_scan(over_upto[:, :], ones_row[:, :], over[:, :], 0.0, ALU.mult, ALU.add))
            then(dve.tensor_tensor(over_base[:, :], over_upto[:, :], over[:, :], ALU.subtract))
            then(dve.tensor_scalar(over_base[:, :], over_base[:, :], float(NE - 1), float(P), ALU.add, ALU.mult))
            dve.tensor_tensor(base_gap[:, :], expert_base[:, :], over_base[:, :], ALU.subtract)
            then(dve.tensor_scalar(low[:, :, :], position[:, :, :], float(P), None, ALU.is_lt))
            then(dve.tensor_tensor(slot_of[:, :, :], low[:, :, :], bc(base_gap[:, :], [P, TT, NE], 1), ALU.mult))
            then(dve.tensor_tensor(slot_of[:, :, :], slot_of[:, :, :], bc(over_base[:, :], [P, TT, NE], 1), ALU.add))
            then(dve.tensor_tensor(slot_of[:, :, :], slot_of[:, :, :], position[:, :, :], ALU.add))
            for k in range(TOPK):
                ins = dve.tensor_tensor(slot_pick[:, k, :, :], picked[:, k, :, :], slot_of[:, :, :], ALU.mult)
            then(ins)
            then(dve.tensor_reduce(slot_f[:, :, :], slot_pick[:, :, :, :], AX.X, ALU.add))
            dve.tensor_copy(slot_i[:, :, :], slot_f[:, :, :]).then_inc(slots_done, 1)
            then(dve.tensor_tensor(passed[:, :, :], bc(over_upto[:, :], [P, MAX_OVER, NE], 1),
                                   bc(block_no[:, :], [P, MAX_OVER, NE], 2), ALU.is_le))
            then(dve.tensor_reduce(over_f[:, 0:MAX_OVER], passed[:, :, :], AX.X, ALU.add))
            then(dve.tensor_scalar(over_f[:, 0:MAX_OVER], over_f[:, 0:MAX_OVER], float(NE - 1), None, ALU.min))
            then(dve.tensor_copy(over_f[:, MAX_OVER:], over_upto[:, NE - 1:NE]))
            dve.tensor_copy(over_expert[:, :], over_f[:, :])
            dve.wait_ge(table_loaded, DMA)
            dve.tensor_copy(scatter_dst[:, :], table[:, :])
            dve.tensor_scalar(gather_src[:, :], table[:, :], SEQ - 1, None, ALU.bitwise_and)


UP_WAVES = 4
DOWN_WAVES = 2
WAVES = UP_WAVES + DOWN_WAVES


class ExpertWeights:

    def __init__(self, nc, ctx, w1, w3, w2):
        shape = [P, WAVES, 2, D]
        at = region(nc, ctx, "weights_at", WAVES * 2 * D * 4)
        self.raw = nc.alloc_sbuf_tensor_at("weights_raw", shape, F32, offset=at)
        self.lo = nc.alloc_sbuf_tensor_at("weights_lo", shape, F32R, offset=at)
        self.hi = ctx.enter_context(nc.sbuf_tensor("weights_hi", shape, F32R))
        self.loaded = [ctx.enter_context(nc.semaphore(f"wave_loaded{w}")) for w in range(WAVES)]
        self.w1 = w1.rearrange("e (w k p) f -> e w p k f", k=2, p=P)
        self.w3 = w3.rearrange("e (w k p) f -> e w p k f", k=2, p=P)
        self.w2 = w2.rearrange("e (w k p) f -> e w p k f", k=2, p=P)

    def load_up(self, sp, n, wave):
        for half, w in enumerate((self.w1, self.w3)):
            sp.dma_start(self.raw[:, wave, :, half * FF:(half + 1) * FF],
                         w[ds(n, 1), wave].rearrange("e p k f -> p (e k) f")).then_inc(self.loaded[wave], DMA)

    def load_down(self, sp, n, wave):
        sp.dma_start(self.raw[:, wave, :, :],
                     self.w2[ds(n, 1), wave - UP_WAVES].rearrange("e p k f -> p (e k) f")).then_inc(self.loaded[wave], DMA)

    def count(self, wave):
        return 2 * DMA if wave < UP_WAVES else DMA


def load_first_expert(sp, weights):
    for w in range(UP_WAVES):
        weights.load_up(sp, 0, w)
    for w in range(UP_WAVES, WAVES):
        weights.load_down(sp, 0, w)


def experts(nc, c, ps, weights, h2_rows, y_rows, gather_src, scatter_dst):
    UP = range(UP_WAVES)
    DOWN = range(UP_WAVES, WAVES)
    BY_POOL = (1, 4)
    with ExitStack() as ctx:
        def sb(name, shape, dt=F32):
            return ctx.enter_context(nc.sbuf_tensor(name, shape, dt))

        def sem(name):
            return ctx.enter_context(nc.semaphore(name))

        index = sb("index", [P, RING, 2], I32)
        x_rows = sb("x_rows", [P, RING, D])
        x_hi = sb("x_hi", [P, RING, KT, P], F32R)
        x_lo = sb("x_lo", [P, RING, KT, P], F32R)
        act_up = sb("act_up", [P, FF])
        g_tok = sb("g_tok", [P, FF])
        g_hi = sb("g_hi", [P, FT, P], F32R)
        g_lo = sb("g_lo", [P, FT, P], F32R)
        y_out = sb("y_out", [P, RING, D])
        w_hi_done = [sem(f"wave_hi{w}") for w in range(WAVES)]
        w_lo_done = [sem(f"wave_lo{w}") for w in range(WAVES)]
        used = [sem(f"wave_used{w}") for w in range(WAVES)]
        held = sem("experts_held")
        indexed = sem("indexed")
        aimed = sem("aimed")
        gathered = [sem(f"gathered{s}") for s in range(RING)]
        scattered = [sem(f"scattered{s}") for s in range(RING)]
        x_turned = sem("moe_x_turned")
        x_hi_done = sem("moe_x_hi")
        x_lo_done = sem("moe_x_lo")
        up_done = used[UP[-1]]
        silu_done = sem("moe_silu_done")
        g_done = sem("g_done")
        g_turned = sem("g_turned")
        g_hi_done = sem("moe_g_hi")
        g_lo_done = sem("moe_g_lo")
        down_done = used[DOWN[-1]]
        y_ready = sem("y_ready")
        y_free = sem("y_free")
        block = ctx.enter_context(nc.Block())

        def rounds(eng, body):
            body(0, 0, True, False)
            with eng.Fori(0, NE // RING - 1) as i:
                body(RING * i + 1, 1, True, True)
                body(RING * i + 2, 0, True, True)
            body(NE - 1, 1, True, True)
            body(NE, 0, False, True)

        def follows(n):
            return not isinstance(n, int) or n + 1 < NE

        @block.sync
        def _(sp):
            def load_up(n):
                for w in UP:
                    sp.wait_ge(used[w], n)
                    weights.load_up(sp, n, w)

            def load_down(n):
                for w in DOWN:
                    sp.wait_ge(used[w], n)
                    weights.load_down(sp, n, w)

            load_up(1)
            with sp.Fori(0, NE - 2) as i:
                load_up(i + 2)
                load_down(i + 1)
            load_down(NE - 1)

        @block.gpsimd
        def _(pool):
            def gather(n, s):
                pool.wait_ge(x_turned, n + 1)
                pool.tensor_copy(index[:, s, 0:1], gather_src[:, ds(n, 1)]).then_inc(indexed, 1)
                pool.wait_ge(indexed, n + 1)
                pool.sem_inc(held, 1)
                pool.indirect_dma_start(out=x_rows[:, s, :], out_offset=None, in_=h2_rows,
                                        in_offset=bass.IndirectOffsetOnAxis(ap=index[:, s, 0:1], axis=0)).then_inc(gathered[s], DMA)

            def scatter(n, s, i):
                if i is not None:
                    pool.wait_ge(scattered[s], DMA * i)
                    pool.sem_inc(y_free, 1)
                pool.tensor_copy(index[:, s, 1:2], scatter_dst[:, ds(n, 1)]).then_inc(aimed, 1)
                pool.wait_ge(aimed, n + 1)
                pool.wait_ge(y_ready, 1 + n + 1)
                pool.sem_inc(held, 1)
                pool.indirect_dma_start(out=y_rows, out_offset=bass.IndirectOffsetOnAxis(ap=index[:, s, 1:2], axis=0),
                                        in_=y_out[:, s, :], in_offset=None).then_inc(scattered[s], DMA)

            def rest(n, w):
                pool.wait_ge(w_hi_done[w], n + 1)
                pool.tensor_tensor(weights.lo[:, w, :, :], weights.raw[:, w, :, :], weights.hi[:, w, :, :].bitcast(F32),
                                   ALU.subtract).then_inc(w_lo_done[w], 1)

            def body(n, s, i, ahead, nxt):
                if ahead:
                    gather(n + RING, s)
                rest(n - 1, DOWN[0])
                if nxt:
                    rest(n + 1, UP[1])
                scatter(n - 1, 1 - s, i)

            pool.sem_inc(y_free, RING)
            for s in range(RING):
                gather(s, s)
            rest(0, UP[1])
            gather(RING, 0)
            rest(1, UP[1])
            body(1, 1, None, True, True)
            body(2, 0, None, True, True)
            with pool.Fori(0, NE // RING - 3) as i:
                body(RING * i + 3, 1, i + 1, True, True)
                body(RING * i + 4, 0, i + 1, True, True)
            body(NE - 3, 1, NE // RING - 2, True, True)
            body(NE - 2, 0, NE // RING - 2, False, True)
            body(NE - 1, 1, NE // RING - 1, False, False)
            body(NE, 0, NE // RING - 1, False, False)
            for s in range(RING):
                pool.wait_ge(scattered[s], DMA * (NE // RING))

        @block.scalar
        def _(act):
            def high(n, w):
                act.wait_ge(weights.loaded[w], weights.count(w) * n + weights.count(w))
                act.activation(weights.hi[:, w, :, :], weights.raw[:, w, :, :], ACT.Copy).then_inc(w_hi_done[w], 1)

            def x_out(n, s):
                act.wait_ge(x_turned, RING + n + 1)
                act.activation(x_hi[:, s, :, :].rearrange("p k t -> p (k t)"), banks(ps, 0, 2), ACT.Copy).then_inc(x_hi_done, 1)

            def body(n, s, up, down):
                if follows(n) and up:
                    x_out(n + 1, 1 - s)
                if down:
                    high(n - 1, DOWN[0])
                    act.wait_ge(g_turned, n)
                    act.activation(g_hi[:, :, :].rearrange("p k t -> p (k t)"), ps[:, 4, :], ACT.Copy).then_inc(g_hi_done, 1)
                    high(n - 1, DOWN[1])
                if follows(n) and up:
                    for w in (0, 1):
                        high(n + 1, w)
                if up:
                    act.wait_ge(up_done, n + 1)
                    act.wait_ge(g_done, 1 + n)
                    act.activation(act_up[:, :], ps[:, 2, :], ACT.Silu).then_inc(silu_done, 1)
                if follows(n) and up:
                    for w in (2, 3):
                        high(n + 1, w)

            for w in UP:
                high(0, w)
            x_out(0, 0)
            rounds(act, body)

        @block.vector
        def _(dve):
            for ready in (g_done, g_lo_done, x_lo_done, y_ready):
                dve.sem_inc(ready, 1)

            def rest(n, w):
                dve.wait_ge(w_hi_done[w], n + 1)
                dve.tensor_tensor(weights.lo[:, w, :, :], weights.raw[:, w, :, :], weights.hi[:, w, :, :].bitcast(F32),
                                  ALU.subtract).then_inc(w_lo_done[w], 1)

            def x_rest(n, s):
                dve.wait_ge(x_hi_done, n + 1)
                dve.tensor_tensor(x_lo[:, s, :, :].rearrange("p k t -> p (k t)"), banks(ps, 0, 2),
                                  x_hi[:, s, :, :].rearrange("p k t -> p (k t)").bitcast(F32), ALU.subtract).then_inc(x_lo_done, 1)

            def body(n, s, up, down):
                nxt = follows(n) and up
                if nxt:
                    x_rest(n + 1, 1 - s)
                if down:
                    dve.wait_ge(g_hi_done, n)
                    dve.tensor_tensor(g_lo[:, :, :].rearrange("p k t -> p (k t)"), ps[:, 4, :],
                                      g_hi[:, :, :].rearrange("p k t -> p (k t)").bitcast(F32), ALU.subtract).then_inc(g_lo_done, 1)
                    rest(n - 1, DOWN[1])
                if nxt:
                    rest(n + 1, 0)
                if up:
                    dve.wait_ge(silu_done, n + 1)
                    dve.tensor_tensor(g_tok[:, :], ps[:, 3, :], act_up[:, :], ALU.mult).then_inc(g_done, 1)
                if nxt:
                    rest(n + 1, 2)
                if down:
                    dve.wait_ge(down_done, n)
                    dve.wait_ge(y_free, n)
                    dve.tensor_copy(y_out[:, 1 - s, :], banks(ps, 5, 2)).then_inc(y_ready, 1)
                if nxt:
                    rest(n + 1, 3)

            for w in UP:
                if w not in BY_POOL:
                    rest(0, w)
            x_rest(0, 0)
            rounds(dve, body)

        @block.tensor
        def _(pe):
            pe.sem_inc(x_turned, RING)

            def turn_x(n, s, i):
                pe.wait_ge(gathered[s], DMA * i + DMA)
                pe.wait_ge(x_lo_done, 1 + n)
                for k in range(KT):
                    last = pe.transpose(ps[:, k // 4, (k % 4) * P:(k % 4 + 1) * P], x_rows[:, s, k * P:(k + 1) * P], c.ident[:, :])
                last.then_inc(x_turned, 1)

            def turn_g(n):
                pe.wait_ge(g_done, 1 + n + 1)
                pe.wait_ge(g_lo_done, 1 + n)
                for k in range(FT):
                    last = pe.transpose(ps[:, 4, k * P:(k + 1) * P], g_tok[:, k * P:(k + 1) * P], c.ident[:, :])
                last.then_inc(g_turned, 1)

            def products(out, w, kk, a_hi, a_lo, first, last):
                for a, b, opens, closes in ((a_hi, weights.hi, first, False), (a_hi, weights.lo, False, False),
                                            (a_lo, weights.hi, False, last)):
                    for h in range(2):
                        ins = pe.matmul(out[h], a, b[:, w, kk, h * HALF:(h + 1) * HALF], start=opens, stop=closes)
                return ins

            def up(n, s):
                pe.wait_ge(x_lo_done, 1 + n + 1)
                pe.wait_ge(g_done, 1 + n)
                for w in UP:
                    pe.wait_ge(w_lo_done[w], n + 1)
                    for kk in range(2):
                        k = 2 * w + kk
                        last = products([ps[:, 2, :], ps[:, 3, :]], w, kk, x_hi[:, s, k, :], x_lo[:, s, k, :], k == 0, k == KT - 1)
                    last.then_inc(used[w], 1)

            def down(n):
                pe.wait_ge(g_lo_done, 1 + n + 1)
                pe.wait_ge(y_ready, 1 + n)
                for w in DOWN:
                    pe.wait_ge(w_lo_done[w], n + 1)
                    for kk in range(2):
                        k = 2 * (w - UP_WAVES) + kk
                        last = products([ps[:, 5, :], ps[:, 6, :]], w, kk, g_hi[:, k, :], g_lo[:, k, :], k == 0, k == FT - 1)
                    last.then_inc(used[w], 1)

            turn_x(0, 0, 0)
            turn_x(1, 1, 0)
            up(0, 0)
            with pe.Fori(0, NE // RING - 1) as i:
                for s in (1, 0):
                    n = RING * i + 2 - s
                    turn_x(n + 1, 1 - s, i + 1)
                    turn_g(n - 1)
                    up(n, s)
                    down(n - 1)
            turn_g(NE - 2)
            up(NE - 1, 1)
            down(NE - 2)
            turn_g(NE - 1)
            down(NE - 1)


def overflow(nc, c, ps, w1, w3, w2, h2_rows, y_rows, gather_src, scatter_dst, over_expert):
    with ExitStack() as ctx:
        def sb(name, shape, dt=F32):
            return ctx.enter_context(nc.sbuf_tensor(name, shape, dt))

        def sem(name):
            return ctx.enter_context(nc.semaphore(name))

        w1_sb = sb("over_w1", [P, KT, FF])
        w3_sb = sb("over_w3", [P, KT, FF])
        w2_sb = sb("over_w2", [P, FT, D])
        index = sb("over_index", [P, 2], I32)
        x_rows = sb("over_x", [P, D])
        x_t = sb("over_x_t", [P, KT, P])
        act_up = sb("over_act_up", [P, FF])
        g_tok = sb("over_g", [P, FF])
        g_t = sb("over_g_t", [P, FT, P])
        y_out = sb("over_y", [P, D])
        loaded = sem("over_loaded")
        held = sem("over_held")
        indexed = sem("over_indexed")
        gathered = sem("over_gathered")
        x_turned = sem("over_x_turned")
        x_ready = sem("over_x_ready")
        up_done = sem("over_up_done")
        silu_done = sem("over_silu_done")
        g_done = sem("over_g_done")
        g_turned = sem("over_g_turned")
        g_ready = sem("over_g_ready")
        down_done = sem("over_down_done")
        y_ready = sem("over_y_ready")
        scattered = sem("over_scattered")
        w1_rows = w1.rearrange("e (k p) f -> e p k f", p=P)
        w3_rows = w3.rearrange("e (k p) f -> e p k f", p=P)
        w2_rows = w2.rearrange("e (k p) f -> e p k f", p=P)
        block = ctx.enter_context(nc.Block())

        def each(eng, body):
            blocks = eng.value_load(over_expert[0:1, MAX_OVER:MAX_OVER + 1], min_val=0, max_val=MAX_OVER)
            with eng.If(blocks > 0):
                with eng.Fori(0, MAX_OVER) as b:
                    with eng.If(b < blocks):
                        body(b)

        @block.sync
        def _(sp):
            def body(b):
                e = sp.value_load(over_expert[0:1, ds(b, 1)], min_val=0, max_val=NE - 1)
                sp.wait_ge(down_done, 1 + b)
                for dst, src in ((w1_sb, w1_rows), (w3_sb, w3_rows), (w2_sb, w2_rows)):
                    sp.dma_start(dst[:, :, :], src[ds(e, 1)].rearrange("e p k f -> p (e k) f")).then_inc(loaded, DMA)

            each(sp, body)

        @block.gpsimd
        def _(pool):
            def body(b):
                pool.tensor_copy(index[:, 0:1], gather_src[:, ds(NE + b, 1)])
                pool.tensor_copy(index[:, 1:2], scatter_dst[:, ds(NE + b, 1)]).then_inc(indexed, 1)
                pool.wait_ge(indexed, b + 1)
                pool.sem_inc(held, 1)
                pool.indirect_dma_start(out=x_rows[:, :], out_offset=None, in_=h2_rows,
                                        in_offset=bass.IndirectOffsetOnAxis(ap=index[:, 0:1], axis=0)).then_inc(gathered, DMA)
                pool.wait_ge(y_ready, 1 + b + 1)
                pool.sem_inc(held, 1)
                pool.indirect_dma_start(out=y_rows, out_offset=bass.IndirectOffsetOnAxis(ap=index[:, 1:2], axis=0),
                                        in_=y_out[:, :], in_offset=None).then_inc(scattered, DMA)
                pool.wait_ge(scattered, DMA * b + DMA)

            each(pool, body)

        @block.scalar
        def _(act):
            def body(b):
                act.wait_ge(x_turned, b + 1)
                act.activation(x_t[:, :, :].rearrange("p k t -> p (k t)"), banks(ps, 0, 2), ACT.Copy).then_inc(x_ready, 1)
                act.wait_ge(up_done, b + 1)
                act.activation(act_up[:, :], ps[:, 2, :], ACT.Silu).then_inc(silu_done, 1)

            each(act, body)

        @block.vector
        def _(dve):
            dve.sem_inc(y_ready, 1)

            def body(b):
                dve.wait_ge(silu_done, b + 1)
                dve.tensor_tensor(g_tok[:, :], ps[:, 3, :], act_up[:, :], ALU.mult).then_inc(g_done, 1)
                dve.wait_ge(g_turned, b + 1)
                dve.tensor_copy(g_t[:, :, :].rearrange("p k t -> p (k t)"), ps[:, 4, :]).then_inc(g_ready, 1)
                dve.wait_ge(down_done, 1 + b + 1)
                dve.tensor_copy(y_out[:, :], banks(ps, 5, 2)).then_inc(y_ready, 1)

            each(dve, body)

        @block.tensor
        def _(pe):
            pe.sem_inc(down_done, 1)

            def body(b):
                pe.wait_ge(gathered, DMA * b + DMA)
                for k in range(KT):
                    last = pe.transpose(ps[:, k // 4, (k % 4) * P:(k % 4 + 1) * P], x_rows[:, k * P:(k + 1) * P], c.ident[:, :])
                last.then_inc(x_turned, 1)
                pe.wait_ge(x_ready, b + 1)
                pe.wait_ge(loaded, 3 * DMA * b + 3 * DMA)
                for n, w in ((2, w1_sb), (3, w3_sb)):
                    for k in range(KT):
                        last = pe.matmul(ps[:, n, :], x_t[:, k, :], w[:, k, :], start=k == 0, stop=k == KT - 1)
                last.then_inc(up_done, 1)
                pe.wait_ge(g_done, b + 1)
                for k in range(FT):
                    last = pe.transpose(ps[:, 4, k * P:(k + 1) * P], g_tok[:, k * P:(k + 1) * P], c.ident[:, :])
                last.then_inc(g_turned, 1)
                pe.wait_ge(g_ready, b + 1)
                pe.wait_ge(y_ready, 1 + b)
                for k in range(FT):
                    for h in range(2):
                        last = pe.matmul(ps[:, 5 + h, :], g_t[:, k, :], w2_sb[:, k, h * HALF:(h + 1) * HALF],
                                         start=k == 0, stop=k == FT - 1)
                last.then_inc(down_done, 1)

            each(pe, body)


def finish(nc, x2, gates, y_rows, gain, out):
    DEPTH = 4
    with ExitStack() as ctx:
        def sb(name, shape, dt=F32):
            return ctx.enter_context(nc.sbuf_tensor(name, shape, dt))

        def sem(name):
            return ctx.enter_context(nc.semaphore(name))

        gain_row = sb("final_row", [P, D])
        y_tile = sb("y_tile", [P, DEPTH, TOPK, D])
        total = sb("total", [P, DEPTH, D])
        squares = sb("final_squares", [P, D])
        sum_sq = sb("final_sum", [P, TT])
        mean_sq = sb("final_mean", [P, TT])
        root = sb("final_root", [P, TT])
        rstd = sb("final_rstd", [P, TT])
        result = sb("result", [P, RING, D])
        gain_loaded = sem("final_gain_loaded")
        y_loaded = [sem(f"y_loaded{s}") for s in range(DEPTH)]
        first_added = sem("first_added")
        summed = sem("final_summed")
        squared = sem("final_squared")
        mean_done = sem("final_mean_done")
        root_done = sem("final_root_done")
        rstd_done = sem("final_rstd_done")
        scaled = sem("final_scaled")
        stored = [sem(f"out_stored{s}") for s in range(RING)]
        y_tiles = y_rows[0:TOPK * SEQ].rearrange("(k t p) d -> t p k d", k=TOPK, p=P)
        out_tiles = out[0].rearrange("(t p) d -> t p d", p=P)
        block = ctx.enter_context(nc.Block())

        @block.sync
        def _(sp):
            with sp.Fori(0, TT // DEPTH) as i:
                for s in range(DEPTH):
                    sp.wait_ge(summed, DEPTH * i + s + 1)
                    sp.dma_start(y_tile[:, s, :, :], y_tiles[ds(DEPTH * i + s, 1)].rearrange("a p k d -> p (a k) d")).then_inc(y_loaded[s], DMA)

        @block.scalar
        def _(act):
            act.dma_start(gain_row[:, :], gain.rearrange("(a d) -> a d", a=1).to_broadcast([P, D])).then_inc(gain_loaded, DMA)
            act.sem_inc(squared, RING)
            for s in range(RING):
                act.sem_inc(stored[s], DMA)
            with act.Fori(0, TT // DEPTH) as i:
                for s in range(DEPTH):
                    t = DEPTH * i + s
                    act.wait_ge(summed, DEPTH + t + 1)
                    act.wait_ge(squared, RING + t)
                    act.activation(squares[:, :], total[:, s, :], ACT.Square, accum_out=sum_sq[:, ds(t, 1)]).then_inc(squared, 1)
                    act.wait_ge(mean_done, t + 1)
                    act.activation(root[:, ds(t, 1)], mean_sq[:, ds(t, 1)], ACT.Sqrt).then_inc(root_done, 1)
                    act.wait_ge(scaled, t + 1)
                    act.dma_start(out_tiles[ds(t, 1)].rearrange("a p d -> p (a d)"), result[:, s % RING, :]).then_inc(stored[s % RING], DMA)
            for s in range(RING):
                act.wait_ge(stored[s], DMA * (TT // RING) + DMA)

        @block.vector
        def _(dve):
            dve.sem_inc(summed, DEPTH)
            dve.wait_ge(gain_loaded, DMA)

            def add_up(i, s):
                t = DEPTH * i + s
                dve.wait_ge(y_loaded[s], DMA * i + DMA)
                dve.scalar_tensor_tensor(out=total[:, s, :], in0=y_tile[:, s, 0, :], scalar=gates[:, 0, ds(t, 1)],
                                         in1=x2[:, ds(t, 1), :].rearrange("p a d -> p (a d)"), op0=ALU.mult,
                                         op1=ALU.add).then_inc(first_added, 1)
                dve.wait_ge(first_added, t + 1)
                dve.scalar_tensor_tensor(out=total[:, s, :], in0=y_tile[:, s, 1, :], scalar=gates[:, 1, ds(t, 1)],
                                         in1=total[:, s, :], op0=ALU.mult, op1=ALU.add).then_inc(summed, 1)

            def scale(i, s):
                t = DEPTH * i + s
                dve.wait_ge(squared, RING + t + 1)
                dve.tensor_scalar(mean_sq[:, ds(t, 1)], sum_sq[:, ds(t, 1)], 1.0 / D, EPS, ALU.mult, ALU.add).then_inc(mean_done, 1)
                dve.wait_ge(root_done, t + 1)
                dve.reciprocal(rstd[:, ds(t, 1)], root[:, ds(t, 1)]).then_inc(rstd_done, 1)
                dve.wait_ge(rstd_done, t + 1)
                dve.wait_ge(stored[s % RING], DMA * (DEPTH // RING) * i + DMA * (s // RING) + DMA)
                dve.scalar_tensor_tensor(out=result[:, s % RING, :], in0=total[:, s, :], scalar=rstd[:, ds(t, 1)],
                                         in1=gain_row[:, :], op0=ALU.mult, op1=ALU.mult).then_inc(scaled, 1)

            with dve.Fori(0, TT // DEPTH) as i:
                add_up(i, 0)
                for s in range(DEPTH):
                    if s + 1 < DEPTH:
                        add_up(i, s + 1)
                    scale(i, s)


def clear_semaphores(nc):
    used = sorted(nc.released_uncleared_semaphores)
    nc.gpsimd.sem_clear(range(used[0], used[-1] + 1))
    nc.all_engine_barrier()


def trunk(nc, x, norm_mix_g, w_in, b_f, conv_w, conv_b, dt_bias, a_log, d_skip, ssd_norm_g, w_br_attn, w_br_ssd,
          w_out, norm_ffn_g, w_group_router, b_group_router, w_expert_router, b_expert_router, w1, w3, w2, final_g, out):
    with ExitStack() as ctx:
        def sb(name, shape, dt=F32):
            return ctx.enter_context(nc.sbuf_tensor(name, shape, dt))

        def dram(name, shape, dt=F32):
            return nc.dram_tensor(name, shape, dt, kind="Internal").ap()

        ps = ctx.enter_context(nc.psum_tensor("ps", [P, 8, HALF], F32))
        c = Constants(ident=sb("ident", [P, P]), ident_bf=sb("ident_bf", [P, P], BF16), ones=sb("ones", [P, P]),
                            tri=sb("tri", [P, P]), tri_after=sb("tri_after", [P, P]), tri_before=sb("tri_before", [P, P]),
                            causal_bf=sb("causal_bf", [P, P], BF16))
        dt_tok = sb("dt_tok", [P, TT, SSD_HEADS])
        a_tok = sb("a_tok", [P, TT, SSD_HEADS])
        gates = sb("gates", [P, TOPK, TT])
        logits = sb("logits", [P, TT, N_GROUPS + NE])
        gather_src = sb("gather_src", [P, BLOCKS], I32)
        scatter_dst = sb("scatter_dst", [P, BLOCKS], I32)
        over_expert = sb("over_expert", [P, MAX_OVER + 1], I32)
        f_rows = dram("f_rows", (HEADS, SEQ))
        silu_z = dram("silu_z", (XB, P, SEQ))
        gate_rows = dram("gate_rows", (2 * KT, P, SEQ))
        h2_rows = dram("h2_rows", (SEQ, D))
        y_rows = dram("y_rows", (TOPK * SEQ + BLOCKS * P, D))
        slot_table = dram("slot_table", (BLOCKS * P, 1), I32)
        make_constants(nc, c)

        held_at = region(nc, ctx, "held", TT * D * 4)
        size = (D_ATTN // P) * SEQ * 4
        ya_hi = nc.alloc_sbuf_tensor_at("ya_hi", [P, D_ATTN // P, SEQ], F32R, offset=held_at)
        ya_lo = nc.alloc_sbuf_tensor_at("ya_lo", [P, D_ATTN // P, SEQ], F32R, offset=held_at + size)
        x2 = nc.alloc_sbuf_tensor_at("x2", [P, TT, D], F32, offset=held_at)
        with ExitStack() as mixer:
            xbc_at = region(nc, mixer, "xbc_at", CB * SEQ * 4)
            xbc = nc.alloc_sbuf_tensor_at("xbc", [P, CB, SEQ], F32, offset=xbc_at)
            gated = xbc[:, 0:XB, :]
            merged = xbc[:, 0:KT, :]
            with ExitStack() as early:
                qkv_at = region(nc, early, "qkv_at", CB * SEQ * 4)
                qkv = nc.alloc_sbuf_tensor_at("qkv", [P, CB, SEQ], F32, offset=qkv_at)
                with ExitStack() as proj:
                    h_hi = proj.enter_context(nc.sbuf_tensor("h_hi", [P, KT, SEQ], F32R))
                    h_lo = proj.enter_context(nc.sbuf_tensor("h_lo", [P, KT, SEQ], F32R))
                    normalise_input(nc, c, ps, x, norm_mix_g, h_hi, h_lo, xbc_at)
                    project(nc, c, ps, w_in[0], [(COL_Q, CB, "keep", qkv), (COL_Z, XB, "silu", silu_z),
                                                 (COL_GA, 2 * KT, "sigmoid", gate_rows), (COL_XBC, CB, "conv", xbc)],
                            h_hi, h_lo, held_at, (conv_w[0], conv_b[0]),
                            lambda at: Decays(nc, at, xbc_at, w_in[0], b_f, dt_bias, a_log, f_rows, dt_tok, a_tok))
                attention(nc, c, ps, qkv, f_rows, ya_hi, ya_lo, held_at + 2 * size - SEQ * 4)
            with ExitStack() as branch:
                square_sum = branch.enter_context(nc.sbuf_tensor("square_sum", [P, SEQ], F32))
                weights = BranchWeights(nc, branch, w_br_attn[0], w_br_ssd[0])
                state_space(nc, c, ps, xbc, dt_tok, a_tok, d_skip, silu_z, gated, square_sum, weights.load_first)
                merge(nc, c, ps, weights, gate_rows, gated, square_sum, ssd_norm_g, ya_hi, ya_lo, merged)
            project_out(nc, c, ps, w_out[0], x, merged, x2, norm_ffn_g, w_group_router[0], b_group_router,
                        w_expert_router[0], b_expert_router, h2_rows, logits)
        clear_semaphores(nc)
        with ExitStack() as moe:
            weights = ExpertWeights(nc, moe, w1[0], w3[0], w2[0])
            route(nc, c, ps, logits, gates, slot_table, gather_src, scatter_dst, over_expert, weights)
            experts(nc, c, ps, weights, h2_rows, y_rows, gather_src, scatter_dst)
        overflow(nc, c, ps, w1[0], w3[0], w2[0], h2_rows, y_rows, gather_src, scatter_dst, over_expert)
        finish(nc, x2, gates, y_rows, final_g, out)


_INS = ["x", "norm_mix_g", "w_in", "b_f", "conv_w", "conv_b", "dt_bias", "a_log", "d_skip", "ssd_norm_g", "w_br_attn",
        "w_br_ssd", "w_out", "norm_ffn_g", "w_group_router", "b_group_router", "w_expert_router", "b_expert_router",
        "w1", "w3", "w2", "final_g"]


def kernel(**inputs):
    import numpy as np
    import concourse.bacc as bacc
    from concourse.bass_utils import run_bass_kernel_spmd

    nc = bacc.Bacc("TRN2", target_bir_lowering=False, num_devices=1)
    arrays, args = {}, []
    for name in _INS:
        a = np.ascontiguousarray(inputs[name])
        arrays[f"in_{name}"] = a
        args.append(nc.dram_tensor(f"in_{name}", a.shape, mybir.dt.from_np(a.dtype), kind="ExternalInput").ap())
    args.append(nc.dram_tensor("result_dram", (1, SEQ, D), F32, kind="ExternalOutput").ap())
    trunk(nc, *args)
    nc.compile()
    r = run_bass_kernel_spmd(nc, [arrays], core_ids=[0])
    return r.results[0]["result_dram"]
```
